# Optimizing a Trainium2 kernel written in Bass

```python
import jax
import jax.numpy as jnp
from jax import lax
import numpy as np

D_MODEL = 1024
BATCH = 1
SEQ = 512
DEPTH = 1

GLA_HEADS = 4
GLA_DK = D_MODEL // 8
GLA_DV = D_MODEL // 4
GLA_GATE_RANK = 16
GLA_TAU = 16.0
GLA_CHUNK = 64
GLA_K_WIDTH = GLA_HEADS * GLA_DK
GLA_V_WIDTH = GLA_HEADS * GLA_DV

ATT_GROUPS = ((128, 1), (512, 4), (2048, 16))
ATT_HEADS_PER_GROUP = 8
ATT_HEAD_DIM = 64
ATT_BLOCK = 128
ROT_DIM = ATT_HEAD_DIM // 4
ROPE_THETA = 500000.0
ATT_QKV_WIDTH = len(ATT_GROUPS) * ATT_HEADS_PER_GROUP * ATT_HEAD_DIM
ATT_OUT_WIDTH = ATT_HEADS_PER_GROUP * ATT_HEAD_DIM

IN_SPLIT_SIZES = (GLA_K_WIDTH, GLA_K_WIDTH, GLA_V_WIDTH, GLA_V_WIDTH, GLA_GATE_RANK,
                  ATT_QKV_WIDTH, ATT_QKV_WIDTH, ATT_QKV_WIDTH, D_MODEL, D_MODEL)
IN_WIDTH = sum(IN_SPLIT_SIZES)

N_EXPERTS = 32
TOP_K = 4
EXPERT_FF = D_MODEL
SWIGLU_LIMIT = 7.0
SWIGLU_ALPHA = 1.702
MOE_BLOCK = 128

EPS = 1e-5

kernel_name = 'hybrid_gla_dilated_attn_moe'

def rmsnorm(x, g):
    xf = x.astype(jnp.float32)
    y = xf * lax.rsqrt(jnp.mean(xf * xf, axis=-1, keepdims=True) + EPS)
    return (y * g.astype(jnp.float32)).astype(x.dtype)

def partial_rotary(t, pos):
    half = ROT_DIM // 2
    inv_freq = ROPE_THETA ** (-jnp.arange(half, dtype=jnp.float32) * (2.0 / ROT_DIM))
    ang = pos[:, None] * inv_freq[None, :]
    cos = jnp.cos(ang)[None, :, None, :]
    sin = jnp.sin(ang)[None, :, None, :]
    tf = t.astype(jnp.float32)
    r1 = tf[..., :half]
    r2 = tf[..., half:ROT_DIM]
    out = jnp.concatenate([r1 * cos - r2 * sin, r2 * cos + r1 * sin, tf[..., ROT_DIM:]], axis=-1)
    return out.astype(t.dtype)

def gla_chunked(q, k, v, log_decay):
    B, S, H, dk = q.shape
    C = GLA_CHUNK
    nc = S // C

    def chunks(t):
        return t.astype(jnp.float32).reshape(B, nc, C, H, t.shape[-1]).transpose(0, 3, 1, 2, 4)

    qc = chunks(q) * (dk ** -0.5)
    kc, vc, gc = chunks(k), chunks(v), chunks(log_decay)
    b = jnp.cumsum(gc, axis=3)
    b_last = b[:, :, :, -1:, :]
    qe = qc * jnp.exp(b)
    ke = kc * jnp.exp(-b)
    kd = kc * jnp.exp(b_last - b)
    causal = jnp.tril(jnp.ones((C, C), dtype=bool))
    A = jnp.where(causal, jnp.einsum('bhnid,bhnjd->bhnij', qe, ke), 0.0)
    o_intra = jnp.einsum('bhnij,bhnjv->bhniv', A, vc)
    U = jnp.einsum('bhnjd,bhnjv->bhndv', kd, vc)
    decay = jnp.exp(b_last[:, :, :, 0, :])

    def step(state, inp):
        dec, u = inp
        return dec[..., None] * state + u, state

    state0 = jnp.zeros((B, H, dk, vc.shape[-1]), jnp.float32)
    _, prev = lax.scan(step, state0, (decay.transpose(2, 0, 1, 3), U.transpose(2, 0, 1, 3, 4)))
    prev = prev.transpose(1, 2, 0, 3, 4)
    o_inter = jnp.einsum('bhnid,bhndv->bhniv', qe, prev)
    o = o_intra + o_inter
    return o.transpose(0, 2, 3, 1, 4).reshape(B, S, H, vc.shape[-1])

def dilated_group(q, k, v, window, dilation):
    B, S, H, hd = q.shape
    L = ATT_BLOCK
    steps = window // dilation
    unit = dilation * L
    Sp = -(-S // unit) * unit
    n = Sp // dilation
    nb = n // L

    def to_blocks(t):
        t = jnp.pad(t, ((0, 0), (0, Sp - S), (0, 0), (0, 0)))
        t = t.reshape(B, n, dilation, H, hd).transpose(0, 2, 3, 1, 4)
        return t.reshape(B, dilation, H, nb, L, hd)

    def with_prev(t):
        prev = jnp.concatenate([jnp.zeros_like(t[:, :, :, :1]), t[:, :, :, :-1]], axis=3)
        return jnp.concatenate([prev, t], axis=4)

    qb = to_blocks(q)
    kw = with_prev(to_blocks(k))
    vw = with_prev(to_blocks(v))
    s = jnp.einsum('brhnqe,brhnke->brhnqk', qb, kw, preferred_element_type=jnp.float32) * (hd ** -0.5)
    qi = jnp.arange(L)[:, None]
    ki = jnp.arange(2 * L)[None, :]
    dist = qi + L - ki
    band = (dist >= 0) & (dist <= steps)
    has_prev = (jnp.arange(nb)[:, None, None] > 0) | (ki >= L)[None]
    mask = band[None] & has_prev
    s = jnp.where(mask, s, -jnp.inf)
    mx = jnp.max(s, axis=-1, keepdims=True)
    e = jnp.exp(s - mx)
    den = jnp.sum(e, axis=-1, keepdims=True)
    o = jnp.einsum('brhnqk,brhnke->brhnqe', e / den, vw.astype(jnp.float32))
    lse = (mx + jnp.log(den))[..., 0]
    o = o.reshape(B, dilation, H, n, hd).transpose(0, 3, 1, 2, 4).reshape(B, Sp, H, hd)[:, :S]
    lse = lse.reshape(B, dilation, H, n).transpose(0, 3, 1, 2).reshape(B, Sp, H)[:, :S]
    return o, lse

def hybrid_mixer(xn, w_in, gla_gate_up, gla_gate_bias, gla_norm_g, w_branch_gla, w_branch_att, w_mix_out):
    B, S, D = xn.shape
    proj = xn @ w_in
    points = np.cumsum(IN_SPLIT_SIZES)[:-1].tolist()
    gq, gk, gv, gr, glr, aq, ak, av, gate_gla, gate_att = jnp.split(proj, points, axis=-1)

    log_decay = jax.nn.log_sigmoid((glr @ gla_gate_up + gla_gate_bias).astype(jnp.float32)) / GLA_TAU
    o = gla_chunked(gq.reshape(B, S, GLA_HEADS, GLA_DK), gk.reshape(B, S, GLA_HEADS, GLA_DK),
                    gv.reshape(B, S, GLA_HEADS, GLA_DV), log_decay.reshape(B, S, GLA_HEADS, GLA_DK))
    o = o * lax.rsqrt(jnp.mean(o * o, axis=-1, keepdims=True) + EPS) * gla_norm_g.astype(jnp.float32)
    o = o * jax.nn.silu(gr.reshape(B, S, GLA_HEADS, GLA_DV).astype(jnp.float32))
    y_gla = o.reshape(B, S, GLA_V_WIDTH).astype(xn.dtype)

    n_heads = len(ATT_GROUPS) * ATT_HEADS_PER_GROUP
    pos = jnp.arange(S, dtype=jnp.float32)
    aq = partial_rotary(aq.reshape(B, S, n_heads, ATT_HEAD_DIM), pos)
    ak = partial_rotary(ak.reshape(B, S, n_heads, ATT_HEAD_DIM), pos)
    av = av.reshape(B, S, n_heads, ATT_HEAD_DIM)
    outs, lses = [], []
    for g, (window, dilation) in enumerate(ATT_GROUPS):
        hs = slice(g * ATT_HEADS_PER_GROUP, (g + 1) * ATT_HEADS_PER_GROUP)
        o_g, lse_g = dilated_group(aq[:, :, hs], ak[:, :, hs], av[:, :, hs], window, dilation)
        outs.append(o_g)
        lses.append(lse_g)
    alpha = jax.nn.softmax(jnp.stack(lses), axis=0)
    y_att = jnp.sum(alpha[..., None] * jnp.stack(outs), axis=0)
    y_att = y_att.reshape(B, S, ATT_OUT_WIDTH).astype(xn.dtype)

    merged = (jax.nn.sigmoid(gate_gla) * (y_gla @ w_branch_gla)
              + jax.nn.sigmoid(gate_att) * (y_att @ w_branch_att))
    return merged @ w_mix_out

def moe(xn, router_w, router_b, w_gate_up, b_gate_up, w_down, b_down):
    N, D = xn.shape
    logits = (xn @ router_w + router_b).astype(jnp.float32)
    top_v, top_e = lax.top_k(logits, TOP_K)
    gates = jax.nn.softmax(top_v, axis=-1)
    M = N * TOP_K
    e_flat = top_e.reshape(M)
    g_flat = gates.reshape(M)
    tok = jnp.arange(M, dtype=jnp.int32) // TOP_K
    order = jnp.argsort(e_flat)
    e_s, tok_s, g_s = e_flat[order], tok[order], g_flat[order]
    counts = jnp.bincount(e_flat, length=N_EXPERTS)
    starts = jnp.cumsum(counts) - counts
    padded = (counts + MOE_BLOCK - 1) // MOE_BLOCK * MOE_BLOCK
    pstarts = jnp.cumsum(padded) - padded
    dest = pstarts[e_s] + jnp.arange(M, dtype=jnp.int32) - starts[e_s]
    n_blocks = -(-M // MOE_BLOCK) + N_EXPERTS
    P = n_blocks * MOE_BLOCK
    x_pad = jnp.zeros((P, D), xn.dtype).at[dest].set(xn[tok_s])
    block_end = jnp.cumsum(padded) // MOE_BLOCK
    block_expert = jnp.minimum(jnp.searchsorted(block_end, jnp.arange(n_blocks), side='right'), N_EXPERTS - 1)

    def expert_block(args):
        xb, e = args
        h = xb @ w_gate_up[e] + b_gate_up[e]
        gate = jnp.minimum(h[:, ::2], SWIGLU_LIMIT)
        up = jnp.clip(h[:, 1::2], -SWIGLU_LIMIT, SWIGLU_LIMIT)
        act = (up + 1.0) * (gate * jax.nn.sigmoid(SWIGLU_ALPHA * gate))
        return act @ w_down[e] + b_down[e]

    y_pad = lax.map(expert_block, (x_pad.reshape(n_blocks, MOE_BLOCK, D), block_expert)).reshape(P, D)
    contrib = y_pad[dest] * g_s[:, None].astype(y_pad.dtype)
    return jax.ops.segment_sum(contrib, tok_s, num_segments=N)

def setup_inputs(seed: int = 0) -> dict:
    key = jax.random.key(seed)
    ks = jax.random.split(key, 17)

    def nrm(k, shape, scale):
        return jax.random.normal(k, shape, jnp.float32) * scale

    return {
        'x': nrm(ks[0], (BATCH, SEQ, D_MODEL), 1.0),
        'norm_mix_g': 1.0 + nrm(ks[1], (DEPTH, D_MODEL), 0.02),
        'w_in': nrm(ks[2], (DEPTH, D_MODEL, IN_WIDTH), D_MODEL ** -0.5),
        'gla_gate_up': nrm(ks[3], (DEPTH, GLA_GATE_RANK, GLA_K_WIDTH), GLA_GATE_RANK ** -0.5),
        'gla_gate_bias': nrm(ks[4], (DEPTH, GLA_K_WIDTH), 0.1),
        'gla_norm_g': 1.0 + nrm(ks[5], (DEPTH, GLA_DV), 0.02),
        'w_branch_gla': nrm(ks[6], (DEPTH, GLA_V_WIDTH, D_MODEL), GLA_V_WIDTH ** -0.5),
        'w_branch_att': nrm(ks[7], (DEPTH, ATT_OUT_WIDTH, D_MODEL), ATT_OUT_WIDTH ** -0.5),
        'w_mix_out': nrm(ks[8], (DEPTH, D_MODEL, D_MODEL), D_MODEL ** -0.5),
        'norm_ffn_g': 1.0 + nrm(ks[9], (DEPTH, D_MODEL), 0.02),
        'router_w': nrm(ks[10], (DEPTH, D_MODEL, N_EXPERTS), D_MODEL ** -0.5),
        'router_b': nrm(ks[11], (DEPTH, N_EXPERTS), 0.01),
        'expert_w_gate_up': nrm(ks[12], (DEPTH, N_EXPERTS, D_MODEL, 2 * EXPERT_FF), D_MODEL ** -0.5),
        'expert_b_gate_up': nrm(ks[13], (DEPTH, N_EXPERTS, 2 * EXPERT_FF), 0.01),
        'expert_w_down': nrm(ks[14], (DEPTH, N_EXPERTS, EXPERT_FF, D_MODEL), EXPERT_FF ** -0.5),
        'expert_b_down': nrm(ks[15], (DEPTH, N_EXPERTS, D_MODEL), 0.01),
        'norm_final_g': 1.0 + nrm(ks[16], (D_MODEL,), 0.02),
    }

def reference(x, norm_mix_g, w_in, gla_gate_up, gla_gate_bias, gla_norm_g, w_branch_gla, w_branch_att,
              w_mix_out, norm_ffn_g, router_w, router_b, expert_w_gate_up, expert_b_gate_up,
              expert_w_down, expert_b_down, norm_final_g):
    B, S, D = x.shape
    h = x
    for l in range(DEPTH):
        h = h + hybrid_mixer(rmsnorm(h, norm_mix_g[l]), w_in[l], gla_gate_up[l], gla_gate_bias[l],
                             gla_norm_g[l], w_branch_gla[l], w_branch_att[l], w_mix_out[l])
        hn = rmsnorm(h, norm_ffn_g[l]).reshape(B * S, D)
        h = h + moe(hn, router_w[l], router_b[l], expert_w_gate_up[l], expert_b_gate_up[l],
                    expert_w_down[l], expert_b_down[l]).reshape(B, S, D)
    return rmsnorm(h, norm_final_g)


_drawn_inputs = setup_inputs


def setup_inputs(seed=0):
    import zlib

    import numpy as np

    out = dict(_drawn_inputs(seed))
    spreads = {}
    factors = {'expert_b_gate_up': 8.0, 'expert_b_down': 8.0, 'norm_final_g': 2.859}
    for name, (base, spread) in spreads.items():
        noise = np.random.default_rng([zlib.crc32(name.encode()), seed]).standard_normal(out[name].shape)
        drawn = base * np.exp(spread * noise) if base else spread * noise
        out[name] = jnp.asarray(drawn.astype(out[name].dtype))
    for name, factor in factors.items():
        out[name] = (out[name] * factor).astype(out[name].dtype)
    return out
```

```python
import math
from contextlib import ExitStack, contextmanager

import numpy as np

import concourse.bass as bass
from concourse import mybir

F32 = mybir.dt.float32
F32R = mybir.dt.float32r
I32 = mybir.dt.int32
U32 = mybir.dt.uint32
ALU = mybir.AluOpType
ACT = mybir.ActivationFunctionType
AX = mybir.AxisListType

P = 128
SEQ, D_MODEL = 512, 1024
NB = SEQ // P
KT = D_MODEL // P
HALF_KT = KT // 2
COLS = 512

GLA_HEADS, GLA_DK, GLA_DV, GLA_CHUNK, GLA_RANK = 4, 128, 256, 64, 16
GLA_TAU = 16.0
GLA_K_WIDTH, GLA_V_WIDTH = GLA_HEADS * GLA_DK, GLA_HEADS * GLA_DV
N_CHUNKS = SEQ // GLA_CHUNK

ATT_GROUPS = ((128, 1), (512, 4), (2048, 16))
ATT_HEADS, HEAD_DIM, ROT_DIM, ROPE_THETA = 8, 64, 16, 500000.0
RES = 4
ATT_OUT = ATT_HEADS * HEAD_DIM
ATT_QKV = len(ATT_GROUPS) * ATT_OUT
ATT_KEYS = SEQ + P + P
MASKED = -1.0e30

COL_GQ = 0
COL_GK = COL_GQ + GLA_K_WIDTH
COL_GV = COL_GK + GLA_K_WIDTH
COL_GR = COL_GV + GLA_V_WIDTH
COL_GLR = COL_GR + GLA_V_WIDTH
COL_AQ = COL_GLR + GLA_RANK
COL_AV = COL_AQ + 2 * ATT_QKV
COL_GATE = COL_AV + ATT_QKV

N_EXPERTS, TOP_K, FF = 32, 4, D_MODEL
SWIGLU_LIMIT, SWIGLU_ALPHA = 7.0, 1.702
EPS = 1e-5


def shape_constants():
    c = {}
    c["identity"] = np.eye(P, dtype=np.float32)
    half = ROT_DIM // 2
    inv = (np.float32(ROPE_THETA) ** (-np.arange(half, dtype=np.float32) * np.float32(2.0 / ROT_DIM))).astype(np.float32)
    ang = (np.arange(SEQ, dtype=np.float32)[:, None] * inv[None, :]).astype(np.float32)
    cos, sin = np.cos(ang).astype(np.float32), np.sin(ang).astype(np.float32)
    c["rope"] = np.concatenate([cos, cos, -sin, sin], axis=1).astype(np.float32)
    t, r = np.arange(P), np.arange(RES)
    q = (RES * t[None, :] + r[:, None])[:, :, None]
    k0 = np.arange(SEQ)[None, None, :]
    window = ATT_GROUPS[0][0]
    ok0 = (q - k0 >= 0) & (q - k0 <= window)
    lag = np.broadcast_to(t[:, None] - t[None, :], (RES, P, P))
    ok1 = lag >= 0
    ok2 = (lag >= 0) & (lag % (ATT_GROUPS[2][1] // RES) == 0)
    ok = np.concatenate([ok0, ok1, ok2], axis=2)
    c["att_mask"] = np.where(ok, 0.0, MASKED).astype(np.float32)
    i = np.arange(P)
    same = (i[:, None] // GLA_CHUNK) == (i[None, :] // GLA_CHUNK)
    c["gla_mask"] = np.where((i[:, None] <= i[None, :]) & same, np.finfo(np.float32).max, 0).astype(np.float32)
    keep = np.ones((P, GLA_HEADS * SEQ), np.float32)
    keep[:, ::GLA_CHUNK] = 0.0
    c["scan_keep"] = keep
    c["before"] = (i[:, None] < i[None, :]).astype(np.float32)
    c["slot_numbers"] = np.broadcast_to(np.arange(P, dtype=np.float32), (P, P)).copy()
    c["expert_numbers"] = np.broadcast_to(np.arange(N_EXPERTS, dtype=np.float32), (P, N_EXPERTS)).copy()
    c["token_numbers"] = (np.arange(NB)[None, :] * P + i[:, None]).astype(np.float32)
    c["block_starts"] = np.broadcast_to(np.arange(SEQ * TOP_K // P, dtype=np.float32) * P, (P, SEQ * TOP_K // P)).copy()
    e = np.zeros((P, N_EXPERTS), np.float32)
    for x in range(N_EXPERTS):
        e[x, x] = e[N_EXPERTS + x, x] = 1.0
    c["bias_row"] = e
    return c


CONSTANTS = shape_constants()


class Chain:

    def __init__(self, engine, semaphore):
        self.engine, self.semaphore, self.at, self.n = engine, semaphore, 0, 0

    def __call__(self, instruction):
        instruction.then_inc(self.semaphore, 1)
        self.n += 1
        self.engine.wait_ge(self.semaphore, self.at + self.n)

    def enter(self, i, per_iteration):
        self.before = self.at + self.n
        self.at, self.n = self.before + i * per_iteration, 0

    def leave(self, iterations, per_iteration):
        assert self.n == per_iteration, (self.n, per_iteration)
        self.at, self.n = self.before + iterations * per_iteration, 0


class Kernel:
    def __init__(self, nc, t):
        self.nc, self.t, self.groups = nc, t, 0

    def sem(self, name):
        handle = self.nc.alloc_semaphore(name=name)
        if self.stage_sems is not None:
            self.stage_sems.append(handle)
        return handle

    @contextmanager
    def stage(self):
        self.stage_sems = []
        with ExitStack() as stack:
            yield stack
        self.nc.clear_and_free_semaphores(self.stage_sems)
        self.nc.all_engine_barrier()
        self.stage_sems = None

    def sb(self, stack, name, shape, dt=F32):
        return stack.enter_context(self.nc.sbuf_tensor(name, shape, dt))

    def build(self):
        nc = self.nc
        with ExitStack() as top:
            self.stage_sems = None
            self.bank = [top.enter_context(nc.psum_tensor(f"bank{i}", [P, COLS], F32)) for i in range(8)]
            self.chain_sem = {e: self.sem(f"chain_{e}") for e in ("pe", "act", "dve", "pool", "sp")}
            self.chain = {}
            self.loaded = [self.sem(f"chunk_loaded{c}") for c in range(2)]
            self.hi_done = [self.sem(f"chunk_hi_done{c}") for c in range(2)]
            self.lo_done = [self.sem(f"chunk_lo_done{c}") for c in range(2)]
            self.chunk_used = self.sem("chunk0_used")
            self.bank_full = [self.sem(f"bank_full{b}") for b in range(NB)]
            self.bank_free = [self.sem(f"bank_free{b}") for b in range(NB)]
            self.ident = self.sb(top, "identity_sb", [P, P])
            self.rank = self.sb(top, "rank_in_expert", [P, NB, N_EXPERTS])
            self.pairs = self.sb(top, "token_and_weight", [P, NB, N_EXPERTS, 2])
            self.place = self.sb(top, "place_in_further", [P, NB, N_EXPERTS])
            self.block_expert = self.sb(top, "further_block_expert", [P, self.FURTHER], I32)
            self.n_further = self.sb(top, "further_blocks", [P, 1], I32)
            self.normed = nc.dram_tensor("normed_rows", [SEQ, D_MODEL], F32).ap()
            self.total = nc.dram_tensor("residual_rows", [SEQ, D_MODEL], F32).ap()
            with ExitStack() as mixer:
                self.mixer(mixer)
            with self.stage() as s:
                self.experts(s)
            with self.stage() as s:
                self.further_blocks(s)
            with self.stage() as s:
                self.normalise_output(s)

    def link(self, name, engine):
        c = self.chain.setdefault(name, Chain(engine, self.chain_sem[name]))
        c.engine = engine
        return c

    def mixer(self, stack):
        self.x_hi = self.sb(stack, "xT_hi", [P, KT, SEQ], F32R)
        self.x_lo = self.sb(stack, "xT_lo", [P, KT, SEQ], F32R)
        self.ring(stack)
        with self.stage() as s:
            self.normalise_input(s)
        self.yg = self.sb(stack, "y_glaT", [P, KT, SEQ])
        with ExitStack() as s:
            self.gla(s)
        self.ya = self.sb(stack, "y_attT", [P, HALF_KT, SEQ])
        with ExitStack() as s:
            self.attention(s)
        with ExitStack() as s:
            self.merge(s)

    def normalise_input(self, stack):
        nc, t = self.nc, self.t
        x = self.sb(stack, "x_sb", [P, NB, D_MODEL])
        sq = self.sb(stack, "x_squares", [P, D_MODEL])
        ss = self.sb(stack, "x_sum_squares", [P, NB])
        rs = self.sb(stack, "x_rstd", [P, NB])
        g = self.sb(stack, "norm_mix_g_col", [P, KT])
        xg = self.sb(stack, "xg", [P, 2, HALF_KT, P])
        minus_half = self.sb(stack, "minus_half0", [P, 1])
        x_in = [self.sem(f"x_in{b}") for b in range(NB)]
        consts_in, sums, powed, scaled = self.sem("consts0_in"), self.sem("x_sums"), self.sem("x_powed"), self.sem("x_scaled")
        turned, xg_done, xh_done, xl_done = self.sem("x_turned"), self.sem("xg_done"), self.sem("xh_done"), self.sem("xl_done")
        with nc.Block() as block:
            @block.sync
            def _(sp):
                for b in range(NB):
                    sp.dma_start(x[:, b, :], t["x"][0, b * P:(b + 1) * P, :]).then_inc(x_in[b], 16)
                sp.dma_start(self.ident[:], t["identity"]).then_inc(consts_in, 16)
                sp.dma_start(g[:], t["norm_mix_g"][0].rearrange("(k p) -> p k", p=P),
                             allow_slow_non_contiguous=True).then_inc(consts_in, 16)

            @block.gpsimd
            def _(pool):
                link = self.link("pool", pool)
                link(pool.memset(minus_half[:], -0.5))
                pool.wait_ge(sums, 1)
                pool.tensor_tensor(rs[:], ss[:], minus_half[:, 0:1].to_broadcast([P, NB]), ALU.pow).then_inc(powed, 1)

            @block.vector
            def _(dve):
                link = self.link("dve", dve)
                for b in range(NB):
                    dve.wait_ge(x_in[b], 16)
                    link(dve.scalar_tensor_tensor(out=sq[:], in0=x[:, b, :], scalar=1.0, in1=x[:, b, :],
                                                  op0=ALU.mult, op1=ALU.mult, accum_out=ss[:, b:b + 1]))
                dve.tensor_scalar(ss[:], ss[:], 1.0 / D_MODEL, EPS, ALU.mult, ALU.add).then_inc(sums, 1)
                dve.wait_ge(powed, 1)
                for b in range(NB):
                    dve.tensor_scalar(x[:, b, :], x[:, b, :], rs[:, b:b + 1], None, ALU.mult).then_inc(scaled, 1)
                dve.wait_ge(consts_in, 32)
                for i in range(2 * NB):
                    b, h = divmod(i, 2)
                    dve.wait_ge(turned, i + 1)
                    if i >= 2:
                        dve.wait_ge(xh_done, i - 1)
                        dve.wait_ge(xl_done, i - 1)
                    dve.tensor_tensor(xg[:, i % 2], self.bank[i % 2][:].rearrange("p (k n) -> p k n", n=P),
                                      g[:, HALF_KT * h:HALF_KT * (h + 1)].unsqueeze(2).to_broadcast([P, HALF_KT, P]),
                                      ALU.mult).then_inc(xg_done, 1)
                    dve.wait_ge(xg_done, i + 1)
                    dve.wait_ge(xh_done, i + 1)
                    dst = (slice(None), slice(HALF_KT * h, HALF_KT * (h + 1)), slice(b * P, (b + 1) * P))
                    dve.tensor_tensor(self.x_lo[dst], xg[:, i % 2], self.x_hi[dst].bitcast(F32),
                                      ALU.subtract).then_inc(xl_done, 1)

            @block.scalar
            def _(act):
                for i in range(2 * NB):
                    b, h = divmod(i, 2)
                    act.wait_ge(xg_done, i + 1)
                    act.copy(self.x_hi[:, HALF_KT * h:HALF_KT * (h + 1), b * P:(b + 1) * P],
                             xg[:, i % 2]).then_inc(xh_done, 1)

            @block.tensor
            def _(pe):
                pe.wait_ge(consts_in, 32)
                for i in range(2 * NB):
                    b, h = divmod(i, 2)
                    pe.wait_ge(scaled, b + 1)
                    if i >= 2:
                        pe.wait_ge(xg_done, i - 1)
                    for k in range(HALF_KT):
                        last = pe.transpose(self.bank[i % 2][:, k * P:(k + 1) * P],
                                            x[:, b, (HALF_KT * h + k) * P:(HALF_KT * h + k + 1) * P], self.ident[:])
                    last.then_inc(turned, 1)

    def ring(self, stack):
        self.raw = [self.sb(stack, f"chunk{c}", [P, HALF_KT, COLS]) for c in range(2)]
        self.whi = [self.sb(stack, f"chunk_hi{c}", [P, HALF_KT, COLS], F32R) for c in range(2)]
        self.wlo = [self.sb(stack, f"chunk_lo{c}", [P, HALF_KT, COLS], F32R) for c in range(2)]

    def load_group(self, sp, g, source):
        for c in range(2):
            sp.wait_ge(self.lo_done[c], g)
            sp.dma_start(self.raw[c][:], source(c)).then_inc(self.loaded[c], 16)

    def split_hi(self, act, g, c):
        act.wait_ge(self.loaded[c], g * 16 + 16)
        act.wait_ge(self.bank_full[NB - 1] if c else self.chunk_used, g)
        act.copy(self.whi[c][:], self.raw[c][:]).then_inc(self.hi_done[c], 1)

    def split_lo(self, dve, g, c):
        dve.wait_ge(self.hi_done[c], g + 1)
        dve.tensor_tensor(self.wlo[c][:], self.raw[c][:], self.whi[c][:].bitcast(F32),
                          ALU.subtract).then_inc(self.lo_done[c], 1)

    def multiply_group(self, pe, g, tokens, weights_stay=False, lhs=None, between=None):
        x_hi, x_lo = lhs or (self.x_hi, self.x_lo)
        for c in range(2):
            pe.wait_ge(self.lo_done[c], g + 1)
            for b in range(NB):
                if c == 0:
                    pe.wait_ge(self.bank_free[b], g)
                for kk in range(HALF_KT):
                    k = HALF_KT * c + kk
                    hi, lo = self.whi[c], self.wlo[c]
                    if weights_stay:
                        col = slice(b * P, (b + 1) * P)
                        passes = ((hi[:, kk, col], x_hi[:, k, :]), (hi[:, kk, col], x_lo[:, k, :]),
                                  (lo[:, kk, col], x_hi[:, k, :]))
                    else:
                        tok = tokens(b)
                        passes = ((x_hi[:, k, tok], hi[:, kk, :]), (x_hi[:, k, tok], lo[:, kk, :]),
                                  (x_lo[:, k, tok], hi[:, kk, :]))
                    for n, (stationary, moving) in enumerate(passes):
                        last = pe.matmul(self.bank[b][:], stationary, moving, start=(k == 0 and n == 0),
                                         stop=(k == KT - 1 and n == 2))
                if c == 1:
                    last.then_inc(self.bank_full[b], 1)
            if c == 0:
                last.then_inc(self.chunk_used, 1)
                if between:
                    between()

    def w_in_chunk(self, col):
        def source(c):
            return self.t["w_in"][0, c * HALF_KT * P:(c + 1) * HALF_KT * P, bass.ds(col, COLS)].rearrange(
                "(k p) n -> p k n", p=P)
        return source

    @staticmethod
    def block_of(b):
        return slice(b * P, (b + 1) * P)

    @staticmethod
    def residue(b):
        return slice(b, SEQ, RES)

    def run_groups(self, kind, engine, base, n, source=None, tokens=None, weights_stay=False, lhs=None,
                   evacuate=None, first_split=False, next_split=False):
        def step(i, last):
            g = base + i
            if kind == "load":
                self.load_group(engine, g, lambda c: source(i)(c))
            elif kind == "multiply":
                self.multiply_group(engine, g, tokens, weights_stay, lhs)
            else:
                split = self.split_hi if kind == "hi" else self.split_lo
                more = next_split or not last
                if more:
                    split(engine, g + 1, 0)
                if evacuate:
                    for b in range(NB):
                        engine.wait_ge(self.bank_full[b], g + 1)
                        evacuate(i, b).then_inc(self.bank_free[b], 1)
                if more:
                    split(engine, g + 1, 1)

        if first_split and kind in ("hi", "lo"):
            for c in range(2):
                (self.split_hi if kind == "hi" else self.split_lo)(engine, base, c)
        if kind in ("load", "multiply"):
            with engine.Fori(0, n) as i:
                step(i, False)
        else:
            if n > 1:
                with engine.Fori(0, n - 1) as i:
                    step(i, False)
            step(n - 1, True)

    def gla(self, stack):
        nc, t = self.nc, self.t
        H, L = GLA_HEADS, SEQ
        qk = self.sb(stack, "gla_qkT", [P, 2, H, L])
        v = self.sb(stack, "gla_v", [P, NB, GLA_V_WIDTH])
        sg = self.sb(stack, "gla_silu_r", [P, NB, GLA_V_WIDTH])
        b_sum = self.sb(stack, "decay_sums", [P, H, L])
        with self.stage() as s:
            self.gla_project(s, qk, v, sg, b_sum)
        with self.stage() as s:
            self.gla_heads(s, qk, v, sg, b_sum)

    def gla_project(self, stack, qk, v, sg, b_sum):
        nc, t = self.nc, self.t
        H, L = GLA_HEADS, SEQ
        base = self.groups
        z = self.sb(stack, "decay_z", [P, H, L])
        soft = self.sb(stack, "decay_soft", [P, H, L])
        keep = self.sb(stack, "scan_keep_sb", [P, H * L])
        w_lr = self.sb(stack, "w_lr", [P, KT, P])
        w_lr_hi = self.sb(stack, "w_lr_hi", [P, KT, P], F32R)
        w_lr_lo = self.sb(stack, "w_lr_lo", [P, KT, P], F32R)
        lrT = self.sb(stack, "lrT", [GLA_RANK, L])
        up = self.sb(stack, "gate_up_sb", [GLA_RANK, GLA_K_WIDTH])
        bias = self.sb(stack, "gate_bias_col", [P, H])
        g_row = self.sb(stack, "gla_norm_g_row", [P, GLA_DV])
        small_in, lr_in = self.sem("gla_small_in"), self.sem("w_lr_in")
        lr_hi, lr_lo, lr_full, lr_out = (self.sem(n) for n in ("lr_hi_done", "lr_lo_done", "lr_full", "lr_out"))
        z_full, z_out, soft_done, silu_done = (self.sem(n) for n in ("z_full", "z_out", "soft_done", "silu_done"))
        GROUPS_QK, GROUPS_V, GROUPS_R = 2 * GLA_K_WIDTH // COLS, GLA_V_WIDTH // COLS, GLA_V_WIDTH // COLS
        base_v, base_r = base + GROUPS_QK, base + GROUPS_QK + GROUPS_V
        self.groups = base_r + GROUPS_R

        with nc.Block() as block:
            @block.sync
            def _(sp):
                self.load_group(sp, base, self.w_in_chunk(COL_GQ))
                sp.dma_start(w_lr[:], t["w_in"][0, :, COL_GLR:COL_GLR + P].rearrange("(k p) n -> p k n", p=P)
                             ).then_inc(lr_in, 16)
                sp.dma_start(up[:], t["gla_gate_up"][0]).then_inc(small_in, 16)
                sp.dma_start(bias[:], t["gla_gate_bias"][0].rearrange("(h p) -> p h", p=P),
                             allow_slow_non_contiguous=True).then_inc(small_in, 16)
                sp.dma_start(keep[:], t["scan_keep"]).then_inc(small_in, 16)
                sp.dma_start(g_row[:], t["gla_norm_g"][0:1, :].partition_broadcast(P).rearrange("p a n -> p (a n)")).then_inc(small_in, 16)
                with sp.Fori(1, 2 * 3) as i:
                    self.load_group(sp, base + i, lambda c: self.w_in_chunk(COL_GQ + COLS * i)(c))

            @block.tensor
            def _(pe):
                pe.wait_ge(lr_lo, 1)
                for k in range(KT):
                    for n, (w, x) in enumerate(((w_lr_hi, self.x_hi), (w_lr_hi, self.x_lo), (w_lr_lo, self.x_hi))):
                        last = pe.matmul(self.bank[4][:], w[:, k, :], x[:, k, :], start=(k == 0 and n == 0),
                                         stop=(k == KT - 1 and n == 2))
                last.then_inc(lr_full, 1)
                pe.wait_ge(small_in, 64)
                pe.wait_ge(lr_out, 1)
                for h in range(H):
                    pe.matmul(self.bank[4 + h][:], up[:, h * P:(h + 1) * P], lrT[:],
                              start=True, stop=True).then_inc(z_full, 1)
                self.run_groups("multiply", pe, base, GROUPS_QK, weights_stay=True)
                self.run_groups("multiply", pe, base_v, GROUPS_V, tokens=self.block_of)
                self.run_groups("multiply", pe, base_r, GROUPS_R, tokens=self.block_of)

            @block.scalar
            def _(act):
                link = self.link("act", act)
                for c in range(2):
                    self.split_hi(act, base, c)
                act.wait_ge(lr_in, 16)
                act.copy(w_lr_hi[:], w_lr[:]).then_inc(lr_hi, 1)
                act.wait_ge(lr_full, 1)
                act.copy(lrT[:], self.bank[4][0:GLA_RANK, :]).then_inc(lr_out, 1)
                act.wait_ge(z_out, H)
                link(act.activation(soft[:], z[:], ACT.Abs))
                link(act.activation(soft[:], soft[:], ACT.Exp, scale=-1.0))
                act.activation(soft[:], soft[:], ACT.Ln, bias=1.0).then_inc(soft_done, 1)
                self.run_groups("hi", act, base, GROUPS_QK, next_split=True,
                                evacuate=lambda i, b: act.copy(qk[:, i, b, :] if isinstance(i, int) else
                                                               qk[:, bass.ds(i, 1), b, :].rearrange("p a n -> p (a n)"),
                                                               self.bank[b][:]))
                self.run_groups("hi", act, base_v, GROUPS_V, next_split=True,
                                evacuate=lambda i, b: act.copy(v[:, b, bass.ds(i * COLS, COLS)], self.bank[b][:]))
                self.run_groups("hi", act, base_r, GROUPS_R,
                                evacuate=lambda i, b: act.activation(sg[:, b, bass.ds(i * COLS, COLS)],
                                                                     self.bank[b][:], ACT.Silu))

            @block.vector
            def _(dve):
                link = self.link("dve", dve)
                for c in range(2):
                    self.split_lo(dve, base, c)
                dve.wait_ge(lr_hi, 1)
                dve.tensor_tensor(w_lr_lo[:], w_lr[:], w_lr_hi[:].bitcast(F32), ALU.subtract).then_inc(lr_lo, 1)
                dve.wait_ge(small_in, 64)
                for h in range(H):
                    dve.wait_ge(z_full, h + 1)
                    dve.tensor_scalar(z[:, h, :], self.bank[4 + h][:], bias[:, h:h + 1], None,
                                      ALU.add).then_inc(z_out, 1)
                self.split_lo(dve, base + 1, 0)
                self.split_lo(dve, base + 1, 1)
                dve.wait_ge(soft_done, 1)
                link(dve.scalar_tensor_tensor(out=z[:], in0=z[:], scalar=0.0, in1=soft[:], op0=ALU.min,
                                              op1=ALU.subtract))
                link(dve.tensor_tensor_scan(b_sum[:].rearrange("p h n -> p (h n)"), keep[:],
                                            z[:].rearrange("p h n -> p (h n)"), 0.0, ALU.mult, ALU.add))
                with dve.Fori(2, 2 * 3) as i:
                    for c in range(2):
                        self.split_lo(dve, base + i, c)
                dve.wait_ge(self.bank_free[NB - 1], base_r + GROUPS_R)
                for b in range(NB):
                    dve.wait_ge(self.bank_free[b], base_r + GROUPS_R)
                    r = sg[:, b, :].rearrange("p (h n) -> p h n", h=H)
                    link(dve.tensor_tensor(r, r, g_row[:].unsqueeze(1).to_broadcast([P, H, GLA_DV]), ALU.mult))

    def gla_heads(self, stack, qk, v, sg, b_sum):
        nc, t = self.nc, self.t
        H, L, C = GLA_HEADS, SEQ, GLA_CHUNK
        grow = self.sb(stack, "exp_b", [P, L])
        fade = self.sb(stack, "exp_minus_b", [P, L])
        rest = self.sb(stack, "exp_last_minus_b", [P, L])
        qe = self.sb(stack, "q_decayed", [P, L])
        ke = self.sb(stack, "k_decayed", [P, L])
        kdT = self.sb(stack, "k_to_chunk_endT", [P, L])
        kd = self.sb(stack, "k_to_chunk_end", [P, NB, P])
        at = self.sb(stack, "products_masked", [P, NB, P])
        mask = self.sb(stack, "gla_mask_sb", [P, P])
        anti = self.sb(stack, "gla_mask_negated", [P, P])
        state = self.sb(stack, "gla_state", [P, N_CHUNKS, GLA_DV])
        sq = self.sb(stack, "gla_squares", [P, GLA_DV])
        ss = self.sb(stack, "gla_sum_squares", [P, NB])
        rs = self.sb(stack, "gla_rstd", [P, NB])
        y = self.sb(stack, "gla_y", [P, NB, GLA_DV])
        vh = self.sb(stack, "gla_v_head", [P, NB, GLA_DV])
        minus_half = self.sb(stack, "minus_half1", [P, 1])
        S = {n: self.sem("gla_" + n) for n in (
            "mask_in", "state_zeroed", "clamped", "half_set", "exps", "to_end", "decayed", "kd_turned", "kd_out", "products",
            "masked", "updates", "state_done", "o_full", "squared", "mean_done", "powed", "y_done", "y_turned",
            "y_out", "v_staged")}
        flat = lambda ap: ap.rearrange("p a n -> p (a n)")
        u_bank = lambda c: self.bank[c % 4][:, (c // 4) * GLA_DV:(c // 4 + 1) * GLA_DV]
        o_bank = lambda n: self.bank[6 + n // 2][:, (n % 2) * GLA_DV:(n % 2 + 1) * GLA_DV]
        chunk = lambda c: slice(c * C, (c + 1) * C)
        UPDATES = N_CHUNKS - 1

        with nc.Block() as block:
            @block.sync
            def _(sp):
                sp.dma_start(mask[:], t["gla_mask"]).then_inc(S["mask_in"], 16)

            @block.gpsimd
            def _(pool):
                pool.memset(state[:, 0, :], 0.0).then_inc(S["state_zeroed"], 1)
                pool.memset(minus_half[:], -0.5).then_inc(S["half_set"], 1)
                pool.wait_ge(S["half_set"], 1)
                for h in range(H):
                    if h:
                        pool.wait_ge(S["o_full"], 2 * h)
                    pool.tensor_copy(vh[:], v[:, :, h * GLA_DV:(h + 1) * GLA_DV]).then_inc(S["v_staged"], 1)
                    pool.wait_ge(S["mean_done"], h + 1)
                    if h:
                        pool.wait_ge(S["y_done"], NB * h)
                    pool.tensor_tensor(rs[:], ss[:], minus_half[:, 0:1].to_broadcast([P, NB]),
                                       ALU.pow).then_inc(S["powed"], 1)

            @block.scalar
            def _(act):
                with act.Fori(0, H) as h:
                    b_h = flat(b_sum[:, bass.ds(h, 1), :])
                    act.wait_ge(S["decayed"], h * 3)
                    act.wait_ge(S["state_done"], h * UPDATES)
                    act.activation(grow[:], b_h, ACT.Exp, scale=1.0 / GLA_TAU).then_inc(S["exps"], 1)
                    act.activation(fade[:], b_h, ACT.Exp, scale=-1.0 / GLA_TAU).then_inc(S["exps"], 1)
                    act.wait_ge(S["to_end"], h + 1)
                    act.activation(rest[:], rest[:], ACT.Exp, scale=1.0 / GLA_TAU).then_inc(S["exps"], 1)
                    act.wait_ge(S["kd_turned"], h + 1)
                    act.wait_ge(S["updates"], h)
                    act.copy(flat(kd[:]), self.bank[4][:]).then_inc(S["kd_out"], 1)
                    for n in range(NB):
                        act.wait_ge(S["o_full"], h * 2 + n // 2 + 1)
                        act.wait_ge(S["squared"], h * NB + n)
                        act.wait_ge(S["powed"], h)
                        act.activation(sq[:], o_bank(n), ACT.Square, accum_out=ss[:, n:n + 1]).then_inc(S["squared"], 1)
                    for d in range(2):
                        act.wait_ge(S["y_turned"], h * 2 + d + 1)
                        act.copy(flat(self.yg[:, bass.ds(2 * h + d, 1), :]), self.bank[4 + d][:]).then_inc(S["y_out"], 1)

            @block.vector
            def _(dve):
                link = self.link("dve", dve)
                dve.wait_ge(S["mask_in"], 16)
                link(dve.tensor_scalar(anti[:], mask[:], -1.0, None, ALU.mult))
                with dve.Fori(0, H) as h:
                    by_chunk = lambda ap: ap.rearrange("p (c n) -> p c n", n=C)
                    b_c = by_chunk(flat(b_sum[:, bass.ds(h, 1), :]))
                    dve.wait_ge(S["decayed"], 3 * h)
                    dve.tensor_tensor(by_chunk(rest[:]), b_c[:, :, C - 1:C].to_broadcast([P, N_CHUNKS, C]), b_c,
                                      ALU.subtract).then_inc(S["to_end"], 1)
                    q_h = qk[:, 0, bass.ds(h, 1), :].rearrange("p a n -> p (a n)")
                    k_h = qk[:, 1, bass.ds(h, 1), :].rearrange("p a n -> p (a n)")
                    dve.wait_ge(S["exps"], 3 * h + 1)
                    dve.wait_ge(S["o_full"], 2 * h)
                    dve.scalar_tensor_tensor(out=qe[:], in0=q_h, scalar=float(GLA_DK) ** -0.5, in1=grow[:],
                                             op0=ALU.mult, op1=ALU.mult).then_inc(S["decayed"], 1)
                    dve.wait_ge(S["exps"], 3 * h + 2)
                    dve.tensor_tensor(ke[:], k_h, fade[:], ALU.mult).then_inc(S["decayed"], 1)
                    dve.wait_ge(S["exps"], 3 * h + 3)
                    dve.tensor_tensor(kdT[:], k_h, rest[:], ALU.mult).then_inc(S["decayed"], 1)
                    dve.wait_ge(S["products"], h + 1)
                    over = lambda m: m[:].unsqueeze(1).to_broadcast([P, NB, P])
                    dve.tensor_tensor(at[:], self.bank[5][:].rearrange("p (a n) -> p a n", n=P), over(mask),
                                      ALU.min).then_inc(S["clamped"], 1)
                    dve.wait_ge(S["clamped"], h + 1)
                    dve.tensor_tensor(at[:], at[:], over(anti), ALU.max).then_inc(S["masked"], 1)
                    for c in range(UPDATES):
                        dve.wait_ge(S["updates"], h + 1)
                        done = h * UPDATES + c
                        dve.wait_ge(S["state_done"], done)
                        if c == 0:
                            dve.tensor_copy(state[:, 1, :], u_bank(0)).then_inc(S["state_done"], 1)
                        else:
                            dve.scalar_tensor_tensor(out=state[:, c + 1, :], in0=state[:, c, :],
                                                     scalar=grow[:, c * C + C - 1:c * C + C], in1=u_bank(c),
                                                     op0=ALU.mult, op1=ALU.add).then_inc(S["state_done"], 1)
                    dve.wait_ge(S["squared"], NB * h + NB)
                    dve.tensor_scalar(ss[:], ss[:], 1.0 / GLA_DV, EPS, ALU.mult, ALU.add).then_inc(S["mean_done"], 1)
                    dve.wait_ge(S["powed"], h + 1)
                    for n in range(NB):
                        dve.wait_ge(S["y_turned"], 2 * h)
                        dve.scalar_tensor_tensor(out=y[:, n, :], in0=o_bank(n), scalar=rs[:, n:n + 1],
                                                 in1=sg[:, n, bass.ds(h * GLA_DV, GLA_DV)],
                                                 op0=ALU.mult, op1=ALU.mult).then_inc(S["y_done"], 1)

            @block.tensor
            def _(pe):
                pe.wait_ge(S["state_zeroed"], 1)
                with pe.Fori(0, H) as h:
                    pe.wait_ge(S["y_out"], 2 * h)
                    pe.wait_ge(S["decayed"], 3 * h + 3)
                    for n in range(NB):
                        last = pe.transpose(self.bank[4][:, n * P:(n + 1) * P], kdT[:, n * P:(n + 1) * P], self.ident[:])
                    last.then_inc(S["kd_turned"], 1)
                    for n in range(NB):
                        blk = self.block_of(n)
                        last = pe.matmul(self.bank[5][:, blk], ke[:, blk], qe[:, blk], start=True, stop=True)
                    last.then_inc(S["products"], 1)
                    pe.wait_ge(S["kd_out"], h + 1)
                    pe.wait_ge(S["v_staged"], h + 1)
                    for c in range(UPDATES):
                        half = slice((c % 2) * C, (c % 2 + 1) * C)
                        last = pe.matmul(u_bank(c), kd[half, c // 2, :], vh[half, c // 2, :], start=True, stop=True)
                    last.then_inc(S["updates"], 1)
                    pe.wait_ge(S["masked"], h + 1)
                    for n in range(NB):
                        pe.wait_ge(S["y_done"], NB * h)
                        pe.matmul(o_bank(n), at[:, n, :], vh[:, n, :], start=True, stop=False)
                        for c in (2 * n, 2 * n + 1):
                            if c:
                                pe.wait_ge(S["state_done"], h * UPDATES + c)
                            last = pe.matmul(o_bank(n)[(c % 2) * C:(c % 2 + 1) * C, :], qe[:, chunk(c)],
                                             state[:, c, :], start=False, stop=True)
                        if n % 2:
                            last.then_inc(S["o_full"], 1)
                    pe.wait_ge(S["y_done"], NB * h + NB)
                    for d in range(2):
                        for n in range(NB):
                            last = pe.transpose(self.bank[4 + d][:, n * P:(n + 1) * P],
                                                y[:, n, d * P:(d + 1) * P], self.ident[:])
                        last.then_inc(S["y_turned"], 1)

    def attention(self, stack):
        G = len(ATT_GROUPS)
        q = self.sb(stack, "att_qT", [P, G * HALF_KT, SEQ])
        k = self.sb(stack, "att_kT", [P, G * HALF_KT, SEQ])
        v = self.sb(stack, "att_v", [P, G, NB, ATT_OUT])
        with self.stage() as s:
            self.att_project(s, q, k, v)
        with self.stage() as s:
            self.att_heads(s, q, k, v)

    def att_project(self, stack, q, k, v):
        nc, t = self.nc, self.t
        G, HALF = len(ATT_GROUPS), ROT_DIM // 2
        base, base_v = self.groups, self.groups + 2 * G
        self.groups = base_v + G
        row = self.sb(stack, "qk_rows", [P, NB, COLS])
        turn = self.sb(stack, "rope_products", [P, 2, ATT_HEADS, ROT_DIM])
        rope = self.sb(stack, "rope_sb", [P, NB, 2 * ROT_DIM])
        rope_in, rotated, turned, stored = (self.sem("att_" + n) for n in ("rope_in", "rotated", "turned", "stored"))
        prod, summed = self.sem("att_rope_products"), self.sem("att_rope_read")

        with nc.Block() as block:
            @block.sync
            def _(sp):
                sp.dma_start(rope[:], t["rope"].rearrange("(b p) n -> p b n", p=P)).then_inc(rope_in, 16)
                with sp.Fori(0, 3 * G) as i:
                    self.load_group(sp, base + i, lambda c: self.w_in_chunk(COL_AQ + COLS * i)(c))

            @block.tensor
            def _(pe):
                def turn_rows(i):
                    for b in range(NB):
                        pe.wait_ge(rotated, NB * i + b + 1)
                        pe.wait_ge(stored, NB * i)
                        for d in range(HALF_KT):
                            last = pe.transpose(self.bank[4 + b][:, d * P:(d + 1) * P],
                                                row[:, b, d * P:(d + 1) * P], self.ident[:])
                        last.then_inc(turned, 1)

                def qk_group(i, before=None):
                    self.multiply_group(pe, base + i, self.block_of, between=before)

                qk_group(0)
                with pe.Fori(1, 2 * G) as i:
                    qk_group(i, lambda: turn_rows(i - 1))
                self.multiply_group(pe, base_v, self.block_of, between=lambda: turn_rows(2 * G - 1))
                self.run_groups("multiply", pe, base_v + 1, G - 1, tokens=self.residue)

            @block.scalar
            def _(act):
                for c in range(2):
                    self.split_hi(act, base, c)

                def rows_out(i, b):
                    act.wait_ge(turned, NB * i)
                    return act.copy(row[:, b, :], self.bank[b][:])

                self.run_groups("hi", act, base, 2 * G, next_split=True, evacuate=rows_out)
                self.run_groups("hi", act, base_v, G,
                                evacuate=lambda i, b: act.copy(v[:, i, b, :] if isinstance(i, int) else
                                                               v[:, bass.ds(i, 1), b, :].rearrange("p a n -> p (a n)"),
                                                               self.bank[b][:]))

            @block.vector
            def _(dve):
                for c in range(2):
                    self.split_lo(dve, base, c)
                dve.wait_ge(rope_in, 16)

                def rotate(i, qk, at):
                    for b in range(NB):
                        heads = row[:, b, :].rearrange("p (h n) -> p h n", n=HEAD_DIM)
                        table = lambda a, n: rope[:, b, a:a + n].unsqueeze(1).to_broadcast([P, ATT_HEADS, n])
                        dve.wait_ge(self.bank_free[b], base + i + 1)
                        dve.wait_ge(rotated, NB * i + b)
                        dve.tensor_tensor(turn[:, 0], heads[:, :, 0:ROT_DIM], table(0, ROT_DIM), ALU.mult).then_inc(prod, 1)
                        dve.tensor_tensor(turn[:, 1, :, 0:HALF], heads[:, :, HALF:ROT_DIM], table(ROT_DIM, HALF),
                                          ALU.mult).then_inc(prod, 1)
                        dve.tensor_tensor(turn[:, 1, :, HALF:], heads[:, :, 0:HALF], table(ROT_DIM + HALF, HALF),
                                          ALU.mult).then_inc(prod, 1)
                        dve.wait_ge(prod, 3 * (NB * i + b + 1))
                        dve.tensor_tensor(heads[:, :, 0:ROT_DIM], turn[:, 0], turn[:, 1], ALU.add).then_inc(rotated, 1)
                    for b in range(NB):
                        dve.wait_ge(turned, NB * i + b + 1)
                        dve.tensor_copy(qk[:, bass.ds(at * HALF_KT, HALF_KT), b * P:(b + 1) * P],
                                        self.bank[4 + b][:].rearrange("p (d n) -> p d n", n=P)).then_inc(stored, 1)

                for first, qk in ((0, q), (G, k)):
                    with dve.Fori(0, G) as i:
                        for c in range(2):
                            self.split_lo(dve, base + first + i + 1, c)
                        rotate(first + i, qk, i)
                with dve.Fori(2 * G + 1, 3 * G) as i:
                    for c in range(2):
                        self.split_lo(dve, base + i, c)

    def att_heads(self, stack, q, k, v):
        nc, t = self.nc, self.t
        G, PAIRS, TILES = len(ATT_GROUPS), ATT_HEADS // 2, ATT_KEYS // P
        mask = self.sb(stack, "att_mask_sb", [P, 2, ATT_KEYS])
        qs = self.sb(stack, "att_q_step", [P, 2, G, P])
        s_ = self.sb(stack, "att_probs", [P, 2, ATT_KEYS])
        pT = self.sb(stack, "att_probsT", [P, TILES, P])
        low = self.sb(stack, "att_minus_max", [P, 2])
        den = self.sb(stack, "att_sum", [P, 2])
        inv = self.sb(stack, "att_inverse_sum", [P, 2])
        y = self.sb(stack, "att_y", [P, 2, ATT_OUT])
        S = {n: self.sem("att_" + n) for n in ("q_staged", "scores", "masked", "max_done", "exp_done", "probs_turned",
                                               "probsT_a", "probsT_b", "pv_done", "inv_done", "y_done", "y_turned", "y_out")}
        mask_in = [self.sem(f"att_mask_in{i}") for i in range(2)]
        SCALE = HEAD_DIM ** -0.5
        with nc.Block() as block:
            @block.sync
            def _(sp):
                for r in range(RES):
                    if r >= 2:
                        sp.wait_ge(S["masked"], 4 * PAIRS * (r - 1))
                    sp.dma_start(mask[:, r % 2, :], t["att_mask"][r]).then_inc(mask_in[r % 2], 16)

            for_r = range(RES)

            @block.gpsimd
            def _(pool):
                for r in for_r:
                    for p in range(PAIRS):
                        n = r * PAIRS + p
                        if n >= 2:
                            pool.wait_ge(S["scores"], 2 * (n - 1))
                        pool.tensor_copy(qs[:, n % 2], q[:, p:p + 2 * HALF_KT + 1:HALF_KT, r:SEQ:RES]).then_inc(S["q_staged"], 1)

            @block.tensor
            def _(pe):
                for r in for_r:
                    for p in range(PAIRS):
                        n = r * PAIRS + p
                        pe.wait_ge(S["q_staged"], n + 1)
                        for h in range(2):
                            part = slice(h * HEAD_DIM, (h + 1) * HEAD_DIM)
                            if n:
                                pe.wait_ge(S["masked"], 4 * n)
                            pe.matmul(self.bank[h][:], qs[part, n % 2, 0, :], k[part, p, :], start=True, stop=True)
                            for g in (1, 2):
                                last = pe.matmul(self.bank[2 + h][:, (g - 1) * P:g * P], qs[part, n % 2, g, :],
                                                 k[part, g * HALF_KT + p, r:SEQ:RES], start=True, stop=True)
                            last.then_inc(S["scores"], 1)
                        for h in range(2):
                            m = 2 * n + h
                            pe.wait_ge(S["exp_done"], m + 1)
                            if m:
                                pe.wait_ge(S["probsT_a"], m)
                                pe.wait_ge(S["probsT_b"], m)
                            for i in range(TILES):
                                last = pe.transpose(self.bank[4 + i // 4][:, (i % 4) * P:(i % 4 + 1) * P],
                                                    s_[:, h, i * P:(i + 1) * P], self.ident[:])
                                if i == 3:
                                    last.then_inc(S["probs_turned"], 1)
                            last.then_inc(S["probs_turned"], 1)
                            pe.wait_ge(S["probsT_a"], m + 1)
                            pe.wait_ge(S["probsT_b"], m + 1)
                            if m:
                                pe.wait_ge(S["y_done"], m)
                            cols = slice((2 * p + h) * HEAD_DIM, (2 * p + h + 1) * HEAD_DIM)
                            for i in range(TILES):
                                val = v[:, 0, i, cols] if i < NB else v[:, i - NB + 1, r, cols]
                                last = pe.matmul(self.bank[6][:, 0:HEAD_DIM], pT[:, i, :], val, start=(i == 0),
                                                 stop=(i == TILES - 1))
                            last.then_inc(S["pv_done"], 1)
                    pe.wait_ge(S["y_done"], 2 * PAIRS * (r + 1))
                    if r:
                        pe.wait_ge(S["y_out"], r)
                    for d in range(HALF_KT):
                        last = pe.transpose(self.bank[7][:, d * P:(d + 1) * P], y[:, r % 2, d * P:(d + 1) * P], self.ident[:])
                    last.then_inc(S["y_turned"], 1)

            @block.scalar
            def _(act):
                for r in for_r:
                    for p in range(PAIRS):
                        for h in range(2):
                            m = 2 * (r * PAIRS + p) + h
                            act.wait_ge(S["max_done"], m + 1)
                            act.activation(s_[:, h, :], s_[:, h, :], ACT.Exp, bias=low[:, h:h + 1], scale=SCALE,
                                           accum_out=den[:, h:h + 1]).then_inc(S["exp_done"], 1)
                        for h in range(2):
                            m = 2 * (r * PAIRS + p) + h
                            act.wait_ge(S["probs_turned"], 2 * m + 1)
                            if m:
                                act.wait_ge(S["pv_done"], m)
                            act.copy(pT[:, 0:NB, :].rearrange("p a n -> p (a n)"), self.bank[4][:]).then_inc(S["probsT_a"], 1)
                    act.wait_ge(S["y_turned"], r + 1)
                    act.copy(self.ya[:, :, r:SEQ:RES], self.bank[7][:].rearrange("p (d n) -> p d n", n=P)).then_inc(S["y_out"], 1)

            @block.vector
            def _(dve):
                link = self.link("dve", dve)
                for r in for_r:
                    dve.wait_ge(mask_in[r % 2], 16 * (r // 2 + 1))
                    for p in range(PAIRS):
                        n = r * PAIRS + p
                        for h in range(2):
                            m = 2 * n + h
                            dve.wait_ge(S["scores"], m + 1)
                            if m >= 2:
                                dve.wait_ge(S["probs_turned"], 2 * (m - 1))
                                dve.wait_ge(S["exp_done"], m - 1)
                            dve.tensor_tensor(s_[:, h, 0:SEQ], self.bank[h][:], mask[:, r % 2, 0:SEQ], ALU.add).then_inc(S["masked"], 1)
                            dve.tensor_tensor(s_[:, h, SEQ:], self.bank[2 + h][:, 0:2 * P], mask[:, r % 2, SEQ:], ALU.add).then_inc(S["masked"], 1)
                            dve.wait_ge(S["masked"], 2 * m + 2)
                            link(dve.tensor_reduce(low[:, h:h + 1], s_[:, h, :], AX.X, ALU.max))
                            dve.tensor_scalar(low[:, h:h + 1], low[:, h:h + 1], -SCALE, None, ALU.mult).then_inc(S["max_done"], 1)
                        for h in range(2):
                            m = 2 * n + h
                            dve.wait_ge(S["probs_turned"], 2 * m + 2)
                            if m:
                                dve.wait_ge(S["pv_done"], m)
                            dve.tensor_copy(pT[:, NB:, :].rearrange("p a n -> p (a n)"), self.bank[5][:, 0:2 * P]).then_inc(S["probsT_b"], 1)
                            dve.wait_ge(S["exp_done"], m + 1)
                            link(dve.reciprocal(inv[:, h:h + 1], den[:, h:h + 1]))
                            dve.wait_ge(S["pv_done"], m + 1)
                            if r >= 2:
                                dve.wait_ge(S["y_turned"], r - 1)
                            dve.tensor_scalar(y[:, r % 2, (2 * p + h) * HEAD_DIM:(2 * p + h + 1) * HEAD_DIM],
                                              self.bank[6][:, 0:HEAD_DIM], inv[:, h:h + 1], None, ALU.mult).then_inc(S["y_done"], 1)

    def chunk_of(self, w, col):
        def source(c):
            return w[c * HALF_KT * P:(c + 1) * HALF_KT * P, bass.ds(col, COLS)].rearrange("(k p) n -> p k n", p=P)
        return source

    def merge(self, stack):
        nc, t = self.nc, self.t
        self.h = self.sb(stack, "h_sb", [P, NB, D_MODEL])
        with self.stage() as s:
            self.gates_and_branches(s)
        with self.stage() as s:
            self.route(s)

    def gates_and_branches(self, stack):
        nc, t = self.nc, self.t
        GATES, GLA, MIX = 2 * D_MODEL // COLS, D_MODEL // COLS, D_MODEL // COLS
        base = self.groups
        base_gla = base + GATES
        base_att = base_gla + GLA
        base_mix = base_att + 1
        self.groups = base_mix + MIX
        gate = self.sb(stack, "gatesT", [P, 2 * KT, SEQ])
        yg_hi = self.sb(stack, "y_glaT_hi", [P, KT, SEQ], F32R)
        yg_lo = self.sb(stack, "y_glaT_lo", [P, KT, SEQ], F32R)
        part = self.sb(stack, "gated_att", [P, 2, SEQ])
        ya_hi, ya_lo = (self.sb(stack, n, [P, HALF_KT, SEQ], F32R) for n in ("y_attT_hi", "y_attT_lo"))
        S = {n: self.sem("mix_" + n) for n in ("y_hi", "y_lo", "x_in", "gla_gated", "att_part", "att_added", "merged_hi",
                                               "merged_lo", "att_free", "gates_ready")}
        att_full = [self.sem(f"att_branch_full{b}") for b in range(NB)]
        merged = self.yg
        w_gla, w_att, w_mix = t["w_branch_gla"][0], t["w_branch_att"][0], t["w_mix_out"][0]

        with nc.Block() as block:
            @block.sync
            def _(sp):
                with sp.Fori(0, GATES) as i:
                    self.load_group(sp, base + i, lambda c: self.w_in_chunk(COL_GATE + COLS * i)(c))
                sp.dma_start(self.h[:], t["x"][0].rearrange("(b p) n -> p b n", p=P)).then_inc(S["x_in"], 16)
                for i in range(GLA):
                    self.load_group(sp, base_gla + i, self.chunk_of(w_gla, i * COLS))
                self.load_group(sp, base_att, lambda c: w_att[:, c * COLS:(c + 1) * COLS].rearrange("(k p) n -> p k n", p=P))
                for i in range(MIX):
                    self.load_group(sp, base_mix + i, self.chunk_of(w_mix, i * COLS))

            @block.tensor
            def _(pe):
                self.run_groups("multiply", pe, base, GATES, weights_stay=True)
                pe.wait_ge(S["y_lo"], 2)
                for i in range(GLA):
                    self.multiply_group(pe, base_gla + i, None, weights_stay=True, lhs=(yg_hi, yg_lo))
                for c in range(2):
                    pe.wait_ge(self.lo_done[c], base_att + 1)
                    for b in range(NB):
                        bank = self.bank[b] if c else self.bank[4 + b]
                        if c:
                            pe.wait_ge(self.bank_free[b], base_att)
                        for k in range(HALF_KT):
                            col = slice(b * P, (b + 1) * P)
                            for n, (w, y) in enumerate(((self.whi, ya_hi), (self.whi, ya_lo), (self.wlo, ya_hi))):
                                last = pe.matmul(bank[:], w[c][:, k, col], y[:, k, :], start=(k == 0 and n == 0),
                                                 stop=(k == HALF_KT - 1 and n == 2))
                        last.then_inc(self.bank_full[b] if c else att_full[b], 1)
                        if c == 0 and b == NB - 1:
                            pe.wait_ge(att_full[b], 1)
                            pe.sem_inc(self.chunk_used, 1)
                pe.wait_ge(S["merged_lo"], KT)
                for i in range(MIX):
                    self.multiply_group(pe, base_mix + i, self.block_of)

            @block.scalar
            def _(act):
                for c in range(2):
                    self.split_hi(act, base, c)
                act.copy(yg_hi[:], self.yg[:]).then_inc(S["y_hi"], 1)
                act.copy(ya_hi[:], self.ya[:]).then_inc(S["y_hi"], 1)
                def gate_out(i, b):
                    return act.activation(gate[:, bass.ds(4 * i + b, 1), :].rearrange("p a n -> p (a n)"),
                                          self.bank[b][:], ACT.Sigmoid)
                self.run_groups("hi", act, base, GATES, next_split=True, evacuate=gate_out)
                act.wait_ge(self.bank_free[NB - 1], base + GATES)
                for b in range(NB):
                    act.wait_ge(self.bank_free[b], base + GATES)
                act.sem_inc(S["gates_ready"], 1)
                for i in range(1, GLA + 2):
                    for c in range(2):
                        self.split_hi(act, base_gla + i, c)
                for m in range(KT):
                    act.wait_ge(S["att_added"], m + 1)
                    if m == 0:
                        act.wait_ge(self.bank_full[NB - 1], base_gla)
                    act.copy(self.x_hi[:, m, :], merged[:, m, :]).then_inc(S["merged_hi"], 1)
                for c in range(2):
                    self.split_hi(act, base_mix + 1, c)

            @block.vector
            def _(dve):
                for c in range(2):
                    self.split_lo(dve, base, c)
                for n, (lo, y, hi) in enumerate(((yg_lo, self.yg, yg_hi), (ya_lo, self.ya, ya_hi))):
                    dve.wait_ge(S["y_hi"], n + 1)
                    dve.tensor_tensor(lo[:], y[:], hi[:].bitcast(F32), ALU.subtract).then_inc(S["y_lo"], 1)
                with dve.Fori(1, GATES + 1) as i:
                    for c in range(2):
                        self.split_lo(dve, base + i, c)
                dve.wait_ge(S["gates_ready"], 1)
                dve.wait_ge(S["y_lo"], 2)
                for i in range(GLA):
                    self.split_lo(dve, base_gla + i + 1, 0)
                    for b in range(NB):
                        m = NB * i + b
                        dve.wait_ge(self.bank_full[b], base_gla + i + 1)
                        dve.tensor_tensor(merged[:, m, :], gate[:, m, :], self.bank[b][:], ALU.mult).then_inc(self.bank_free[b], 1)
                    self.split_lo(dve, base_gla + i + 1, 1)
                self.split_lo(dve, base_mix, 0)
                self.split_lo(dve, base_mix, 1)
                for m in range(KT):
                    c, b = divmod(m, NB)
                    dve.wait_ge(self.bank_full[b] if c else att_full[b], base_att + 1 if c else 1)
                    if m >= 2:
                        dve.wait_ge(S["att_added"], m - 1)
                    bank = self.bank[b] if c else self.bank[4 + b]
                    dve.tensor_tensor(part[:, m % 2], gate[:, KT + m, :], bank[:], ALU.mult).then_inc(
                        self.bank_free[b] if c else S["att_part"], 1)
                    dve.wait_ge(self.bank_free[b] if c else S["att_part"], base_att + 1 if c else m + 1)
                    dve.wait_ge(self.bank_free[b], base_att)
                    dve.tensor_tensor(merged[:, m, :], merged[:, m, :], part[:, m % 2], ALU.add).then_inc(S["att_added"], 1)
                    if m:
                        self.merged_lo(dve, S, merged, m - 1)
                self.merged_lo(dve, S, merged, KT - 1)
                self.split_lo(dve, base_mix + 1, 0)
                self.split_lo(dve, base_mix + 1, 1)
                dve.wait_ge(S["x_in"], 16)
                for i in range(MIX):
                    for b in range(NB):
                        dve.wait_ge(self.bank_full[b], base_mix + i + 1)
                        part_h = self.h[:, b, i * COLS:(i + 1) * COLS]
                        dve.tensor_tensor(part_h, part_h, self.bank[b][:], ALU.add).then_inc(self.bank_free[b], 1)

    def merged_lo(self, dve, S, merged, m):
        dve.wait_ge(S["merged_hi"], m + 1)
        dve.tensor_tensor(self.x_lo[:, m, :], merged[:, m, :], self.x_hi[:, m, :].bitcast(F32),
                          ALU.subtract).then_inc(S["merged_lo"], 1)


    def route(self, stack):
        nc, t = self.nc, self.t
        h = self.h
        E = N_EXPERTS
        sq = self.sb(stack, "h_squares", [P, D_MODEL])
        ss = self.sb(stack, "h_sum_squares", [P, NB])
        rs = self.sb(stack, "h_rstd", [P, NB])
        g = self.sb(stack, "norm_ffn_g_row", [P, D_MODEL])
        hn = self.sb(stack, "hn", [P, NB, D_MODEL])
        hT = self.sb(stack, "hnT", [P, KT, SEQ])
        rw = self.sb(stack, "router_w_sb", [P, KT, E])
        rb = self.sb(stack, "router_b_row", [P, E])
        logits = self.sb(stack, "logits", [P, NB, E])
        top = self.sb(stack, "top_logits", [P, NB, 8])
        who = self.sb(stack, "top_experts", [P, NB, 8], U32)
        who_f = self.sb(stack, "top_experts_f", [P, NB, TOP_K])
        low = self.sb(stack, "minus_top", [P, NB])
        ex = self.sb(stack, "top_exps", [P, NB, TOP_K])
        tot = self.sb(stack, "top_sums", [P, NB])
        weight = self.sb(stack, "top_weights", [P, NB, TOP_K])
        hot = self.sb(stack, "one_hot", [P, NB, E])
        hot_w = self.sb(stack, "one_hot_weighted", [P, NB, E])
        sel = self.sb(stack, "selected", [P, NB, E])
        wsum = self.sb(stack, "weights", [P, NB, E])
        before = self.sb(stack, "before_sb", [P, P])
        ones = self.sb(stack, "ones_sb", [P, P])
        e_no = self.sb(stack, "expert_numbers_sb", [P, E])
        tok = self.sb(stack, "token_numbers_sb", [P, NB])
        half = self.sb(stack, "minus_half2", [P, 1])
        extra, run, past, ones_e = (self.sb(stack, n, [P, E]) for n in ("extra_blocks", "extra_sums", "past", "ones_e"))
        starts = self.sb(stack, "block_starts_sb", [P, self.FURTHER])
        cmp = self.sb(stack, "blocks_before", [P, self.FURTHER, E])
        be = self.sb(stack, "block_expert_f", [P, self.FURTHER])
        far = self.sb(stack, "beyond_first_block", [P, NB, E])
        S = {n: self.sem("route_" + n) for n in ("in", "sums", "powed", "hn_done", "stored", "turned", "hT_out", "logits",
                                                 "low", "exps", "selected", "ranks")}
        with nc.Block() as block:
            @block.sync
            def _(sp):
                sp.dma_start(g[:], t["norm_ffn_g"][0:1, :].partition_broadcast(P).rearrange("p a n -> p (a n)")).then_inc(S["in"], 16)
                sp.dma_start(rw[:], t["router_w"][0].rearrange("(k p) n -> p k n", p=P)).then_inc(S["in"], 16)
                sp.dma_start(rb[:], t["router_b"][0:1, :].partition_broadcast(P).rearrange("p a n -> p (a n)")).then_inc(S["in"], 16)
                sp.dma_start(before[:], t["before"]).then_inc(S["in"], 16)
                sp.dma_start(e_no[:], t["expert_numbers"]).then_inc(S["in"], 16)
                sp.dma_start(tok[:], t["token_numbers"]).then_inc(S["in"], 16)
                sp.dma_start(starts[:], t["block_starts"]).then_inc(S["in"], 16)
                sp.dma_start(self.total.rearrange("(b p) n -> p b n", p=P), h[:]).then_inc(S["stored"], 16)
                sp.wait_ge(S["hn_done"], NB)
                sp.dma_start(self.normed.rearrange("(b p) n -> p b n", p=P), hn[:]).then_inc(S["stored"], 16)
                sp.wait_ge(S["stored"], 32)

            @block.gpsimd
            def _(pool):
                link = self.link("pool", pool)
                pool.memset(ones[:], 1.0)
                link(pool.memset(half[:], -0.5))
                pool.wait_ge(S["sums"], 1)
                pool.tensor_tensor(rs[:], ss[:], half[:, 0:1].to_broadcast([P, NB]), ALU.pow).then_inc(S["powed"], 1)

            @block.tensor
            def _(pe):
                for b in range(NB):
                    pe.wait_ge(S["hn_done"], b + 1)
                    for hf in range(2):
                        i = 2 * b + hf
                        if i >= 2:
                            pe.wait_ge(S["hT_out"], i - 1)
                        for k in range(HALF_KT):
                            last = pe.transpose(self.bank[i % 2][:, k * P:(k + 1) * P],
                                                hn[:, b, (HALF_KT * hf + k) * P:(HALF_KT * hf + k + 1) * P], self.ident[:])
                        last.then_inc(S["turned"], 1)
                pe.wait_ge(S["in"], 7 * 16)
                pe.wait_ge(S["hT_out"], 2 * NB)
                for b in range(NB):
                    for k in range(KT):
                        last = pe.matmul(self.bank[2][:, b * E:(b + 1) * E], hT[:, k, b * P:(b + 1) * P], rw[:, k, :],
                                         start=(k == 0), stop=(k == KT - 1))
                last.then_inc(S["logits"], 1)
                pe.wait_ge(S["selected"], 1)
                pe.wait_ge(S["powed"], 1)
                for b in range(NB):
                    for a in range(b + 1):
                        last = pe.matmul(self.bank[3][:, b * E:(b + 1) * E], (before if a == b else ones)[:], sel[:, a, :],
                                         start=(a == 0), stop=(a == b))
                for a in range(NB):
                    last = pe.matmul(self.bank[4][:, 0:E], ones[:], sel[:, a, :], start=(a == 0), stop=(a == NB - 1))
                last.then_inc(S["ranks"], 1)

            @block.scalar
            def _(act):
                for i in range(2 * NB):
                    b, hf = divmod(i, 2)
                    act.wait_ge(S["turned"], i + 1)
                    act.copy(hT[:, HALF_KT * hf:HALF_KT * (hf + 1), b * P:(b + 1) * P],
                             self.bank[i % 2][:].rearrange("p (k n) -> p k n", n=P)).then_inc(S["hT_out"], 1)
                act.wait_ge(S["low"], 1)
                for b in range(NB):
                    act.activation(ex[:, b, :], top[:, b, 0:TOP_K], ACT.Exp, bias=low[:, b:b + 1],
                                   accum_out=tot[:, b:b + 1]).then_inc(S["exps"], 1)

            @block.vector
            def _(dve):
                link = self.link("dve", dve)
                for b in range(NB):
                    link(dve.scalar_tensor_tensor(out=sq[:], in0=h[:, b, :], scalar=1.0, in1=h[:, b, :], op0=ALU.mult,
                                                  op1=ALU.mult, accum_out=ss[:, b:b + 1]))
                dve.tensor_scalar(ss[:], ss[:], 1.0 / D_MODEL, EPS, ALU.mult, ALU.add).then_inc(S["sums"], 1)
                dve.wait_ge(S["in"], 7 * 16)
                dve.wait_ge(S["powed"], 1)
                for b in range(NB):
                    dve.scalar_tensor_tensor(out=hn[:, b, :], in0=h[:, b, :], scalar=rs[:, b:b + 1], in1=g[:],
                                             op0=ALU.mult, op1=ALU.mult).then_inc(S["hn_done"], 1)
                dve.wait_ge(S["logits"], 1)
                link(dve.tensor_tensor(logits[:], self.bank[2][:, 0:NB * E].rearrange("p (b n) -> p b n", n=E),
                                       rb[:].unsqueeze(1).to_broadcast([P, NB, E]), ALU.add))
                for b in range(NB):
                    link(dve.max(top[:, b, :], logits[:, b, :]))
                    link(dve.max_index(who[:, b, :], top[:, b, :], logits[:, b, :]))
                dve.tensor_scalar(low[:], top[:, :, 0], -1.0, None, ALU.mult).then_inc(S["low"], 1)
                link(dve.tensor_copy(who_f[:], who[:, :, 0:TOP_K]))
                dve.wait_ge(S["exps"], NB)
                link(dve.reciprocal(tot[:], tot[:]))
                link(dve.tensor_tensor(weight[:], ex[:], tot[:].unsqueeze(2).to_broadcast([P, NB, TOP_K]), ALU.mult))
                for k in range(TOP_K):
                    dst, dst_w = (hot, hot_w) if k else (sel, wsum)
                    link(dve.tensor_tensor(dst[:], e_no[:].unsqueeze(1).to_broadcast([P, NB, E]),
                                           who_f[:, :, k:k + 1].to_broadcast([P, NB, E]), ALU.is_equal))
                    link(dve.tensor_tensor(dst_w[:], dst[:], weight[:, :, k:k + 1].to_broadcast([P, NB, E]), ALU.mult))
                    if k:
                        link(dve.tensor_tensor(sel[:], sel[:], hot[:], ALU.add))
                        link(dve.tensor_tensor(wsum[:], wsum[:], hot_w[:], ALU.add))
                dve.sem_inc(S["selected"], 1)
                dve.tensor_copy(self.pairs[:, :, :, 1], wsum[:])
                dve.tensor_scalar(self.pairs[:, :, :, 0], tok[:].unsqueeze(2).to_broadcast([P, NB, E]), 1.0, None, ALU.add)
                dve.wait_ge(S["ranks"], 1)
                link(dve.scalar_tensor_tensor(out=self.rank[:], in0=self.bank[3][:, 0:NB * E].rearrange("p (b n) -> p b n", n=E),
                                              scalar=1.0, in1=sel[:], op0=ALU.add, op1=ALU.mult))
                link(dve.tensor_scalar(self.rank[:], self.rank[:], -1.0, None, ALU.add))
                counts = self.bank[4][:, 0:E]
                link(dve.tensor_scalar(extra[:], counts, float(P), None, ALU.is_gt))
                for n in range(2, NB):
                    link(dve.tensor_scalar(past[:], counts, float(n * P), None, ALU.is_gt))
                    link(dve.tensor_tensor(extra[:], extra[:], past[:], ALU.add))
                link(dve.memset(ones_e[:], 1.0))
                link(dve.tensor_tensor_scan(run[:], ones_e[:], extra[:], 0.0, ALU.mult, ALU.add))
                link(dve.tensor_copy(self.n_further[:], run[:, E - 1:E]))
                link(dve.tensor_scalar(past[:], run[:], float(P), None, ALU.mult))
                link(dve.tensor_tensor(cmp[:], past[:].unsqueeze(1).to_broadcast([P, self.FURTHER, E]),
                                       starts[:].unsqueeze(2).to_broadcast([P, self.FURTHER, E]), ALU.is_le))
                link(dve.tensor_reduce(be[:], cmp[:], AX.X, ALU.add))
                link(dve.tensor_scalar(self.block_expert[:], be[:], float(E - 1), None, ALU.min))
                link(dve.tensor_scalar(extra[:], extra[:], -float(P), 1.0 - P, ALU.mult, ALU.add))
                link(dve.tensor_tensor(extra[:], extra[:], past[:], ALU.add))
                link(dve.tensor_scalar(far[:], self.rank[:], float(P), None, ALU.is_ge))
                link(dve.tensor_tensor(self.place[:], self.rank[:], extra[:].unsqueeze(1).to_broadcast([P, NB, E]), ALU.add))
                link(dve.tensor_tensor(self.place[:], self.place[:], far[:], ALU.mult))
                link(dve.tensor_scalar(self.place[:], self.place[:], -1.0, None, ALU.add))

    CHUNKS, PER_HALF, SLOTS, WIDE = 12, 4, 3, 1024
    FURTHER = SEQ * TOP_K // P

    def experts(self, stack):
        nc, t = self.nc, self.t
        E, N, W = N_EXPERTS, self.CHUNKS, self.WIDE
        wgu, wd = t["expert_w_gate_up"][0], t["expert_w_down"][0]
        raw = [self.sb(stack, f"expert_chunk{j}", [P, 2, W]) for j in range(N)]
        whi = [self.sb(stack, f"expert_hi{j}", [P, 2, W], F32R) for j in range(self.SLOTS)]
        wlo = [self.sb(stack, f"expert_lo{j}", [P, 2, W], F32R) for j in range(self.SLOTS)]
        bias = self.sb(stack, "bias_hi_lo", [P, 3 * W], F32R)
        rows = self.sb(stack, "rows_in", [P, W])
        x_hi, x_lo = (self.sb(stack, n, [P, KT, P], F32R) for n in ("rowsT_hi", "rowsT_lo"))
        gv = self.sb(stack, "gate_values", [P, 2, W // 4])
        uv = self.sb(stack, "up_values", [P, 2, W // 4])
        sg = self.sb(stack, "gate_sigmoid", [P, 2, W // 4])
        a = self.sb(stack, "activations", [P, FF])
        a_hi, a_lo = (self.sb(stack, n, [P, KT, P], F32R) for n in ("activationsT_hi", "activationsT_lo"))
        y = self.sb(stack, "rows_out", [P, W])
        hot = self.sb(stack, "slots_one_hot", [P, NB, P])
        slot_no = self.sb(stack, "slot_numbers_sb", [P, P])
        bias_row = self.sb(stack, "bias_row_sb", [P, E])
        pick = self.sb(stack, "bias_pick", [P, P], F32R)
        none = self.sb(stack, "empty_slot", [P, 1])
        index = [self.sb(stack, f"row_index{u}", [P, 1], I32) for u in range(2)]
        weight = [self.sb(stack, f"row_weight{u}", [P, 1]) for u in range(2)]
        S = {n: self.sem("moe_" + n) for n in (
            "tables_in", "bias_in", "bias_hi", "hi", "lo", "slots_free", "hA_full", "hB_full", "gu", "sig", "p", "act",
            "act_turned", "aT_hi", "aT_lo", "y_full", "y_out", "scattered", "hot", "listed", "none", "index", "gathered",
            "x_turned", "x_hi", "x_lo", "picked", "cleared", "bias_zeroed", "bias_lo", "passed")}
        loaded = [self.sem(f"expert_chunk_loaded{j}") for j in range(N)]
        h_full = (S["hA_full"], S["hB_full"])
        QUARTER = W // 4

        def weights(e, j):
            if j < 2 * self.PER_HALF:
                half, k = divmod(j, self.PER_HALF)
                src = wgu[bass.ds(e, 1), k * 2 * P:(k + 1) * 2 * P, half * W:(half + 1) * W]
            else:
                k = j - 2 * self.PER_HALF
                src = wd[bass.ds(e, 1), k * 2 * P:(k + 1) * 2 * P, :]
            return src.rearrange("a (k p) n -> p (a k) n", p=P)

        def hi(act, e, j):
            act.wait_ge(loaded[j], 16 * e + 16)
            act.wait_ge(S["slots_free"], N * e + j + 1)
            act.copy(whi[j % self.SLOTS][:], raw[j][:]).then_inc(S["hi"], 1)

        def lo(dve, e, j):
            dve.wait_ge(S["hi"], N * e + j + 1)
            s = j % self.SLOTS
            dve.tensor_tensor(wlo[s][:], raw[j][:], whi[s][:].bitcast(F32), ALU.subtract).then_inc(S["lo"], 1)

        def list_hot(dve, e):
            dve.wait_ge(S["listed"], e)
            dve.tensor_tensor(hot[:], slot_no[:].unsqueeze(1).to_broadcast([P, NB, P]),
                              self.rank[:, :, bass.ds(e, 1)].to_broadcast([P, NB, P]), ALU.is_equal).then_inc(S["hot"], 1)

        def list_rows(pe, e):
            pe.wait_ge(S["hot"], e + 1)
            pe.wait_ge(S["y_out"], 2 * e - 2) if not isinstance(e, int) or e else None
            for b in range(NB):
                last = pe.matmul(self.bank[4][:, 0:2], hot[:, b, :],
                                 self.pairs[:, b, bass.ds(e, 1), :].rearrange("p a n -> p (a n)"),
                                 start=(b == 0), stop=(b == NB - 1))
            last.then_inc(S["listed"], 1)

        def list_index(dve, e, u):
            dve.wait_ge(S["listed"], e + 1)
            dve.wait_ge(S["index"], 2 * e)
            if not isinstance(e, int) or e:
                dve.wait_ge(S["scattered"], 16 * (e - 1))
            dve.tensor_scalar(none[:], self.bank[4][:, 0:1], 0.0, 8.0 * SEQ, ALU.is_equal, ALU.mult).then_inc(S["none"], 1)
            dve.wait_ge(S["none"], e + 1)
            dve.scalar_tensor_tensor(out=index[u][:], in0=none[:], scalar=-1.0, in1=self.bank[4][:, 0:1],
                                     op0=ALU.add, op1=ALU.add).then_inc(S["index"], 1)
            dve.tensor_copy(weight[u][:], self.bank[4][:, 1:2]).then_inc(S["index"], 1)

        def gather(pool, e, u):
            pool.wait_ge(S["index"], 2 * e + 2)
            if not isinstance(e, int) or e:
                pool.wait_ge(S["x_turned"], 2 * e)
            pool.sem_inc(S["passed"], 1)
            pool.indirect_dma_start(rows[:], None, self.normed, bass.IndirectOffsetOnAxis(ap=index[u][:, 0:1], axis=0),
                                    bounds_check=self.last_row, oob_is_err=False).then_inc(S["gathered"], 16)

        def turn_rows(pe, e):
            pe.wait_ge(S["gathered"], 16 * e + 16)
            pe.wait_ge(S["aT_lo"], 2 * e)
            for f in range(2):
                for k in range(HALF_KT):
                    last = pe.transpose(self.bank[6 + f][:, k * P:(k + 1) * P],
                                        rows[:, (HALF_KT * f + k) * P:(HALF_KT * f + k + 1) * P], self.ident[:])
                last.then_inc(S["x_turned"], 1)

        def split_turned(eng, e, part, f, turned, first, second, hi_t, lo_t):
            dst = slice(HALF_KT * f, HALF_KT * (f + 1))
            bank = self.bank[6 + f][:].rearrange("p (k n) -> p k n", n=P)
            if part == "hi":
                eng.wait_ge(turned, 2 * e + f + 1)
                eng.copy(hi_t[:, dst, :], bank).then_inc(first, 1)
            else:
                eng.wait_ge(first, 2 * e + f + 1)
                eng.tensor_tensor(lo_t[:, dst, :], bank, hi_t[:, dst, :].bitcast(F32), ALU.subtract).then_inc(second, 1)

        x_part = lambda eng, e, part, f: split_turned(eng, e, part, f, S["x_turned"], S["x_hi"], S["x_lo"], x_hi, x_lo)
        a_part = lambda eng, e, part, f: split_turned(eng, e, part, f, S["act_turned"], S["aT_hi"], S["aT_lo"], a_hi, a_lo)

        def pick_bias(dve, e):
            dve.tensor_copy(pick[:], bias_row[:, bass.ds(e, 1)].to_broadcast([P, P])).then_inc(S["picked"], 1)

        def expert_pe(pe, e, more):
            for j in range(N):
                s = j % self.SLOTS
                stage, k = divmod(j, self.PER_HALF)
                banks = [self.bank[2 * stage + i] for i in range(2)]
                t_hi, t_lo = (a_hi, a_lo) if stage == 2 else (x_hi, x_lo)
                if j == 0:
                    pe.wait_ge(S["x_lo"], 2 * e + 2)
                    pe.wait_ge(S["picked"], e + 1)
                if stage == 2:
                    pe.wait_ge(S["aT_lo"], 2 * e + k // 2 + 1)
                if k == 0:
                    if stage < 2:
                        pe.wait_ge(S["gu"], 8 * e)
                    else:
                        pe.wait_ge(S["y_out"], 2 * e)
                        if more:
                            pe.wait_ge(S["index"], 2 * e + 4)
                    for i, bank in enumerate(banks):
                        col = stage * W + i * COLS
                        pe.matmul(bank[:], pick[:], bias[:, col:col + COLS], start=True, stop=False)
                pe.wait_ge(S["lo"], N * e + j + 1)
                for kk in range(2):
                    row = 2 * k + kk
                    for x, w in ((t_hi, whi), (t_hi, wlo), (t_lo, whi)):
                        for i, bank in enumerate(banks):
                            last = pe.matmul(bank[:], x[:, row, :], w[s][:, kk, i * COLS:(i + 1) * COLS], start=False,
                                             stop=(k == self.PER_HALF - 1 and kk == 1 and x is t_lo))
                last.then_inc(S["slots_free"], 1)
                if j == 2 and more:
                    list_rows(pe, e + 1)
                if j in (5, 8):
                    f = j // 8
                    pe.wait_ge(S["act"], 4 * e + 2 * f + 2)
                    pe.wait_ge(S["x_lo"], 2 * e + 2)
                    for k2 in range(HALF_KT):
                        last = pe.transpose(self.bank[6 + f][:, k2 * P:(k2 + 1) * P],
                                            a[:, (HALF_KT * f + k2) * P:(HALF_KT * f + k2 + 1) * P], self.ident[:])
                    last.then_inc(S["act_turned"], 1)
                if j == 9 and more:
                    turn_rows(pe, e + 1)

        def gate_sigmoid(act, e, i):
            act.wait_ge(S["gu"], 8 * e + 2 * i + 1)
            act.wait_ge(S["act"], 4 * e + (2 if i >= 2 else 0))
            act.activation(sg[:, i % 2, :], gv[:, i % 2, :], ACT.Sigmoid, scale=SWIGLU_ALPHA).then_inc(S["sig"], 1)

        def rows_out(act, e, u):
            for i in range(2):
                act.wait_ge(S["slots_free"], N * e + N + self.SLOTS)
                act.wait_ge(S["scattered"], 16 * e)
                act.activation(y[:, i * COLS:(i + 1) * COLS], self.bank[4 + i][:], ACT.Copy,
                               scale=weight[u][:, 0:1]).then_inc(S["y_out"], 1)

        def expert_act(act, e, u, more):
            for j in range(self.SLOTS, N):
                hi(act, e, j)
                if j in (6, 9):
                    for i in range(2):
                        gate_sigmoid(act, e, 2 * (j // 9) + i)
                if j == 8:
                    a_part(act, e, "hi", 0)
                if j == 10:
                    a_part(act, e, "hi", 1)
            if more:
                hi(act, e + 1, 0)
                for f in range(2):
                    x_part(act, e + 1, "hi", f)
                hi(act, e + 1, 1)
                hi(act, e + 1, 2)
            rows_out(act, e, u)

        def swiglu_in(dve, e, half):
            dve.wait_ge(S["slots_free"], N * e + self.PER_HALF * (half + 1) + self.SLOTS)
            for i in (2 * half, 2 * half + 1):
                both = self.bank[i][:].rearrange("p (n a) -> p n a", a=2)
                dve.wait_ge(S["act"], 4 * e + 2 * half)
                dve.tensor_scalar(gv[:, i % 2, :], both[:, :, 0], SWIGLU_LIMIT, None, ALU.min).then_inc(S["gu"], 1)
                dve.tensor_scalar(uv[:, i % 2, :], both[:, :, 1], SWIGLU_LIMIT, -SWIGLU_LIMIT, ALU.min,
                                  ALU.max).then_inc(S["gu"], 1)

        def swiglu_out(dve, e, half):
            for i in (2 * half, 2 * half + 1):
                dve.wait_ge(S["gu"], 8 * e + 2 * i + 2)
                dve.scalar_tensor_tensor(out=uv[:, i % 2, :], in0=uv[:, i % 2, :], scalar=1.0, in1=gv[:, i % 2, :],
                                         op0=ALU.add, op1=ALU.mult).then_inc(S["p"], 1)
            for i in (2 * half, 2 * half + 1):
                dve.wait_ge(S["p"], 4 * e + i + 1)
                dve.wait_ge(S["sig"], 4 * e + i + 1)
                dve.wait_ge(S["act_turned"], 2 * e)
                dve.tensor_tensor(a[:, i * QUARTER:(i + 1) * QUARTER], uv[:, i % 2, :], sg[:, i % 2, :],
                                  ALU.mult).then_inc(S["act"], 1)

        def expert_dve(dve, e, u, more):
            for j in range(self.SLOTS, N):
                if j in (6, 10):
                    swiglu_in(dve, e, j // 8)
                lo(dve, e, j) if j != 10 else None
                if j in (6, 10):
                    swiglu_out(dve, e, j // 8)
                lo(dve, e, j) if j == 10 else None
                if j == 3 and more:
                    list_hot(dve, e + 1)
                if j == 5 and more:
                    list_index(dve, e + 1, 1 - u)
                if j in (8, 10):
                    a_part(dve, e, "lo", j // 9)
            if more:
                dve.wait_ge(S["slots_free"], N * e + 9 + self.SLOTS)
                pick_bias(dve, e + 1)
                lo(dve, e + 1, 0)
                for f in range(2):
                    x_part(dve, e + 1, "lo", f)
                lo(dve, e + 1, 1)
                lo(dve, e + 1, 2)

        def scatter(pool, e, u):
            pool.wait_ge(S["y_out"], 2 * e + 2)
            pool.wait_ge(S["scattered"], 16 * e)
            pool.sem_inc(S["passed"], 1)
            pool.indirect_dma_start(self.total, bass.IndirectOffsetOnAxis(ap=index[u][:, 0:1], axis=0), y[:], None,
                                    bounds_check=self.last_row, oob_is_err=False, compute_op=ALU.add).then_inc(S["scattered"], 16)

        def over_experts(engine, body):
            with engine.Fori(0, E // 2 - 1) as i:
                for u in range(2):
                    body(2 * i + u, u, True)
            body(E - 2, 0, True)
            body(E - 1, 1, False)

        with nc.Block() as block:
            @block.sync
            def _(sp):
                sp.dma_start(slot_no[:], t["slot_numbers"]).then_inc(S["tables_in"], 16)
                sp.dma_start(bias_row[:], t["bias_row"]).then_inc(S["tables_in"], 16)
                for n in range(2):
                    at = slice(n * E, (n + 1) * E)
                    sp.dma_start(raw[0][at].rearrange("p k n -> p (k n)"), t["expert_b_gate_up"][0]).then_inc(S["bias_in"], 16)
                    sp.dma_start(raw[1][at, 0, :], t["expert_b_down"][0]).then_inc(S["bias_in"], 16)
                for j in range(2, N):
                    sp.dma_start(raw[j][:], weights(0, j)).then_inc(loaded[j], 16)
                sp.wait_ge(S["bias_lo"], 2)
                for j in range(2):
                    sp.dma_start(raw[j][:], weights(0, j)).then_inc(loaded[j], 16)
                with sp.Fori(0, E - 1) as e:
                    for j in range(N):
                        sp.wait_ge(S["lo"], N * e + j + 1)
                        sp.dma_start(raw[j][:], weights(e + 1, j)).then_inc(loaded[j], 16)

            @block.gpsimd
            def _(pool):
                pool.memset(rows[:], 0.0).then_inc(S["cleared"], 1)
                self.last_row = pool.to_reg(SEQ - 1)
                pool.wait_ge(S["cleared"], 1)
                pool.memset(bias[2 * E:, :].bitcast(F32), 0.0).then_inc(S["bias_zeroed"], 1)
                pool.wait_ge(S["bias_zeroed"], 1)
                gather(pool, 0, 0)
                def body(e, u, more):
                    if more:
                        gather(pool, e + 1, 1 - u)
                    scatter(pool, e, u)
                over_experts(pool, body)
                pool.wait_ge(S["scattered"], 16 * E)

            @block.scalar
            def _(act):
                act.wait_ge(S["bias_in"], 64)
                act.copy(bias[0:2 * E, 0:2 * W], raw[0][0:2 * E].rearrange("p k n -> p (k n)")).then_inc(S["bias_hi"], 1)
                act.copy(bias[0:2 * E, 2 * W:], raw[1][0:2 * E, 0, :]).then_inc(S["bias_hi"], 1)
                for f in range(2):
                    x_part(act, 0, "hi", f)
                for j in (2, 0, 1) if False else (0, 1, 2):
                    hi(act, 0, j)
                over_experts(act, lambda e, u, more: expert_act(act, e, u, more))

            @block.vector
            def _(dve):
                dve.wait_ge(S["tables_in"], 32)
                list_hot(dve, 0)
                list_index(dve, 0, 0)
                pick_bias(dve, 0)
                dve.wait_ge(S["bias_hi"], 2)
                low_rows = slice(E, 2 * E)
                dve.tensor_tensor(bias[low_rows, 0:2 * W], raw[0][low_rows].rearrange("p k n -> p (k n)"),
                                  bias[low_rows, 0:2 * W].bitcast(F32), ALU.subtract).then_inc(S["bias_lo"], 1)
                dve.tensor_tensor(bias[low_rows, 2 * W:], raw[1][low_rows, 0, :],
                                  bias[low_rows, 2 * W:].bitcast(F32), ALU.subtract).then_inc(S["bias_lo"], 1)
                for f in range(2):
                    x_part(dve, 0, "lo", f)
                for j in range(self.SLOTS):
                    lo(dve, 0, j)
                over_experts(dve, lambda e, u, more: expert_dve(dve, e, u, more))

            @block.tensor
            def _(pe):
                pe.sem_inc(S["slots_free"], self.SLOTS)
                list_rows(pe, 0)
                turn_rows(pe, 0)
                pe.wait_ge(S["bias_lo"], 2)
                pe.wait_ge(S["bias_zeroed"], 1)
                over_experts(pe, lambda e, u, more: expert_pe(pe, e, more))

    def further_blocks(self, stack):
        nc, t = self.nc, self.t
        E, N, W, RING = N_EXPERTS, self.CHUNKS, self.WIDE, 4
        wgu, wd = t["expert_w_gate_up"][0], t["expert_w_down"][0]
        ring = [self.sb(stack, f"further_chunk{j}", [P, 2, W]) for j in range(RING)]
        bias = self.sb(stack, "further_biases", [E, 3 * W])
        rows = self.sb(stack, "further_rows", [P, W])
        xT = self.sb(stack, "further_rowsT", [P, KT, P])
        gv, uv, sg, a = (self.sb(stack, "further_" + n, [P, FF]) for n in ("gate", "up", "sigmoid", "act"))
        aT = self.sb(stack, "further_actT", [P, KT, P])
        y = self.sb(stack, "further_out", [P, W])
        hot = self.sb(stack, "further_one_hot", [P, NB, P])
        slot_no = self.sb(stack, "further_slot_numbers", [P, P])
        starts = self.sb(stack, "further_starts", [P, self.FURTHER])
        one = self.sb(stack, "further_bias_rows", [P, E])
        pick = self.sb(stack, "further_bias_pick", [E, P])
        place = self.sb(stack, "further_place", [P, NB])
        none = self.sb(stack, "further_empty", [P, 1])
        index = self.sb(stack, "further_index", [P, 1], I32)
        weight = self.sb(stack, "further_weight", [P, 1])
        S = {n: self.sem("further_" + n) for n in (
            "in", "cleared", "place", "hot", "listed", "none", "index", "gathered", "x_turned", "xT", "picked", "used",
            "h_full", "split", "sig", "p", "act", "a_turned", "aT", "y_full", "y_out", "scattered", "passed")}
        loaded = [self.sem(f"further_loaded{j}") for j in range(RING)]
        flat = lambda ap: ap.rearrange("p k n -> p (k n)")

        def when_any(engine, body):
            n = engine.value_load(self.n_further[0:1, 0:1], min_val=0, max_val=self.FURTHER)
            with engine.If(n > 0):
                with engine.Fori(0, self.FURTHER) as i:
                    body(i)
            with engine.Else():
                engine.nop()

        def expert_of(engine, i):
            return engine.value_load(self.block_expert[0:1, bass.ds(i, 1)], min_val=0, max_val=E - 1)

        with nc.Block() as block:
            @block.sync
            def _(sp):
                sp.dma_start(slot_no[:], t["slot_numbers"]).then_inc(S["in"], 16)
                sp.dma_start(starts[:], t["block_starts"]).then_inc(S["in"], 16)
                sp.dma_start(one[:], t["bias_row"]).then_inc(S["in"], 16)
                sp.dma_start(bias[:, 0:2 * W], t["expert_b_gate_up"][0]).then_inc(S["in"], 16)
                sp.dma_start(bias[:, 2 * W:], t["expert_b_down"][0]).then_inc(S["in"], 16)
                sp.wait_ge(S["in"], 80)

                def body(i):
                    e = expert_of(sp, i)
                    for j in range(N):
                        half, k = divmod(j, self.PER_HALF)
                        rows_ = slice(k * 2 * P, (k + 1) * 2 * P)
                        src = wd[bass.ds(e, 1), rows_, :] if half == 2 else wgu[bass.ds(e, 1), rows_, half * W:(half + 1) * W]
                        sp.wait_ge(S["used"], N * i + j + 1)
                        sp.dma_start(ring[j % RING][:], src.rearrange("a (k p) n -> p (a k) n", p=P)).then_inc(loaded[j % RING], 16)
                when_any(sp, body)

            @block.gpsimd
            def _(pool):
                pool.memset(rows[:], 0.0).then_inc(S["cleared"], 1)
                pool.wait_ge(S["cleared"], 1)
                last_row = pool.to_reg(SEQ - 1)

                def body(i):
                    pool.wait_ge(S["index"], 2 * i + 2)
                    pool.sem_inc(S["passed"], 1)
                    pool.indirect_dma_start(rows[:], None, self.normed, bass.IndirectOffsetOnAxis(ap=index[:, 0:1], axis=0),
                                            bounds_check=last_row, oob_is_err=False).then_inc(S["gathered"], 16)
                    pool.wait_ge(S["y_out"], 2 * i + 2)
                    pool.sem_inc(S["passed"], 1)
                    pool.indirect_dma_start(self.total, bass.IndirectOffsetOnAxis(ap=index[:, 0:1], axis=0), y[:], None,
                                            bounds_check=last_row, oob_is_err=False,
                                            compute_op=ALU.add).then_inc(S["scattered"], 16)
                    pool.wait_ge(S["scattered"], 16 * i + 16)
                    pool.sem_inc(S["passed"], 1)
                when_any(pool, body)

            @block.scalar
            def _(act):
                def body(i):
                    for f in range(2):
                        act.wait_ge(S["x_turned"], i + 1)
                        act.copy(flat(xT[:, HALF_KT * f:HALF_KT * (f + 1), :]), self.bank[6 + f][:]).then_inc(S["xT"], 1)
                    act.wait_ge(S["split"], 8 * i + 8)
                    act.activation(sg[:], gv[:], ACT.Sigmoid, scale=SWIGLU_ALPHA).then_inc(S["sig"], 1)
                    for f in range(2):
                        act.wait_ge(S["a_turned"], i + 1)
                        act.copy(flat(aT[:, HALF_KT * f:HALF_KT * (f + 1), :]), self.bank[6 + f][:]).then_inc(S["aT"], 1)
                    for f in range(2):
                        act.wait_ge(S["y_full"], i + 1)
                        act.activation(y[:, f * COLS:(f + 1) * COLS], self.bank[4 + f][:], ACT.Copy,
                                       scale=weight[:, 0:1]).then_inc(S["y_out"], 1)
                when_any(act, body)

            @block.vector
            def _(dve):
                dve.wait_ge(S["in"], 80)

                def body(i):
                    e = expert_of(dve, i)
                    dve.wait_ge(S["scattered"], 16 * i)
                    dve.tensor_tensor(place[:], self.place[:, :, bass.ds(e, 1)].rearrange("p b a -> p (b a)"),
                                      starts[:, bass.ds(i, 1)].to_broadcast([P, NB]), ALU.subtract).then_inc(S["place"], 1)
                    dve.wait_ge(S["place"], i + 1)
                    dve.tensor_tensor(hot[:], slot_no[:].unsqueeze(1).to_broadcast([P, NB, P]),
                                      place[:].unsqueeze(2).to_broadcast([P, NB, P]), ALU.is_equal).then_inc(S["hot"], 1)
                    dve.tensor_copy(pick[:], one[0:E, bass.ds(e, 1)].to_broadcast([E, P])).then_inc(S["picked"], 1)
                    dve.wait_ge(S["listed"], i + 1)
                    dve.tensor_scalar(none[:], self.bank[4][:, 0:1], 0.0, 8.0 * SEQ, ALU.is_equal, ALU.mult).then_inc(S["none"], 1)
                    dve.wait_ge(S["none"], i + 1)
                    dve.scalar_tensor_tensor(out=index[:], in0=none[:], scalar=-1.0, in1=self.bank[4][:, 0:1],
                                             op0=ALU.add, op1=ALU.add).then_inc(S["index"], 1)
                    dve.tensor_copy(weight[:], self.bank[4][:, 1:2]).then_inc(S["index"], 1)
                    dve.wait_ge(S["h_full"], i + 1)
                    for n in range(4):
                        both = self.bank[n][:].rearrange("p (n a) -> p n a", a=2)
                        at = slice(n * W // 4, (n + 1) * W // 4)
                        dve.tensor_scalar(gv[:, at], both[:, :, 0], SWIGLU_LIMIT, None, ALU.min).then_inc(S["split"], 1)
                        dve.tensor_scalar(uv[:, at], both[:, :, 1], SWIGLU_LIMIT, -SWIGLU_LIMIT, ALU.min,
                                          ALU.max).then_inc(S["split"], 1)
                    dve.wait_ge(S["split"], 8 * i + 8)
                    dve.scalar_tensor_tensor(out=uv[:], in0=uv[:], scalar=1.0, in1=gv[:], op0=ALU.add,
                                             op1=ALU.mult).then_inc(S["p"], 1)
                    dve.wait_ge(S["p"], i + 1)
                    dve.wait_ge(S["sig"], i + 1)
                    dve.tensor_tensor(a[:], uv[:], sg[:], ALU.mult).then_inc(S["act"], 1)
                when_any(dve, body)

            @block.tensor
            def _(pe):
                pe.wait_ge(S["in"], 80)
                pe.sem_inc(S["used"], RING)

                def turn(src, f_done):
                    for f in range(2):
                        for k in range(HALF_KT):
                            last = pe.transpose(self.bank[6 + f][:, k * P:(k + 1) * P],
                                                src[:, (HALF_KT * f + k) * P:(HALF_KT * f + k + 1) * P], self.ident[:])
                    last.then_inc(f_done, 1)

                def body(i):
                    e = expert_of(pe, i)
                    pe.wait_ge(S["hot"], i + 1)
                    pe.wait_ge(S["y_out"], 2 * i)
                    for b in range(NB):
                        last = pe.matmul(self.bank[4][:, 0:2], hot[:, b, :],
                                         self.pairs[:, b, bass.ds(e, 1), :].rearrange("p a n -> p (a n)"),
                                         start=(b == 0), stop=(b == NB - 1))
                    last.then_inc(S["listed"], 1)
                    pe.wait_ge(S["gathered"], 16 * i + 16)
                    turn(rows, S["x_turned"])
                    pe.wait_ge(S["xT"], 2 * i + 2)
                    pe.wait_ge(S["picked"], i + 1)
                    for j in range(N):
                        half, k = divmod(j, self.PER_HALF)
                        banks = [self.bank[2 * half + m] for m in range(2)]
                        if j == 2 * self.PER_HALF:
                            pe.wait_ge(S["act"], i + 1)
                            turn(a, S["a_turned"])
                            pe.wait_ge(S["aT"], 2 * i + 2)
                            pe.wait_ge(S["index"], 2 * i + 2)
                        if k == 0:
                            for m, bank in enumerate(banks):
                                col = half * W + m * COLS
                                pe.matmul(bank[:], pick[:], bias[:, col:col + COLS], start=True, stop=False)
                        pe.wait_ge(loaded[j % RING], 16 * ((N // RING) * i + j // RING + 1))
                        x = aT if half == 2 else xT
                        for kk in range(2):
                            for m, bank in enumerate(banks):
                                last = pe.matmul(bank[:], x[:, 2 * k + kk, :], ring[j % RING][:, kk, m * COLS:(m + 1) * COLS],
                                                 start=False, stop=(k == self.PER_HALF - 1 and kk == 1))
                        last.then_inc(S["used"], 1)
                        if j == 2 * self.PER_HALF - 1:
                            pe.wait_ge(S["used"], N * i + j + 1 + RING)
                            pe.sem_inc(S["h_full"], 1)
                    pe.wait_ge(S["used"], N * i + N + RING)
                    pe.sem_inc(S["y_full"], 1)
                when_any(pe, body)

    def normalise_output(self, stack):
        nc, t = self.nc, self.t
        h = self.sb(stack, "total_sb", [P, NB, D_MODEL])
        sq = self.sb(stack, "total_squares", [P, D_MODEL])
        ss = self.sb(stack, "total_sum_squares", [P, NB])
        rs = self.sb(stack, "total_rstd", [P, NB])
        g = self.sb(stack, "norm_final_g_row", [P, D_MODEL])
        half = self.sb(stack, "minus_half3", [P, 1])
        h_in = [self.sem(f"total_in{b}") for b in range(NB)]
        S = {n: self.sem("final_" + n) for n in ("g_in", "sums", "powed", "done", "stored")}
        with nc.Block() as block:
            @block.sync
            def _(sp):
                for b in range(NB):
                    sp.dma_start(h[:, b, :], self.total[b * P:(b + 1) * P, :]).then_inc(h_in[b], 16)
                sp.dma_start(g[:], t["norm_final_g"].unsqueeze(0).partition_broadcast(P).rearrange("p a n -> p (a n)")).then_inc(S["g_in"], 16)
                for b in range(NB):
                    sp.wait_ge(S["done"], b + 1)
                    sp.dma_start(t["out"][0, b * P:(b + 1) * P, :], h[:, b, :]).then_inc(S["stored"], 16)
                sp.wait_ge(S["stored"], 16 * NB)

            @block.gpsimd
            def _(pool):
                link = self.link("pool", pool)
                link(pool.memset(half[:], -0.5))
                for b in range(NB):
                    pool.wait_ge(S["sums"], b + 1)
                    pool.tensor_tensor(rs[:, b:b + 1], ss[:, b:b + 1], half[:], ALU.pow).then_inc(S["powed"], 1)

            @block.vector
            def _(dve):
                link = self.link("dve", dve)
                for b in range(NB):
                    dve.wait_ge(h_in[b], 16)
                    link(dve.scalar_tensor_tensor(out=sq[:], in0=h[:, b, :], scalar=1.0, in1=h[:, b, :], op0=ALU.mult,
                                                  op1=ALU.mult, accum_out=ss[:, b:b + 1]))
                    dve.tensor_scalar(ss[:, b:b + 1], ss[:, b:b + 1], 1.0 / D_MODEL, EPS, ALU.mult,
                                      ALU.add).then_inc(S["sums"], 1)
                dve.wait_ge(S["g_in"], 16)
                for b in range(NB):
                    dve.wait_ge(S["powed"], b + 1)
                    dve.scalar_tensor_tensor(out=h[:, b, :], in0=h[:, b, :], scalar=rs[:, b:b + 1], in1=g[:],
                                             op0=ALU.mult, op1=ALU.mult).then_inc(S["done"], 1)


_OUT = ("out", (1, SEQ, D_MODEL), F32)


def kernel(**inputs):
    import concourse.bacc as bacc
    from concourse.bass_utils import run_bass_kernel_spmd

    nc = bacc.Bacc("TRN2", target_bir_lowering=False, num_devices=1)
    arrays, tensors = {}, {}
    for name, a in list(inputs.items()) + list(CONSTANTS.items()):
        a = np.ascontiguousarray(a)
        arrays[f"in_{name}"] = a
        tensors[name] = nc.dram_tensor(f"in_{name}", a.shape, mybir.dt.from_np(a.dtype), kind="ExternalInput").ap()
    name, shape, dt = _OUT
    tensors[name] = nc.dram_tensor(name, shape, dt, kind="ExternalOutput").ap()
    Kernel(nc, tensors).build()
    results = run_bass_kernel_spmd(nc, [arrays], core_ids=[0])
    return results.results[0][name]
```

```python
import math
from contextlib import ExitStack, contextmanager

import numpy as np

import concourse.bass as bass
from concourse import mybir

F32 = mybir.dt.float32
F32R = mybir.dt.float32r
I32 = mybir.dt.int32
U32 = mybir.dt.uint32
ALU = mybir.AluOpType
ACT = mybir.ActivationFunctionType
AX = mybir.AxisListType

P = 128
SEQ, D_MODEL = 512, 1024
NB = SEQ // P
KT = D_MODEL // P
HALF_KT = KT // 2
COLS = 512

GLA_HEADS, GLA_DK, GLA_DV, GLA_CHUNK, GLA_RANK = 4, 128, 256, 64, 16
GLA_TAU = 16.0
GLA_K_WIDTH, GLA_V_WIDTH = GLA_HEADS * GLA_DK, GLA_HEADS * GLA_DV
N_CHUNKS = SEQ // GLA_CHUNK

ATT_GROUPS = ((128, 1), (512, 4), (2048, 16))
ATT_HEADS, HEAD_DIM, ROT_DIM, ROPE_THETA = 8, 64, 16, 500000.0
RES = 4
ATT_OUT = ATT_HEADS * HEAD_DIM
ATT_QKV = len(ATT_GROUPS) * ATT_OUT
ATT_KEYS = SEQ + P + P
MASKED = -1.0e30

COL_GQ = 0
COL_GK = COL_GQ + GLA_K_WIDTH
COL_GV = COL_GK + GLA_K_WIDTH
COL_GR = COL_GV + GLA_V_WIDTH
COL_GLR = COL_GR + GLA_V_WIDTH
COL_AQ = COL_GLR + GLA_RANK
COL_AV = COL_AQ + 2 * ATT_QKV
COL_GATE = COL_AV + ATT_QKV

N_EXPERTS, TOP_K, FF = 32, 4, D_MODEL
SWIGLU_LIMIT, SWIGLU_ALPHA = 7.0, 1.702
EPS = 1e-5


def shape_constants():
    c = {}
    c["identity"] = np.eye(P, dtype=np.float32)
    half = ROT_DIM // 2
    inv = (np.float32(ROPE_THETA) ** (-np.arange(half, dtype=np.float32) * np.float32(2.0 / ROT_DIM))).astype(np.float32)
    ang = (np.arange(SEQ, dtype=np.float32)[:, None] * inv[None, :]).astype(np.float32)
    cos, sin = np.cos(ang).astype(np.float32), np.sin(ang).astype(np.float32)
    c["rope"] = np.concatenate([cos, cos, -sin, sin], axis=1).astype(np.float32)
    t, r = np.arange(P), np.arange(RES)
    q = (RES * t[None, :] + r[:, None])[:, :, None]
    k0 = np.arange(SEQ)[None, None, :]
    window = ATT_GROUPS[0][0]
    ok0 = (q - k0 >= 0) & (q - k0 <= window)
    lag = np.broadcast_to(t[:, None] - t[None, :], (RES, P, P))
    ok1 = lag >= 0
    ok2 = (lag >= 0) & (lag % (ATT_GROUPS[2][1] // RES) == 0)
    ok = np.concatenate([ok0, ok1, ok2], axis=2)
    c["att_mask"] = np.where(ok, 0.0, MASKED).astype(np.float32)
    i = np.arange(P)
    same = (i[:, None] // GLA_CHUNK) == (i[None, :] // GLA_CHUNK)
    c["gla_mask"] = np.where((i[:, None] <= i[None, :]) & same, np.finfo(np.float32).max, 0).astype(np.float32)
    keep = np.ones((P, GLA_HEADS * SEQ), np.float32)
    keep[:, ::GLA_CHUNK] = 0.0
    c["scan_keep"] = keep
    c["before"] = (i[:, None] < i[None, :]).astype(np.float32)
    c["slot_numbers"] = np.broadcast_to(np.arange(P, dtype=np.float32), (P, P)).copy()
    c["expert_numbers"] = np.broadcast_to(np.arange(N_EXPERTS, dtype=np.float32), (P, N_EXPERTS)).copy()
    c["token_numbers"] = (np.arange(NB)[None, :] * P + i[:, None]).astype(np.float32)
    c["block_starts"] = np.broadcast_to(np.arange(SEQ * TOP_K // P, dtype=np.float32) * P, (P, SEQ * TOP_K // P)).copy()
    e = np.zeros((P, N_EXPERTS), np.float32)
    for x in range(N_EXPERTS):
        e[x, x] = e[N_EXPERTS + x, x] = 1.0
    c["bias_row"] = e
    return c


CONSTANTS = shape_constants()


class Chain:

    def __init__(self, engine, semaphore):
        self.engine, self.semaphore, self.at, self.n = engine, semaphore, 0, 0

    def __call__(self, instruction):
        instruction.then_inc(self.semaphore, 1)
        self.n += 1
        self.engine.wait_ge(self.semaphore, self.at + self.n)

    def enter(self, i, per_iteration):
        self.before = self.at + self.n
        self.at, self.n = self.before + i * per_iteration, 0

    def leave(self, iterations, per_iteration):
        assert self.n == per_iteration, (self.n, per_iteration)
        self.at, self.n = self.before + iterations * per_iteration, 0


class Kernel:
    def __init__(self, nc, t):
        self.nc, self.t, self.groups = nc, t, 0

    def sem(self, name):
        handle = self.nc.alloc_semaphore(name=name)
        if self.stage_sems is not None:
            self.stage_sems.append(handle)
        return handle

    @contextmanager
    def stage(self):
        self.stage_sems = []
        with ExitStack() as stack:
            yield stack
        self.nc.clear_and_free_semaphores(self.stage_sems)
        self.nc.all_engine_barrier()
        self.stage_sems = None

    def sb(self, stack, name, shape, dt=F32):
        return stack.enter_context(self.nc.sbuf_tensor(name, shape, dt))

    def build(self):
        nc = self.nc
        with ExitStack() as top:
            self.stage_sems = None
            self.psum = top.enter_context(nc.psum_tensor("psum", [P, 8, COLS], F32))
            self.bank = [self.psum[:, i, :] for i in range(8)]
            self.chain_sem = {e: self.sem(f"chain_{e}") for e in ("pe", "act", "dve", "pool", "sp")}
            self.chain = {}
            self.loaded = [self.sem(f"chunk_loaded{c}") for c in range(2)]
            self.hi_done = [self.sem(f"chunk_hi_done{c}") for c in range(2)]
            self.lo_done = [self.sem(f"chunk_lo_done{c}") for c in range(2)]
            self.chunk_used = self.sem("chunk0_used")
            self.bank_full = [self.sem(f"bank_full{b}") for b in range(NB)]
            self.bank_free = [self.sem(f"bank_free{b}") for b in range(NB)]
            self.ident = self.sb(top, "identity_sb", [P, P])
            self.rank = self.sb(top, "rank_in_expert", [P, NB, N_EXPERTS])
            self.pairs = self.sb(top, "token_and_weight", [P, NB, N_EXPERTS, 2])
            self.place = self.sb(top, "place_in_further", [P, NB, N_EXPERTS])
            self.block_expert = self.sb(top, "further_block_expert", [P, self.FURTHER], I32)
            self.n_further = self.sb(top, "further_blocks", [P, 1], I32)
            self.normed = nc.dram_tensor("normed_rows", [SEQ, D_MODEL], F32).ap()
            self.total = nc.dram_tensor("residual_rows", [SEQ, D_MODEL], F32).ap()
            self.h = self.sb(top, "h_sb", [P, NB, D_MODEL])
            with ExitStack() as mixer:
                self.mixer(mixer)
            with ExitStack() as moe:
                self.first_expert = [self.sem(f"expert_chunk_loaded{j}") for j in range(self.CHUNKS)]
                self.expert_ring = [self.sb(moe, f"expert_chunk{j}", [P, 2, self.WIDE]) for j in range(self.CHUNKS)]
                self.bias = self.sb(moe, "bias_hi_lo", [P, 3 * self.WIDE], F32R)
                with self.stage() as s:
                    self.route(s)
                with self.stage() as s:
                    self.experts(s)
            with self.stage() as s:
                self.further_blocks(s)
            with self.stage() as s:
                self.normalise_output(s)

    def link(self, name, engine):
        c = self.chain.setdefault(name, Chain(engine, self.chain_sem[name]))
        c.engine = engine
        return c

    def mixer(self, stack):
        self.x_hi = self.sb(stack, "xT_hi", [P, KT, SEQ], F32R)
        self.x_lo = self.sb(stack, "xT_lo", [P, KT, SEQ], F32R)
        with self.stage() as s:
            self.normalise_input(s)
        self.yg = self.sb(stack, "y_glaT", [P, KT, SEQ])
        with ExitStack() as s:
            self.gla(s)
        self.ya = self.h[:, 0:NB // 2, :].rearrange("p b n -> p (b n)").rearrange("p (k n) -> p k n", n=SEQ)
        with ExitStack() as s:
            self.attention(s)
        with ExitStack() as s:
            self.merge(s)

    def normalise_input(self, stack):
        nc, t = self.nc, self.t
        x = self.sb(stack, "x_sb", [P, NB, D_MODEL])
        sq = self.sb(stack, "x_squares", [P, D_MODEL])
        ss = self.sb(stack, "x_sum_squares", [P, NB])
        rs = self.sb(stack, "x_rstd", [P, NB])
        g = self.sb(stack, "norm_mix_g_col", [P, KT])
        xg = self.sb(stack, "xg", [P, 2, HALF_KT, P])
        minus_half = self.sb(stack, "minus_half0", [P, 1])
        x_in = [self.sem(f"x_in{b}") for b in range(NB)]
        consts_in, sums, powed, scaled = self.sem("consts0_in"), self.sem("x_sums"), self.sem("x_powed"), self.sem("x_scaled")
        turned, xg_done, xh_done, xl_done = self.sem("x_turned"), self.sem("xg_done"), self.sem("xh_done"), self.sem("xl_done")
        with nc.Block() as block:
            @block.sync
            def _(sp):
                for b in range(NB):
                    sp.dma_start(x[:, b, :], t["x"][0, b * P:(b + 1) * P, :]).then_inc(x_in[b], 16)
                sp.dma_start(self.ident[:], t["identity"]).then_inc(consts_in, 16)
                sp.dma_start(g[:], t["norm_mix_g"][0].rearrange("(k p) -> p k", p=P),
                             allow_slow_non_contiguous=True).then_inc(consts_in, 16)

            @block.gpsimd
            def _(pool):
                link = self.link("pool", pool)
                link(pool.memset(minus_half[:], -0.5))
                pool.wait_ge(sums, 1)
                pool.tensor_tensor(rs[:], ss[:], minus_half[:, 0:1].to_broadcast([P, NB]), ALU.pow).then_inc(powed, 1)

            @block.vector
            def _(dve):
                link = self.link("dve", dve)
                for b in range(NB):
                    dve.wait_ge(x_in[b], 16)
                    link(dve.scalar_tensor_tensor(out=sq[:], in0=x[:, b, :], scalar=1.0, in1=x[:, b, :],
                                                  op0=ALU.mult, op1=ALU.mult, accum_out=ss[:, b:b + 1]))
                dve.tensor_scalar(ss[:], ss[:], 1.0 / D_MODEL, EPS, ALU.mult, ALU.add).then_inc(sums, 1)
                dve.wait_ge(powed, 1)
                for b in range(NB):
                    dve.tensor_scalar(x[:, b, :], x[:, b, :], rs[:, b:b + 1], None, ALU.mult).then_inc(scaled, 1)
                dve.wait_ge(consts_in, 32)
                for i in range(2 * NB):
                    b, h = divmod(i, 2)
                    dve.wait_ge(turned, i + 1)
                    if i >= 2:
                        dve.wait_ge(xh_done, i - 1)
                        dve.wait_ge(xl_done, i - 1)
                    dve.tensor_tensor(xg[:, i % 2], self.bank[i % 2].rearrange("p (k n) -> p k n", n=P),
                                      g[:, HALF_KT * h:HALF_KT * (h + 1)].unsqueeze(2).to_broadcast([P, HALF_KT, P]),
                                      ALU.mult).then_inc(xg_done, 1)
                    dve.wait_ge(xg_done, i + 1)
                    dve.wait_ge(xh_done, i + 1)
                    dst = (slice(None), slice(HALF_KT * h, HALF_KT * (h + 1)), slice(b * P, (b + 1) * P))
                    dve.tensor_tensor(self.x_lo[dst], xg[:, i % 2], self.x_hi[dst].bitcast(F32),
                                      ALU.subtract).then_inc(xl_done, 1)

            @block.scalar
            def _(act):
                for i in range(2 * NB):
                    b, h = divmod(i, 2)
                    act.wait_ge(xg_done, i + 1)
                    act.copy(self.x_hi[:, HALF_KT * h:HALF_KT * (h + 1), b * P:(b + 1) * P],
                             xg[:, i % 2]).then_inc(xh_done, 1)

            @block.tensor
            def _(pe):
                pe.wait_ge(consts_in, 32)
                for i in range(2 * NB):
                    b, h = divmod(i, 2)
                    pe.wait_ge(scaled, b + 1)
                    if i >= 2:
                        pe.wait_ge(xg_done, i - 1)
                    for k in range(HALF_KT):
                        last = pe.transpose(self.bank[i % 2][:, k * P:(k + 1) * P],
                                            x[:, b, (HALF_KT * h + k) * P:(HALF_KT * h + k + 1) * P], self.ident[:])
                    last.then_inc(turned, 1)

    def ring(self, stack, stage):
        self.raw = [self.sb(stack, f"{stage}_chunk{c}", [P, HALF_KT, COLS]) for c in range(2)]
        self.whi = [self.sb(stack, f"{stage}_chunk_hi{c}", [P, HALF_KT, COLS], F32R) for c in range(2)]
        self.wlo = [self.sb(stack, f"{stage}_chunk_lo{c}", [P, HALF_KT, COLS], F32R) for c in range(2)]

    def load_group(self, sp, g, source):
        for c in range(2):
            sp.wait_ge(self.lo_done[c], g)
            sp.dma_start(self.raw[c][:], source(c)).then_inc(self.loaded[c], 16)

    def split_hi(self, act, g, c):
        act.wait_ge(self.loaded[c], g * 16 + 16)
        act.wait_ge(self.bank_full[NB - 1] if c else self.chunk_used, g)
        act.copy(self.whi[c][:], self.raw[c][:]).then_inc(self.hi_done[c], 1)

    def split_lo(self, dve, g, c):
        dve.wait_ge(self.hi_done[c], g + 1)
        dve.tensor_tensor(self.wlo[c][:], self.raw[c][:], self.whi[c][:].bitcast(F32),
                          ALU.subtract).then_inc(self.lo_done[c], 1)

    def multiply_group(self, pe, g, tokens, weights_stay=False, lhs=None, between=None, ready=None):
        x_hi, x_lo = lhs or (self.x_hi, self.x_lo)
        for c in range(2):
            pe.wait_ge(self.lo_done[c], g + 1)
            if ready:
                ready(c)
            for b in range(NB):
                if c == 0:
                    pe.wait_ge(self.bank_free[b], g)
                for kk in range(HALF_KT):
                    k = HALF_KT * c + kk
                    hi, lo = self.whi[c], self.wlo[c]
                    if weights_stay:
                        col = slice(b * P, (b + 1) * P)
                        passes = ((hi[:, kk, col], x_hi[:, k, :]), (hi[:, kk, col], x_lo[:, k, :]),
                                  (lo[:, kk, col], x_hi[:, k, :]))
                    else:
                        tok = tokens(b)
                        passes = ((x_hi[:, k, tok], hi[:, kk, :]), (x_hi[:, k, tok], lo[:, kk, :]),
                                  (x_lo[:, k, tok], hi[:, kk, :]))
                    for n, (stationary, moving) in enumerate(passes):
                        last = pe.matmul(self.bank[b], stationary, moving, start=(k == 0 and n == 0),
                                         stop=(k == KT - 1 and n == 2))
                if c == 1:
                    last.then_inc(self.bank_full[b], 1)
            if c == 0:
                last.then_inc(self.chunk_used, 1)
                if between:
                    between()

    def w_in_chunk(self, col):
        def source(c):
            return self.t["w_in"][0, c * HALF_KT * P:(c + 1) * HALF_KT * P, bass.ds(col, COLS)].rearrange(
                "(k p) n -> p k n", p=P)
        return source

    @staticmethod
    def block_of(b):
        return slice(b * P, (b + 1) * P)

    @staticmethod
    def residue(b):
        return slice(b, SEQ, RES)

    def run_groups(self, kind, engine, base, n, source=None, tokens=None, weights_stay=False, lhs=None,
                   evacuate=None, first_split=False, next_split=False):
        def step(i, last):
            g = base + i
            if kind == "load":
                self.load_group(engine, g, lambda c: source(i)(c))
            elif kind == "multiply":
                self.multiply_group(engine, g, tokens, weights_stay, lhs)
            else:
                split = self.split_hi if kind == "hi" else self.split_lo
                more = next_split or not last
                if more:
                    split(engine, g + 1, 0)
                if evacuate:
                    for b in range(NB):
                        engine.wait_ge(self.bank_full[b], g + 1)
                        evacuate(i, b).then_inc(self.bank_free[b], 1)
                if more:
                    split(engine, g + 1, 1)

        if first_split and kind in ("hi", "lo"):
            for c in range(2):
                (self.split_hi if kind == "hi" else self.split_lo)(engine, base, c)
        if kind in ("load", "multiply"):
            with engine.Fori(0, n) as i:
                step(i, False)
        else:
            if n > 1:
                with engine.Fori(0, n - 1) as i:
                    step(i, False)
            step(n - 1, True)

    def gla(self, stack):
        nc, t = self.nc, self.t
        H, L = GLA_HEADS, SEQ
        qk = self.sb(stack, "gla_qkT", [P, 2, H, L])
        v = self.sb(stack, "gla_v", [P, NB, GLA_V_WIDTH])
        sg = self.sb(stack, "gla_silu_r", [P, NB, GLA_V_WIDTH])
        b_sum = self.sb(stack, "decay_sums", [P, H, L])
        with self.stage() as s:
            self.gla_project(s, qk, v, sg, b_sum)
        with self.stage() as s:
            self.gla_heads(s, qk, v, sg, b_sum)

    def gla_project(self, stack, qk, v, sg, b_sum):
        nc, t = self.nc, self.t
        H, L = GLA_HEADS, SEQ
        base = self.groups
        self.ring(stack, "gla")
        z = self.sb(stack, "decay_z", [P, H, L])
        soft = sg[:, 0:NB // 2, :].rearrange("p b n -> p (b n)").rearrange("p (h n) -> p h n", n=L)
        keep = self.sb(stack, "scan_keep_sb", [P, H * L])
        w_lr = self.sb(stack, "w_lr", [P, KT, P])
        w_lr_hi = self.sb(stack, "w_lr_hi", [P, KT, P], F32R)
        w_lr_lo = self.sb(stack, "w_lr_lo", [P, KT, P], F32R)
        lrT = self.sb(stack, "lrT", [GLA_RANK, L])
        up = self.sb(stack, "gate_up_sb", [GLA_RANK, GLA_K_WIDTH])
        bias = self.sb(stack, "gate_bias_col", [P, H])
        g_row = self.sb(stack, "gla_norm_g_row", [P, GLA_DV])
        small_in, lr_in = self.sem("gla_small_in"), self.sem("w_lr_in")
        lr_hi, lr_lo, lr_full, lr_out = (self.sem(n) for n in ("lr_hi_done", "lr_lo_done", "lr_full", "lr_out"))
        z_full, z_out, soft_done, silu_done = (self.sem(n) for n in ("z_full", "z_out", "soft_done", "silu_done"))
        GROUPS_QK, GROUPS_V, GROUPS_R = 2 * GLA_K_WIDTH // COLS, GLA_V_WIDTH // COLS, GLA_V_WIDTH // COLS
        base_v, base_r = base + GROUPS_QK, base + GROUPS_QK + GROUPS_V
        self.groups = base_r + GROUPS_R

        with nc.Block() as block:
            @block.sync
            def _(sp):
                self.load_group(sp, base, self.w_in_chunk(COL_GQ))
                sp.dma_start(w_lr[:], t["w_in"][0, :, COL_GLR:COL_GLR + P].rearrange("(k p) n -> p k n", p=P)
                             ).then_inc(lr_in, 16)
                sp.dma_start(up[:], t["gla_gate_up"][0]).then_inc(small_in, 16)
                sp.dma_start(bias[:], t["gla_gate_bias"][0].rearrange("(h p) -> p h", p=P),
                             allow_slow_non_contiguous=True).then_inc(small_in, 16)
                sp.dma_start(keep[:], t["scan_keep"]).then_inc(small_in, 16)
                sp.dma_start(g_row[:], t["gla_norm_g"][0:1, :].partition_broadcast(P).rearrange("p a n -> p (a n)")).then_inc(small_in, 16)
                with sp.Fori(1, 2 * 3) as i:
                    self.load_group(sp, base + i, lambda c: self.w_in_chunk(COL_GQ + COLS * i)(c))

            @block.tensor
            def _(pe):
                pe.wait_ge(lr_lo, 1)
                for k in range(KT):
                    for n, (w, x) in enumerate(((w_lr_hi, self.x_hi), (w_lr_hi, self.x_lo), (w_lr_lo, self.x_hi))):
                        last = pe.matmul(self.bank[4], w[:, k, :], x[:, k, :], start=(k == 0 and n == 0),
                                         stop=(k == KT - 1 and n == 2))
                last.then_inc(lr_full, 1)
                pe.wait_ge(small_in, 64)
                pe.wait_ge(lr_out, 1)
                for h in range(H):
                    pe.matmul(self.bank[4 + h], up[:, h * P:(h + 1) * P], lrT[:],
                              start=True, stop=True).then_inc(z_full, 1)
                self.run_groups("multiply", pe, base, GROUPS_QK, weights_stay=True)
                self.run_groups("multiply", pe, base_v, GROUPS_V, tokens=self.block_of)
                self.run_groups("multiply", pe, base_r, GROUPS_R, tokens=self.block_of)

            @block.scalar
            def _(act):
                link = self.link("act", act)
                for c in range(2):
                    self.split_hi(act, base, c)
                act.wait_ge(lr_in, 16)
                act.copy(w_lr_hi[:], w_lr[:]).then_inc(lr_hi, 1)
                act.wait_ge(lr_full, 1)
                act.copy(lrT[:], self.bank[4][0:GLA_RANK, :]).then_inc(lr_out, 1)
                act.wait_ge(z_out, H)
                link(act.activation(soft, z[:], ACT.Abs))
                link(act.activation(soft, soft, ACT.Exp, scale=-1.0))
                act.activation(soft, soft, ACT.Ln, bias=1.0).then_inc(soft_done, 1)
                self.run_groups("hi", act, base, GROUPS_QK, next_split=True,
                                evacuate=lambda i, b: act.copy(qk[:, i, b, :] if isinstance(i, int) else
                                                               qk[:, bass.ds(i, 1), b, :].rearrange("p a n -> p (a n)"),
                                                               self.bank[b]))
                self.run_groups("hi", act, base_v, GROUPS_V, next_split=True,
                                evacuate=lambda i, b: act.copy(v[:, b, bass.ds(i * COLS, COLS)], self.bank[b]))
                self.run_groups("hi", act, base_r, GROUPS_R,
                                evacuate=lambda i, b: act.activation(sg[:, b, bass.ds(i * COLS, COLS)],
                                                                     self.bank[b], ACT.Silu))

            @block.vector
            def _(dve):
                link = self.link("dve", dve)
                for c in range(2):
                    self.split_lo(dve, base, c)
                dve.wait_ge(lr_hi, 1)
                dve.tensor_tensor(w_lr_lo[:], w_lr[:], w_lr_hi[:].bitcast(F32), ALU.subtract).then_inc(lr_lo, 1)
                dve.wait_ge(small_in, 64)
                for h in range(H):
                    dve.wait_ge(z_full, h + 1)
                    dve.tensor_scalar(z[:, h, :], self.bank[4 + h], bias[:, h:h + 1], None,
                                      ALU.add).then_inc(z_out, 1)
                self.split_lo(dve, base + 1, 0)
                self.split_lo(dve, base + 1, 1)
                dve.wait_ge(soft_done, 1)
                link(dve.scalar_tensor_tensor(out=z[:], in0=z[:], scalar=0.0, in1=soft, op0=ALU.min,
                                              op1=ALU.subtract))
                link(dve.tensor_tensor_scan(b_sum[:].rearrange("p h n -> p (h n)"), keep[:],
                                            z[:].rearrange("p h n -> p (h n)"), 0.0, ALU.mult, ALU.add))
                with dve.Fori(2, 2 * 3) as i:
                    for c in range(2):
                        self.split_lo(dve, base + i, c)
                dve.wait_ge(self.bank_free[NB - 1], base_r + GROUPS_R)
                for b in range(NB):
                    dve.wait_ge(self.bank_free[b], base_r + GROUPS_R)
                    r = sg[:, b, :].rearrange("p (h n) -> p h n", h=H)
                    link(dve.tensor_tensor(r, r, g_row[:].unsqueeze(1).to_broadcast([P, H, GLA_DV]), ALU.mult))

    def gla_heads(self, stack, qk, v, sg, b_sum):
        nc, t = self.nc, self.t
        H, L, C = GLA_HEADS, SEQ, GLA_CHUNK
        grow = self.sb(stack, "exp_b", [P, L])
        fade = self.sb(stack, "exp_minus_b", [P, L])
        rest = self.sb(stack, "exp_last_minus_b", [P, L])
        qe = self.sb(stack, "q_decayed", [P, L])
        ke = self.sb(stack, "k_decayed", [P, L])
        kdT = self.sb(stack, "k_to_chunk_endT", [P, L])
        kd = self.sb(stack, "k_to_chunk_end", [P, NB, P])
        at = self.sb(stack, "products_masked", [P, NB, P])
        mask = self.sb(stack, "gla_mask_sb", [P, P])
        anti = self.sb(stack, "gla_mask_negated", [P, P])
        state = self.sb(stack, "gla_state", [P, N_CHUNKS, GLA_DV])
        sq = self.sb(stack, "gla_squares", [P, GLA_DV])
        ss = self.sb(stack, "gla_sum_squares", [P, NB])
        rs = self.sb(stack, "gla_rstd", [P, NB])
        y = self.sb(stack, "gla_y", [P, NB, GLA_DV])
        vh = self.sb(stack, "gla_v_head", [P, NB, GLA_DV])
        minus_half = self.sb(stack, "minus_half1", [P, 1])
        S = {n: self.sem("gla_" + n) for n in (
            "mask_in", "state_zeroed", "clamped", "half_set", "exps", "to_end", "decayed", "kd_turned", "kd_out", "products",
            "masked", "updates", "state_done", "o_full", "squared", "mean_done", "powed", "y_done", "y_turned",
            "y_out", "v_staged")}
        flat = lambda ap: ap.rearrange("p a n -> p (a n)")
        u_bank = lambda c: self.bank[c % 4][:, (c // 4) * GLA_DV:(c // 4 + 1) * GLA_DV]
        o_bank = lambda n: self.bank[6 + n // 2][:, (n % 2) * GLA_DV:(n % 2 + 1) * GLA_DV]
        chunk = lambda c: slice(c * C, (c + 1) * C)
        UPDATES = N_CHUNKS - 1

        with nc.Block() as block:
            @block.sync
            def _(sp):
                sp.dma_start(mask[:], t["gla_mask"]).then_inc(S["mask_in"], 16)

            @block.gpsimd
            def _(pool):
                pool.memset(state[:, 0, :], 0.0).then_inc(S["state_zeroed"], 1)
                pool.memset(minus_half[:], -0.5).then_inc(S["half_set"], 1)
                pool.wait_ge(S["half_set"], 1)
                for h in range(H):
                    if h:
                        pool.wait_ge(S["o_full"], 2 * h)
                    pool.tensor_copy(vh[:], v[:, :, h * GLA_DV:(h + 1) * GLA_DV]).then_inc(S["v_staged"], 1)
                    pool.wait_ge(S["mean_done"], h + 1)
                    if h:
                        pool.wait_ge(S["y_done"], NB * h)
                    pool.tensor_tensor(rs[:], ss[:], minus_half[:, 0:1].to_broadcast([P, NB]),
                                       ALU.pow).then_inc(S["powed"], 1)

            @block.scalar
            def _(act):
                with act.Fori(0, H) as h:
                    b_h = flat(b_sum[:, bass.ds(h, 1), :])
                    act.wait_ge(S["decayed"], h * 3)
                    act.wait_ge(S["state_done"], h * UPDATES)
                    act.activation(grow[:], b_h, ACT.Exp, scale=1.0 / GLA_TAU).then_inc(S["exps"], 1)
                    act.activation(fade[:], b_h, ACT.Exp, scale=-1.0 / GLA_TAU).then_inc(S["exps"], 1)
                    act.wait_ge(S["to_end"], h + 1)
                    act.activation(rest[:], rest[:], ACT.Exp, scale=1.0 / GLA_TAU).then_inc(S["exps"], 1)
                    act.wait_ge(S["kd_turned"], h + 1)
                    act.wait_ge(S["updates"], h)
                    act.copy(flat(kd[:]), self.bank[4]).then_inc(S["kd_out"], 1)
                    for n in range(NB):
                        act.wait_ge(S["o_full"], h * 2 + n // 2 + 1)
                        act.wait_ge(S["squared"], h * NB + n)
                        act.wait_ge(S["powed"], h)
                        act.activation(sq[:], o_bank(n), ACT.Square, accum_out=ss[:, n:n + 1]).then_inc(S["squared"], 1)
                    for d in range(2):
                        act.wait_ge(S["y_turned"], h * 2 + d + 1)
                        act.copy(flat(self.yg[:, bass.ds(2 * h + d, 1), :]), self.bank[4 + d]).then_inc(S["y_out"], 1)

            @block.vector
            def _(dve):
                link = self.link("dve", dve)
                dve.wait_ge(S["mask_in"], 16)
                link(dve.tensor_scalar(anti[:], mask[:], -1.0, None, ALU.mult))
                with dve.Fori(0, H) as h:
                    by_chunk = lambda ap: ap.rearrange("p (c n) -> p c n", n=C)
                    b_c = by_chunk(flat(b_sum[:, bass.ds(h, 1), :]))
                    dve.wait_ge(S["decayed"], 3 * h)
                    dve.tensor_tensor(by_chunk(rest[:]), b_c[:, :, C - 1:C].to_broadcast([P, N_CHUNKS, C]), b_c,
                                      ALU.subtract).then_inc(S["to_end"], 1)
                    q_h = qk[:, 0, bass.ds(h, 1), :].rearrange("p a n -> p (a n)")
                    k_h = qk[:, 1, bass.ds(h, 1), :].rearrange("p a n -> p (a n)")
                    dve.wait_ge(S["exps"], 3 * h + 1)
                    dve.wait_ge(S["o_full"], 2 * h)
                    dve.scalar_tensor_tensor(out=qe[:], in0=q_h, scalar=float(GLA_DK) ** -0.5, in1=grow[:],
                                             op0=ALU.mult, op1=ALU.mult).then_inc(S["decayed"], 1)
                    dve.wait_ge(S["exps"], 3 * h + 2)
                    dve.tensor_tensor(ke[:], k_h, fade[:], ALU.mult).then_inc(S["decayed"], 1)
                    dve.wait_ge(S["exps"], 3 * h + 3)
                    dve.tensor_tensor(kdT[:], k_h, rest[:], ALU.mult).then_inc(S["decayed"], 1)
                    dve.wait_ge(S["products"], h + 1)
                    over = lambda m: m[:].unsqueeze(1).to_broadcast([P, NB, P])
                    dve.tensor_tensor(at[:], self.bank[5].rearrange("p (a n) -> p a n", n=P), over(mask),
                                      ALU.min).then_inc(S["clamped"], 1)
                    dve.wait_ge(S["clamped"], h + 1)
                    dve.tensor_tensor(at[:], at[:], over(anti), ALU.max).then_inc(S["masked"], 1)
                    for c in range(UPDATES):
                        dve.wait_ge(S["updates"], h + 1)
                        done = h * UPDATES + c
                        dve.wait_ge(S["state_done"], done)
                        if c == 0:
                            dve.tensor_copy(state[:, 1, :], u_bank(0)).then_inc(S["state_done"], 1)
                        else:
                            dve.scalar_tensor_tensor(out=state[:, c + 1, :], in0=state[:, c, :],
                                                     scalar=grow[:, c * C + C - 1:c * C + C], in1=u_bank(c),
                                                     op0=ALU.mult, op1=ALU.add).then_inc(S["state_done"], 1)
                    dve.wait_ge(S["squared"], NB * h + NB)
                    dve.tensor_scalar(ss[:], ss[:], 1.0 / GLA_DV, EPS, ALU.mult, ALU.add).then_inc(S["mean_done"], 1)
                    dve.wait_ge(S["powed"], h + 1)
                    for n in range(NB):
                        dve.wait_ge(S["y_turned"], 2 * h)
                        dve.scalar_tensor_tensor(out=y[:, n, :], in0=o_bank(n), scalar=rs[:, n:n + 1],
                                                 in1=sg[:, n, bass.ds(h * GLA_DV, GLA_DV)],
                                                 op0=ALU.mult, op1=ALU.mult).then_inc(S["y_done"], 1)

            @block.tensor
            def _(pe):
                pe.wait_ge(S["state_zeroed"], 1)
                with pe.Fori(0, H) as h:
                    pe.wait_ge(S["y_out"], 2 * h)
                    pe.wait_ge(S["decayed"], 3 * h + 3)
                    for n in range(NB):
                        last = pe.transpose(self.bank[4][:, n * P:(n + 1) * P], kdT[:, n * P:(n + 1) * P], self.ident[:])
                    last.then_inc(S["kd_turned"], 1)
                    for n in range(NB):
                        blk = self.block_of(n)
                        last = pe.matmul(self.bank[5][:, blk], ke[:, blk], qe[:, blk], start=True, stop=True)
                    last.then_inc(S["products"], 1)
                    pe.wait_ge(S["kd_out"], h + 1)
                    pe.wait_ge(S["v_staged"], h + 1)
                    for c in range(UPDATES):
                        half = slice((c % 2) * C, (c % 2 + 1) * C)
                        last = pe.matmul(u_bank(c), kd[half, c // 2, :], vh[half, c // 2, :], start=True, stop=True)
                    last.then_inc(S["updates"], 1)
                    pe.wait_ge(S["masked"], h + 1)
                    for n in range(NB):
                        pe.wait_ge(S["y_done"], NB * h)
                        pe.matmul(o_bank(n), at[:, n, :], vh[:, n, :], start=True, stop=False)
                        for c in (2 * n, 2 * n + 1):
                            if c:
                                pe.wait_ge(S["state_done"], h * UPDATES + c)
                            last = pe.matmul(o_bank(n)[(c % 2) * C:(c % 2 + 1) * C, :], qe[:, chunk(c)],
                                             state[:, c, :], start=False, stop=True)
                        if n % 2:
                            last.then_inc(S["o_full"], 1)
                    pe.wait_ge(S["y_done"], NB * h + NB)
                    for d in range(2):
                        for n in range(NB):
                            last = pe.transpose(self.bank[4 + d][:, n * P:(n + 1) * P],
                                                y[:, n, d * P:(d + 1) * P], self.ident[:])
                        last.then_inc(S["y_turned"], 1)

    def attention(self, stack):
        G = len(ATT_GROUPS)
        q = self.sb(stack, "att_qT", [P, G * HALF_KT, SEQ])
        k = self.sb(stack, "att_kT", [P, G * HALF_KT, SEQ])
        v = self.sb(stack, "att_v", [P, G, NB, ATT_OUT])
        with self.stage() as s:
            self.att_project(s, q, k, v)
        with self.stage() as s:
            self.att_heads(s, q, k, v)

    def att_project(self, stack, q, k, v):
        nc, t = self.nc, self.t
        G, HALF = len(ATT_GROUPS), ROT_DIM // 2
        base, base_v = self.groups, self.groups + 2 * G
        self.groups = base_v + G
        self.ring(stack, "att")
        row = self.sb(stack, "qk_rows", [P, NB, COLS])
        turn = self.sb(stack, "rope_products", [P, 2, ATT_HEADS, ROT_DIM])
        rope = self.sb(stack, "rope_sb", [P, NB, 2 * ROT_DIM])
        rope_in, rotated, turned, stored = (self.sem("att_" + n) for n in ("rope_in", "rotated", "turned", "stored"))
        prod, summed = self.sem("att_rope_products"), self.sem("att_rope_read")

        with nc.Block() as block:
            @block.sync
            def _(sp):
                sp.dma_start(rope[:], t["rope"].rearrange("(b p) n -> p b n", p=P)).then_inc(rope_in, 16)
                with sp.Fori(0, 3 * G) as i:
                    self.load_group(sp, base + i, lambda c: self.w_in_chunk(COL_AQ + COLS * i)(c))

            @block.tensor
            def _(pe):
                def turn_rows(i):
                    for b in range(NB):
                        pe.wait_ge(rotated, NB * i + b + 1)
                        pe.wait_ge(stored, NB * i)
                        for d in range(HALF_KT):
                            last = pe.transpose(self.bank[4 + b][:, d * P:(d + 1) * P],
                                                row[:, b, d * P:(d + 1) * P], self.ident[:])
                        last.then_inc(turned, 1)

                def qk_group(i, before=None):
                    self.multiply_group(pe, base + i, self.block_of, between=before)

                qk_group(0)
                with pe.Fori(1, 2 * G) as i:
                    qk_group(i, lambda: turn_rows(i - 1))
                self.multiply_group(pe, base_v, self.block_of, between=lambda: turn_rows(2 * G - 1))
                self.run_groups("multiply", pe, base_v + 1, G - 1, tokens=self.residue)

            @block.scalar
            def _(act):
                for c in range(2):
                    self.split_hi(act, base, c)

                def rows_out(i, b):
                    act.wait_ge(turned, NB * i)
                    return act.copy(row[:, b, :], self.bank[b])

                self.run_groups("hi", act, base, 2 * G, next_split=True, evacuate=rows_out)
                self.run_groups("hi", act, base_v, G,
                                evacuate=lambda i, b: act.copy(v[:, i, b, :] if isinstance(i, int) else
                                                               v[:, bass.ds(i, 1), b, :].rearrange("p a n -> p (a n)"),
                                                               self.bank[b]))

            @block.vector
            def _(dve):
                for c in range(2):
                    self.split_lo(dve, base, c)
                dve.wait_ge(rope_in, 16)

                def rotate(i, qk, at):
                    for b in range(NB):
                        heads = row[:, b, :].rearrange("p (h n) -> p h n", n=HEAD_DIM)
                        table = lambda a, n: rope[:, b, a:a + n].unsqueeze(1).to_broadcast([P, ATT_HEADS, n])
                        dve.wait_ge(self.bank_free[b], base + i + 1)
                        dve.wait_ge(rotated, NB * i + b)
                        dve.tensor_tensor(turn[:, 0], heads[:, :, 0:ROT_DIM], table(0, ROT_DIM), ALU.mult).then_inc(prod, 1)
                        dve.tensor_tensor(turn[:, 1, :, 0:HALF], heads[:, :, HALF:ROT_DIM], table(ROT_DIM, HALF),
                                          ALU.mult).then_inc(prod, 1)
                        dve.tensor_tensor(turn[:, 1, :, HALF:], heads[:, :, 0:HALF], table(ROT_DIM + HALF, HALF),
                                          ALU.mult).then_inc(prod, 1)
                        dve.wait_ge(prod, 3 * (NB * i + b + 1))
                        dve.tensor_tensor(heads[:, :, 0:ROT_DIM], turn[:, 0], turn[:, 1], ALU.add).then_inc(rotated, 1)
                    for b in range(NB):
                        dve.wait_ge(turned, NB * i + b + 1)
                        dve.tensor_copy(qk[:, bass.ds(at * HALF_KT, HALF_KT), b * P:(b + 1) * P],
                                        self.bank[4 + b].rearrange("p (d n) -> p d n", n=P)).then_inc(stored, 1)

                for first, qk in ((0, q), (G, k)):
                    with dve.Fori(0, G) as i:
                        for c in range(2):
                            self.split_lo(dve, base + first + i + 1, c)
                        rotate(first + i, qk, i)
                with dve.Fori(2 * G + 1, 3 * G) as i:
                    for c in range(2):
                        self.split_lo(dve, base + i, c)

    def att_heads(self, stack, q, k, v):
        nc, t = self.nc, self.t
        HEADS, TILES = ATT_HEADS, ATT_KEYS // P
        STEPS = RES * HEADS
        mask = self.sb(stack, "att_mask_sb", [P, 2, ATT_KEYS])
        neg = self.sb(stack, "att_negated", [P, 2, ATT_KEYS])
        pT = self.sb(stack, "att_probsT", [P, 2, TILES, P])
        low = self.sb(stack, "att_minus_max", [P, 2])
        den = self.sb(stack, "att_sum", [P, 2])
        inv = self.sb(stack, "att_inverse_sum", [P, 2])
        y = self.sb(stack, "att_y", [P, ATT_OUT])
        S = {n: self.sem("att_" + n) for n in ("scores", "max_done", "exp_done", "probs_turned", "probsT_a", "probsT_b",
                                               "pv_done", "inverted", "y_done", "y_turned", "y_out")}
        mask_in = [self.sem(f"att_mask_in{i}") for i in range(2)]
        SCALE = HEAD_DIM ** -0.5
        scores = [self.psum[:, 2 * u:2 * u + 2, :].rearrange("p a n -> p (a n)") for u in range(2)]
        def turn_y(r):
            pe = nc.tensor
            pe.wait_ge(S["y_done"], HEADS * (r + 1))
            if r:
                pe.wait_ge(S["y_out"], r)
            for d in range(HALF_KT):
                last = pe.transpose(self.bank[7][:, d * P:(d + 1) * P], y[:, d * P:(d + 1) * P], self.ident[:])
            last.then_inc(S["y_turned"], 1)

        def y_out(act, r):
            act.wait_ge(S["y_turned"], r + 1)
            act.copy(self.ya[:, :, r:SEQ:RES], self.bank[7].rearrange("p (d n) -> p d n", n=P)).then_inc(S["y_out"], 1)

        with nc.Block() as block:
            @block.sync
            def _(sp):
                for r in range(RES):
                    if r >= 2:
                        sp.wait_ge(S["max_done"], HEADS * (r - 1))
                    sp.dma_start(mask[:, r % 2, :], t["att_mask"][r]).then_inc(mask_in[r % 2], 16)

            @block.tensor
            def _(pe):
                def score(m):
                    r, head = divmod(m, HEADS)
                    p, h = divmod(head, 2)
                    part = slice(h * HEAD_DIM, (h + 1) * HEAD_DIM)
                    by4 = slice(r, SEQ, RES)
                    if m >= 2:
                        pe.wait_ge(S["max_done"], m - 1)
                    out = scores[m % 2]
                    pe.matmul(out[:, 0:SEQ], q[part, p, by4], k[part, p, :], start=True, stop=True)
                    for g in (1, 2):
                        at = SEQ + (g - 1) * P
                        last = pe.matmul(out[:, at:at + P], q[part, g * HALF_KT + p, by4], k[part, g * HALF_KT + p, by4],
                                         start=True, stop=True)
                    last.then_inc(S["scores"], 1)

                score(0)
                score(1)
                for m in range(STEPS):
                    r, head = divmod(m, HEADS)
                    u = m % 2
                    pe.wait_ge(S["exp_done"], m + 1)
                    if m:
                        pe.wait_ge(S["probsT_a"], m)
                        pe.wait_ge(S["probsT_b"], m)
                    for i in range(TILES):
                        last = pe.transpose(self.bank[4 + i // NB][:, (i % NB) * P:(i % NB + 1) * P],
                                            neg[:, u, i * P:(i + 1) * P], self.ident[:])
                        if i in (NB - 1, TILES - 1):
                            last.then_inc(S["probs_turned"], 1)
                    if m + 2 < STEPS:
                        score(m + 2)
                    pe.wait_ge(S["probsT_a"], m + 1)
                    pe.wait_ge(S["probsT_b"], m + 1)
                    if m:
                        pe.wait_ge(S["y_done"], m)
                    cols = slice(head * HEAD_DIM, (head + 1) * HEAD_DIM)
                    for i in range(TILES):
                        val = v[:, 0, i, cols] if i < NB else v[:, i - NB + 1, r, cols]
                        last = pe.matmul(self.bank[6][:, 0:HEAD_DIM], pT[:, u, i, :], val, start=(i == 0),
                                         stop=(i == TILES - 1))
                    last.then_inc(S["pv_done"], 1)
                    if head == HEADS - 1:
                        turn_y(r)

            @block.scalar
            def _(act):
                def exps(m):
                    act.wait_ge(S["max_done"], m + 1)
                    act.activation(neg[:, m % 2, :], neg[:, m % 2, :], ACT.Exp, bias=low[:, m % 2:m % 2 + 1], scale=-1.0,
                                   accum_out=den[:, m % 2:m % 2 + 1]).then_inc(S["exp_done"], 1)
                exps(0)
                exps(1)
                for m in range(STEPS):
                    r, head = divmod(m, HEADS)
                    act.wait_ge(S["probs_turned"], 2 * m + 1)
                    if m >= 2:
                        act.wait_ge(S["pv_done"], m - 1)
                    act.copy(pT[:, m % 2, 0:NB, :].rearrange("p a n -> p (a n)"), self.bank[4]).then_inc(S["probsT_a"], 1)
                    if m + 2 < STEPS:
                        act.wait_ge(S["inverted"], m + 1)
                        exps(m + 2)
                    if head == 0 and r:
                        y_out(act, r - 1)
                y_out(act, RES - 1)

            @block.vector
            def _(dve):
                def mask_and_max(m):
                    r, u = m // HEADS, m % 2
                    if m % HEADS == 0:
                        dve.wait_ge(mask_in[r % 2], 16 * (r // 2 + 1))
                    dve.wait_ge(S["scores"], m + 1)
                    if m >= 2:
                        dve.wait_ge(S["probs_turned"], 2 * (m - 1))
                    dve.tensor_tensor_reduce(out=neg[:, u, :], in0=scores[u][:, 0:ATT_KEYS], in1=mask[:, r % 2, :],
                                             scale=-SCALE, scalar=3.0e38, op0=ALU.add, op1=ALU.min,
                                             accum_out=low[:, u:u + 1]).then_inc(S["max_done"], 1)
                mask_and_max(0)
                mask_and_max(1)
                for m in range(STEPS):
                    r, head = divmod(m, HEADS)
                    u = m % 2
                    if m >= 2:
                        dve.wait_ge(S["y_done"], m - 1)
                    dve.wait_ge(S["exp_done"], m + 1)
                    dve.reciprocal(inv[:, u:u + 1], den[:, u:u + 1]).then_inc(S["inverted"], 1)
                    dve.wait_ge(S["probs_turned"], 2 * m + 2)
                    if m >= 2:
                        dve.wait_ge(S["pv_done"], m - 1)
                    dve.tensor_copy(pT[:, u, NB:, :].rearrange("p a n -> p (a n)"), self.bank[5][:, 0:2 * P]).then_inc(S["probsT_b"], 1)
                    if m + 2 < STEPS:
                        mask_and_max(m + 2)
                    dve.wait_ge(S["inverted"], m + 1)
                    dve.wait_ge(S["pv_done"], m + 1)
                    if r:
                        dve.wait_ge(S["y_turned"], r)
                    dve.tensor_scalar(y[:, head * HEAD_DIM:(head + 1) * HEAD_DIM], self.bank[6][:, 0:HEAD_DIM],
                                      inv[:, u:u + 1], None, ALU.mult).then_inc(S["y_done"], 1)

    def chunk_of(self, w, col):
        def source(c):
            return w[c * HALF_KT * P:(c + 1) * HALF_KT * P, bass.ds(col, COLS)].rearrange("(k p) n -> p k n", p=P)
        return source

    def merge(self, stack):
        with self.stage() as s:
            self.gates_and_branches(s)

    def gates_and_branches(self, stack):
        nc, t = self.nc, self.t
        GATES, GLA, MIX = 2 * D_MODEL // COLS, D_MODEL // COLS, D_MODEL // COLS
        base = self.groups
        base_att = base + GATES
        base_gla = base_att + 1
        base_mix = base_gla + GLA
        self.groups = base_mix + MIX
        self.ring(stack, "gates")
        gate = self.sb(stack, "gatesT", [P, 2 * KT, SEQ])
        yg_hi = self.sb(stack, "y_glaT_hi", [P, KT, SEQ], F32R)
        yg_lo = self.sb(stack, "y_glaT_lo", [P, KT, SEQ], F32R)
        part = self.sb(stack, "gated_gla", [P, 2, SEQ])
        ya_hi, ya_lo = (self.sb(stack, n, [P, HALF_KT, SEQ], F32R) for n in ("y_attT_hi", "y_attT_lo"))
        S = {n: self.sem("mix_" + n) for n in ("y_hi", "y_lo", "x_in", "att_gated", "gla_gated", "added", "merged_hi",
                                               "merged_lo", "gates_ready")}
        att_full = [self.sem(f"att_branch_full{b}") for b in range(NB)]
        merged = self.yg
        w_gla, w_att, w_mix = t["w_branch_gla"][0], t["w_branch_att"][0], t["w_mix_out"][0]

        with nc.Block() as block:
            @block.sync
            def _(sp):
                with sp.Fori(0, GATES) as i:
                    self.load_group(sp, base + i, lambda c: self.w_in_chunk(COL_GATE + COLS * i)(c))
                self.load_group(sp, base_att, lambda c: w_att[:, c * COLS:(c + 1) * COLS].rearrange("(k p) n -> p k n", p=P))
                for i in range(GLA):
                    self.load_group(sp, base_gla + i, self.chunk_of(w_gla, i * COLS))
                sp.wait_ge(S["y_lo"], 2)
                sp.dma_start(self.h[:], t["x"][0].rearrange("(b p) n -> p b n", p=P)).then_inc(S["x_in"], 16)
                for i in range(MIX):
                    self.load_group(sp, base_mix + i, self.chunk_of(w_mix, i * COLS))

            @block.tensor
            def _(pe):
                self.run_groups("multiply", pe, base, GATES, weights_stay=True)
                pe.wait_ge(S["y_lo"], 2)
                for c in range(2):
                    pe.wait_ge(self.lo_done[c], base_att + 1)
                    for b in range(NB):
                        bank = self.bank[b] if c else self.bank[4 + b]
                        if c:
                            pe.wait_ge(self.bank_free[b], base_att)
                        for k in range(HALF_KT):
                            col = slice(b * P, (b + 1) * P)
                            for n, (w, y) in enumerate(((self.whi, ya_hi), (self.whi, ya_lo), (self.wlo, ya_hi))):
                                last = pe.matmul(bank, w[c][:, k, col], y[:, k, :], start=(k == 0 and n == 0),
                                                 stop=(k == HALF_KT - 1 and n == 2))
                        last.then_inc(self.bank_full[b] if c else att_full[b], 1)
                        if c == 0 and b == NB - 1:
                            pe.wait_ge(att_full[b], 1)
                            pe.sem_inc(self.chunk_used, 1)
                for i in range(GLA):
                    self.multiply_group(pe, base_gla + i, None, weights_stay=True, lhs=(yg_hi, yg_lo))
                for i in range(MIX):
                    self.multiply_group(pe, base_mix + i, self.block_of,
                                        ready=lambda c: pe.wait_ge(S["merged_lo"], HALF_KT * (c + 1)))

            @block.scalar
            def _(act):
                for c in range(2):
                    self.split_hi(act, base, c)
                act.copy(ya_hi[:], self.ya[:]).then_inc(S["y_hi"], 1)
                act.copy(yg_hi[:], self.yg[:]).then_inc(S["y_hi"], 1)
                def gate_out(i, b):
                    return act.activation(gate[:, bass.ds(4 * i + b, 1), :].rearrange("p a n -> p (a n)"),
                                          self.bank[b], ACT.Sigmoid)
                self.run_groups("hi", act, base, GATES, next_split=True, evacuate=gate_out)
                for b in range(NB):
                    act.wait_ge(self.bank_free[b], base + GATES)
                act.sem_inc(S["gates_ready"], 1)
                for g in range(base_gla, base_mix + 1):
                    self.split_hi(act, g, 0)
                    self.split_hi(act, g, 1)
                    if g > base_gla:
                        self.merged_hi(act, S, merged, g - 1 - base_gla)
                self.split_hi(act, base_mix + 1, 0)
                self.split_hi(act, base_mix + 1, 1)

            @block.vector
            def _(dve):
                for c in range(2):
                    self.split_lo(dve, base, c)
                for n, (lo, y, hi) in enumerate(((ya_lo, self.ya, ya_hi), (yg_lo, self.yg, yg_hi))):
                    dve.wait_ge(S["y_hi"], n + 1)
                    dve.tensor_tensor(lo[:], y[:], hi[:].bitcast(F32), ALU.subtract).then_inc(S["y_lo"], 1)
                with dve.Fori(1, GATES + 1) as i:
                    for c in range(2):
                        self.split_lo(dve, base + i, c)
                dve.wait_ge(S["gates_ready"], 1)
                dve.wait_ge(S["y_lo"], 2)
                for c in range(2):
                    for b in range(NB):
                        m = NB * c + b
                        dve.wait_ge(self.bank_full[b] if c else att_full[b], base_att + 1 if c else 1)
                        dve.tensor_tensor(merged[:, m, :], gate[:, KT + m, :], self.bank[b] if c else self.bank[4 + b],
                                          ALU.mult).then_inc(self.bank_free[b] if c else S["att_gated"], 1)
                    self.split_lo(dve, base_gla, c)
                for i in range(GLA):
                    self.split_lo(dve, base_gla + i + 1, 0)
                    for b in range(NB):
                        m = NB * i + b
                        dve.wait_ge(self.bank_full[b], base_gla + i + 1)
                        if m >= 2:
                            dve.wait_ge(S["added"], m - 1)
                        dve.tensor_tensor(part[:, m % 2], gate[:, m, :], self.bank[b], ALU.mult).then_inc(self.bank_free[b], 1)
                        dve.wait_ge(self.bank_free[b], base_gla + i + 1)
                        dve.wait_ge(S["att_gated"], NB)
                        dve.wait_ge(self.bank_free[b], base_gla)
                        dve.tensor_tensor(merged[:, m, :], merged[:, m, :], part[:, m % 2], ALU.add).then_inc(S["added"], 1)
                        if b == NB - 1:
                            self.split_lo(dve, base_gla + i + 1, 1)
                        if b:
                            self.merged_lo(dve, S, merged, m - 1)
                    self.merged_lo(dve, S, merged, m)
                self.split_lo(dve, base_mix + 1, 0)
                dve.wait_ge(S["x_in"], 16)
                for i in range(MIX):
                    for b in range(NB):
                        dve.wait_ge(self.bank_full[b], base_mix + i + 1)
                        part_h = self.h[:, b, i * COLS:(i + 1) * COLS]
                        dve.tensor_tensor(part_h, part_h, self.bank[b], ALU.add).then_inc(self.bank_free[b], 1)
                    if i == 0:
                        self.split_lo(dve, base_mix + 1, 1)

    def merged_hi(self, act, S, merged, i):
        for m in range(NB * i, NB * (i + 1)):
            act.wait_ge(S["added"], m + 1)
            act.copy(self.x_hi[:, m, :], merged[:, m, :]).then_inc(S["merged_hi"], 1)

    def merged_lo(self, dve, S, merged, m):
        dve.wait_ge(S["merged_hi"], m + 1)
        dve.tensor_tensor(self.x_lo[:, m, :], merged[:, m, :], self.x_hi[:, m, :].bitcast(F32),
                          ALU.subtract).then_inc(S["merged_lo"], 1)


    def route(self, stack):
        nc, t = self.nc, self.t
        h = self.h
        E = N_EXPERTS
        sq = self.sb(stack, "h_squares", [P, D_MODEL])
        ss = self.sb(stack, "h_sum_squares", [P, NB])
        rs = self.sb(stack, "h_rstd", [P, NB])
        g = self.sb(stack, "norm_ffn_g_row", [P, D_MODEL])
        hn = self.sb(stack, "hn", [P, NB, D_MODEL])
        hT = self.sb(stack, "hnT", [P, KT, SEQ])
        rw = self.sb(stack, "router_w_sb", [P, KT, E])
        rb = self.sb(stack, "router_b_row", [P, E])
        logits = self.sb(stack, "logits", [P, NB, E])
        top = self.sb(stack, "top_logits", [P, NB, 8])
        who = self.sb(stack, "top_experts", [P, NB, 8], U32)
        who_f = self.sb(stack, "top_experts_f", [P, NB, TOP_K])
        low = self.sb(stack, "minus_top", [P, NB])
        ex = self.sb(stack, "top_exps", [P, NB, TOP_K])
        tot = self.sb(stack, "top_sums", [P, NB])
        weight = self.sb(stack, "top_weights", [P, NB, TOP_K])
        hot = self.sb(stack, "one_hot", [P, NB, E])
        hot_w = self.sb(stack, "one_hot_weighted", [P, NB, E])
        sel = self.sb(stack, "selected", [P, NB, E])
        wsum = self.sb(stack, "weights", [P, NB, E])
        before = self.sb(stack, "before_sb", [P, P])
        ones = self.sb(stack, "ones_sb", [P, P])
        e_no = self.sb(stack, "expert_numbers_sb", [P, E])
        tok = self.sb(stack, "token_numbers_sb", [P, NB])
        half = self.sb(stack, "minus_half2", [P, 1])
        extra, run, past, ones_e = (self.sb(stack, n, [P, E]) for n in ("extra_blocks", "extra_sums", "past", "ones_e"))
        starts = self.sb(stack, "block_starts_sb", [P, self.FURTHER])
        cmp = self.sb(stack, "blocks_before", [P, self.FURTHER, E])
        be = self.sb(stack, "block_expert_f", [P, self.FURTHER])
        far = self.sb(stack, "beyond_first_block", [P, NB, E])
        S = {n: self.sem("route_" + n) for n in ("in", "sums", "powed", "hn_done", "stored", "turned", "hT_out", "logits",
                                                 "low", "exps", "selected", "ranks", "bias_in", "bias_hi")}
        bias, raw_bias = self.bias, self.sb(stack, "biases_twice", [2 * E, 3 * self.WIDE])
        with nc.Block() as block:
            @block.sync
            def _(sp):
                sp.dma_start(self.total.rearrange("(b p) n -> p b n", p=P), h[:]).then_inc(S["stored"], 16)
                sp.dma_start(g[:], t["norm_ffn_g"][0:1, :].partition_broadcast(P).rearrange("p a n -> p (a n)")).then_inc(S["in"], 16)
                sp.dma_start(rw[:], t["router_w"][0].rearrange("(k p) n -> p k n", p=P)).then_inc(S["in"], 16)
                sp.dma_start(rb[:], t["router_b"][0:1, :].partition_broadcast(P).rearrange("p a n -> p (a n)")).then_inc(S["in"], 16)
                sp.dma_start(before[:], t["before"]).then_inc(S["in"], 16)
                sp.dma_start(e_no[:], t["expert_numbers"]).then_inc(S["in"], 16)
                sp.dma_start(tok[:], t["token_numbers"]).then_inc(S["in"], 16)
                sp.dma_start(starts[:], t["block_starts"]).then_inc(S["in"], 16)
                for n in range(2):
                    at = slice(n * E, (n + 1) * E)
                    sp.dma_start(raw_bias[at, 0:2 * self.WIDE], t["expert_b_gate_up"][0]).then_inc(S["bias_in"], 16)
                    sp.dma_start(raw_bias[at, 2 * self.WIDE:], t["expert_b_down"][0]).then_inc(S["bias_in"], 16)
                for j in range(2):
                    sp.dma_start(self.expert_ring[j][:], self.expert_weights(0, j)).then_inc(self.first_expert[j], 16)
                sp.wait_ge(S["hn_done"], NB)
                sp.dma_start(self.normed.rearrange("(b p) n -> p b n", p=P), hn[:]).then_inc(S["stored"], 16)
                for j in range(2, self.CHUNKS):
                    sp.dma_start(self.expert_ring[j][:], self.expert_weights(0, j)).then_inc(self.first_expert[j], 16)
                sp.wait_ge(S["stored"], 32)

            @block.gpsimd
            def _(pool):
                link = self.link("pool", pool)
                link(pool.memset(bias[2 * E:, :].bitcast(F32), 0.0))
                link(pool.memset(ones[:], 1.0))
                link(pool.memset(half[:], -0.5))
                pool.wait_ge(S["sums"], 1)
                pool.tensor_tensor(rs[:], ss[:], half[:, 0:1].to_broadcast([P, NB]), ALU.pow).then_inc(S["powed"], 1)

            @block.tensor
            def _(pe):
                for b in range(NB):
                    pe.wait_ge(S["hn_done"], b + 1)
                    for hf in range(2):
                        i = 2 * b + hf
                        if i >= 2:
                            pe.wait_ge(S["hT_out"], i - 1)
                        for k in range(HALF_KT):
                            last = pe.transpose(self.bank[i % 2][:, k * P:(k + 1) * P],
                                                hn[:, b, (HALF_KT * hf + k) * P:(HALF_KT * hf + k + 1) * P], self.ident[:])
                        last.then_inc(S["turned"], 1)
                pe.wait_ge(S["in"], 7 * 16)
                pe.wait_ge(S["hT_out"], 2 * NB)
                for b in range(NB):
                    for k in range(KT):
                        last = pe.matmul(self.bank[2][:, b * E:(b + 1) * E], hT[:, k, b * P:(b + 1) * P], rw[:, k, :],
                                         start=(k == 0), stop=(k == KT - 1))
                last.then_inc(S["logits"], 1)
                pe.wait_ge(S["selected"], 1)
                pe.wait_ge(S["powed"], 1)
                for b in range(NB):
                    for a in range(b + 1):
                        last = pe.matmul(self.bank[3][:, b * E:(b + 1) * E], (before if a == b else ones)[:], sel[:, a, :],
                                         start=(a == 0), stop=(a == b))
                for a in range(NB):
                    last = pe.matmul(self.bank[4][:, 0:E], ones[:], sel[:, a, :], start=(a == 0), stop=(a == NB - 1))
                last.then_inc(S["ranks"], 1)

            @block.scalar
            def _(act):
                for i in range(2 * NB):
                    b, hf = divmod(i, 2)
                    act.wait_ge(S["turned"], i + 1)
                    act.copy(hT[:, HALF_KT * hf:HALF_KT * (hf + 1), b * P:(b + 1) * P],
                             self.bank[i % 2].rearrange("p (k n) -> p k n", n=P)).then_inc(S["hT_out"], 1)
                act.wait_ge(S["bias_in"], 64)
                act.copy(bias[0:2 * E, :], raw_bias[:]).then_inc(S["bias_hi"], 1)
                act.wait_ge(S["low"], 1)
                for b in range(NB):
                    act.activation(ex[:, b, :], top[:, b, 0:TOP_K], ACT.Exp, bias=low[:, b:b + 1],
                                   accum_out=tot[:, b:b + 1]).then_inc(S["exps"], 1)

            @block.vector
            def _(dve):
                link = self.link("dve", dve)
                for b in range(NB):
                    link(dve.scalar_tensor_tensor(out=sq[:], in0=h[:, b, :], scalar=1.0, in1=h[:, b, :], op0=ALU.mult,
                                                  op1=ALU.mult, accum_out=ss[:, b:b + 1]))
                dve.tensor_scalar(ss[:], ss[:], 1.0 / D_MODEL, EPS, ALU.mult, ALU.add).then_inc(S["sums"], 1)
                dve.wait_ge(S["in"], 7 * 16)
                dve.wait_ge(S["powed"], 1)
                for b in range(NB):
                    dve.scalar_tensor_tensor(out=hn[:, b, :], in0=h[:, b, :], scalar=rs[:, b:b + 1], in1=g[:],
                                             op0=ALU.mult, op1=ALU.mult).then_inc(S["hn_done"], 1)
                dve.wait_ge(S["bias_hi"], 1)
                low_rows = slice(E, 2 * E)
                link(dve.tensor_tensor(bias[low_rows, :], raw_bias[low_rows, :], bias[low_rows, :].bitcast(F32), ALU.subtract))
                dve.wait_ge(S["logits"], 1)
                link(dve.tensor_tensor(logits[:], self.bank[2][:, 0:NB * E].rearrange("p (b n) -> p b n", n=E),
                                       rb[:].unsqueeze(1).to_broadcast([P, NB, E]), ALU.add))
                for b in range(NB):
                    link(dve.max(top[:, b, :], logits[:, b, :]))
                    link(dve.max_index(who[:, b, :], top[:, b, :], logits[:, b, :]))
                dve.tensor_scalar(low[:], top[:, :, 0], -1.0, None, ALU.mult).then_inc(S["low"], 1)
                link(dve.tensor_copy(who_f[:], who[:, :, 0:TOP_K]))
                dve.wait_ge(S["exps"], NB)
                link(dve.reciprocal(tot[:], tot[:]))
                link(dve.tensor_tensor(weight[:], ex[:], tot[:].unsqueeze(2).to_broadcast([P, NB, TOP_K]), ALU.mult))
                for k in range(TOP_K):
                    dst, dst_w = (hot, hot_w) if k else (sel, wsum)
                    link(dve.tensor_tensor(dst[:], e_no[:].unsqueeze(1).to_broadcast([P, NB, E]),
                                           who_f[:, :, k:k + 1].to_broadcast([P, NB, E]), ALU.is_equal))
                    link(dve.tensor_tensor(dst_w[:], dst[:], weight[:, :, k:k + 1].to_broadcast([P, NB, E]), ALU.mult))
                    if k:
                        link(dve.tensor_tensor(sel[:], sel[:], hot[:], ALU.add))
                        link(dve.tensor_tensor(wsum[:], wsum[:], hot_w[:], ALU.add))
                dve.sem_inc(S["selected"], 1)
                dve.tensor_copy(self.pairs[:, :, :, 1], wsum[:])
                dve.tensor_scalar(self.pairs[:, :, :, 0], tok[:].unsqueeze(2).to_broadcast([P, NB, E]), 1.0, None, ALU.add)
                dve.wait_ge(S["ranks"], 1)
                link(dve.scalar_tensor_tensor(out=self.rank[:], in0=self.bank[3][:, 0:NB * E].rearrange("p (b n) -> p b n", n=E),
                                              scalar=1.0, in1=sel[:], op0=ALU.add, op1=ALU.mult))
                link(dve.tensor_scalar(self.rank[:], self.rank[:], -1.0, None, ALU.add))
                counts = self.bank[4][:, 0:E]
                link(dve.tensor_scalar(extra[:], counts, float(P), None, ALU.is_gt))
                for n in range(2, NB):
                    link(dve.tensor_scalar(past[:], counts, float(n * P), None, ALU.is_gt))
                    link(dve.tensor_tensor(extra[:], extra[:], past[:], ALU.add))
                link(dve.memset(ones_e[:], 1.0))
                link(dve.tensor_tensor_scan(run[:], ones_e[:], extra[:], 0.0, ALU.mult, ALU.add))
                link(dve.tensor_copy(self.n_further[:], run[:, E - 1:E]))
                link(dve.tensor_scalar(past[:], run[:], float(P), None, ALU.mult))
                link(dve.tensor_tensor(cmp[:], past[:].unsqueeze(1).to_broadcast([P, self.FURTHER, E]),
                                       starts[:].unsqueeze(2).to_broadcast([P, self.FURTHER, E]), ALU.is_le))
                link(dve.tensor_reduce(be[:], cmp[:], AX.X, ALU.add))
                link(dve.tensor_scalar(self.block_expert[:], be[:], float(E - 1), None, ALU.min))
                link(dve.tensor_scalar(extra[:], extra[:], -float(P), 1.0 - P, ALU.mult, ALU.add))
                link(dve.tensor_tensor(extra[:], extra[:], past[:], ALU.add))
                link(dve.tensor_scalar(far[:], self.rank[:], float(P), None, ALU.is_ge))
                link(dve.tensor_tensor(self.place[:], self.rank[:], extra[:].unsqueeze(1).to_broadcast([P, NB, E]), ALU.add))
                link(dve.tensor_tensor(self.place[:], self.place[:], far[:], ALU.mult))
                link(dve.tensor_scalar(self.place[:], self.place[:], -1.0, None, ALU.add))

    CHUNKS, PER_HALF, SLOTS, WIDE = 12, 4, 3, 1024
    FURTHER = SEQ * TOP_K // P

    def expert_weights(self, e, j):
        wgu, wd, W = self.t["expert_w_gate_up"][0], self.t["expert_w_down"][0], self.WIDE
        stage, k = divmod(j, self.PER_HALF)
        rows = slice(k * 2 * P, (k + 1) * 2 * P)
        src = wd[bass.ds(e, 1), rows, :] if stage == 2 else wgu[bass.ds(e, 1), rows, stage * W:(stage + 1) * W]
        return src.rearrange("a (k p) n -> p (a k) n", p=P)

    def experts(self, stack):
        nc, t = self.nc, self.t
        E, N, W = N_EXPERTS, self.CHUNKS, self.WIDE
        raw, loaded = self.expert_ring, self.first_expert
        whi = [self.sb(stack, f"expert_hi{j}", [P, 2, W], F32R) for j in range(self.SLOTS)]
        wlo = [self.sb(stack, f"expert_lo{j}", [P, 2, W], F32R) for j in range(self.SLOTS)]
        bias = self.bias
        rows, y, a = (self.h[:, b, :] for b in range(3))
        x_hi, x_lo = (self.sb(stack, n, [P, KT, P], F32R) for n in ("rowsT_hi", "rowsT_lo"))
        gv = self.sb(stack, "gate_values", [P, 2, W // 4])
        uv = self.sb(stack, "up_values", [P, 2, W // 4])
        sg = self.sb(stack, "gate_sigmoid", [P, 2, W // 4])
        a_hi, a_lo = (self.sb(stack, n, [P, KT, P], F32R) for n in ("activationsT_hi", "activationsT_lo"))
        hot = self.sb(stack, "slots_one_hot", [P, NB, P])
        slot_no = self.sb(stack, "slot_numbers_sb", [P, P])
        bias_row = self.sb(stack, "bias_row_sb", [P, E])
        pick = self.sb(stack, "bias_pick", [P, P], F32R)
        none = self.sb(stack, "empty_slot", [P, 1])
        index = [self.sb(stack, f"row_index{u}", [P, 1], I32) for u in range(2)]
        weight = [self.sb(stack, f"row_weight{u}", [P, 1]) for u in range(2)]
        S = {n: self.sem("moe_" + n) for n in (
            "tables_in", "hi", "lo", "slots_free", "hA_full", "hB_full", "gu", "sig", "p", "act",
            "act_turned", "aT_hi", "aT_lo", "y_full", "y_out", "scattered", "hot", "listed", "none", "index", "gathered",
            "x_turned", "x_hi", "x_lo", "picked", "cleared", "passed")}
        h_full = (S["hA_full"], S["hB_full"])
        QUARTER = W // 4

        def hi(act, e, j):
            act.wait_ge(loaded[j], 16 * e + 16)
            act.wait_ge(S["slots_free"], N * e + j + 1)
            act.copy(whi[j % self.SLOTS][:], raw[j][:]).then_inc(S["hi"], 1)

        def lo(dve, e, j):
            dve.wait_ge(S["hi"], N * e + j + 1)
            s = j % self.SLOTS
            dve.tensor_tensor(wlo[s][:], raw[j][:], whi[s][:].bitcast(F32), ALU.subtract).then_inc(S["lo"], 1)

        def list_hot(dve, e):
            dve.wait_ge(S["listed"], e)
            dve.tensor_tensor(hot[:], slot_no[:].unsqueeze(1).to_broadcast([P, NB, P]),
                              self.rank[:, :, bass.ds(e, 1)].to_broadcast([P, NB, P]), ALU.is_equal).then_inc(S["hot"], 1)

        def list_rows(pe, e):
            pe.wait_ge(S["hot"], e + 1)
            if not isinstance(e, int) or e:
                pe.wait_ge(S["y_out"], 2 * e - 2)
            for b in range(NB):
                last = pe.matmul(self.bank[4][:, 0:2], hot[:, b, :],
                                 self.pairs[:, b, bass.ds(e, 1), :].rearrange("p a n -> p (a n)"),
                                 start=(b == 0), stop=(b == NB - 1))
            last.then_inc(S["listed"], 1)

        def list_index(dve, e, u):
            dve.wait_ge(S["listed"], e + 1)
            dve.wait_ge(S["index"], 2 * e)
            if not isinstance(e, int) or e:
                dve.wait_ge(S["scattered"], 16 * (e - 1))
            dve.tensor_scalar(none[:], self.bank[4][:, 0:1], 0.0, 8.0 * SEQ, ALU.is_equal, ALU.mult).then_inc(S["none"], 1)
            dve.wait_ge(S["none"], e + 1)
            dve.scalar_tensor_tensor(out=index[u][:], in0=none[:], scalar=-1.0, in1=self.bank[4][:, 0:1],
                                     op0=ALU.add, op1=ALU.add).then_inc(S["index"], 1)
            dve.tensor_copy(weight[u][:], self.bank[4][:, 1:2]).then_inc(S["index"], 1)

        def gather(pool, e, u):
            pool.wait_ge(S["index"], 2 * e + 2)
            if not isinstance(e, int) or e:
                pool.wait_ge(S["x_turned"], 2 * e)
            pool.sem_inc(S["passed"], 1)
            pool.indirect_dma_start(rows, None, self.normed, bass.IndirectOffsetOnAxis(ap=index[u][:, 0:1], axis=0),
                                    bounds_check=self.last_row, oob_is_err=False).then_inc(S["gathered"], 16)

        def turn_rows(pe, e):
            pe.wait_ge(S["gathered"], 16 * e + 16)
            pe.wait_ge(S["aT_lo"], 2 * e)
            for f in range(2):
                for k in range(HALF_KT):
                    last = pe.transpose(self.bank[6 + f][:, k * P:(k + 1) * P],
                                        rows[:, (HALF_KT * f + k) * P:(HALF_KT * f + k + 1) * P], self.ident[:])
                last.then_inc(S["x_turned"], 1)

        def split_turned(eng, e, part, f, turned, first, second, hi_t, lo_t):
            dst = slice(HALF_KT * f, HALF_KT * (f + 1))
            bank = self.bank[6 + f].rearrange("p (k n) -> p k n", n=P)
            if part == "hi":
                eng.wait_ge(turned, 2 * e + f + 1)
                eng.copy(hi_t[:, dst, :], bank).then_inc(first, 1)
            else:
                eng.wait_ge(first, 2 * e + f + 1)
                eng.tensor_tensor(lo_t[:, dst, :], bank, hi_t[:, dst, :].bitcast(F32), ALU.subtract).then_inc(second, 1)

        x_part = lambda eng, e, part, f: split_turned(eng, e, part, f, S["x_turned"], S["x_hi"], S["x_lo"], x_hi, x_lo)
        a_part = lambda eng, e, part, f: split_turned(eng, e, part, f, S["act_turned"], S["aT_hi"], S["aT_lo"], a_hi, a_lo)

        def pick_bias(dve, e):
            dve.tensor_copy(pick[:], bias_row[:, bass.ds(e, 1)].to_broadcast([P, P])).then_inc(S["picked"], 1)

        def expert_pe(pe, e, more):
            for j in range(N):
                s = j % self.SLOTS
                stage, k = divmod(j, self.PER_HALF)
                banks = [self.bank[2 * stage + i] for i in range(2)]
                t_hi, t_lo = (a_hi, a_lo) if stage == 2 else (x_hi, x_lo)
                if j == 0:
                    pe.wait_ge(S["x_lo"], 2 * e + 2)
                    pe.wait_ge(S["picked"], e + 1)
                if stage == 2:
                    pe.wait_ge(S["aT_lo"], 2 * e + k // 2 + 1)
                if k == 0:
                    if stage < 2:
                        pe.wait_ge(S["gu"], 8 * e)
                    else:
                        pe.wait_ge(S["y_out"], 2 * e)
                        if more:
                            pe.wait_ge(S["index"], 2 * e + 4)
                    for i, bank in enumerate(banks):
                        col = stage * W + i * COLS
                        pe.matmul(bank, pick[:], bias[:, col:col + COLS], start=True, stop=False)
                pe.wait_ge(S["lo"], N * e + j + 1)
                for kk in range(2):
                    row = 2 * k + kk
                    for x, w in ((t_hi, whi), (t_hi, wlo), (t_lo, whi)):
                        for i, bank in enumerate(banks):
                            last = pe.matmul(bank, x[:, row, :], w[s][:, kk, i * COLS:(i + 1) * COLS], start=False,
                                             stop=(k == self.PER_HALF - 1 and kk == 1 and x is t_lo))
                last.then_inc(S["slots_free"], 1)
                if j == 2 and more:
                    list_rows(pe, e + 1)
                if j in (5, 8):
                    f = j // 8
                    pe.wait_ge(S["act"], 4 * e + 2 * f + 2)
                    pe.wait_ge(S["x_lo"], 2 * e + 2)
                    for k2 in range(HALF_KT):
                        last = pe.transpose(self.bank[6 + f][:, k2 * P:(k2 + 1) * P],
                                            a[:, (HALF_KT * f + k2) * P:(HALF_KT * f + k2 + 1) * P], self.ident[:])
                    last.then_inc(S["act_turned"], 1)
                if j == 9 and more:
                    turn_rows(pe, e + 1)

        def gate_sigmoid(act, e, i):
            act.wait_ge(S["gu"], 8 * e + 2 * i + 1)
            act.wait_ge(S["act"], 4 * e + (2 if i >= 2 else 0))
            act.activation(sg[:, i % 2, :], gv[:, i % 2, :], ACT.Sigmoid, scale=SWIGLU_ALPHA).then_inc(S["sig"], 1)

        def rows_out(act, e, u):
            for i in range(2):
                act.wait_ge(S["slots_free"], N * e + N + self.SLOTS)
                act.wait_ge(S["scattered"], 16 * e)
                act.activation(y[:, i * COLS:(i + 1) * COLS], self.bank[4 + i], ACT.Copy,
                               scale=weight[u][:, 0:1]).then_inc(S["y_out"], 1)

        def expert_act(act, e, u, more):
            for j in range(self.SLOTS, N):
                hi(act, e, j)
                if j in (6, 9):
                    for i in range(2):
                        gate_sigmoid(act, e, 2 * (j // 9) + i)
                if j == 8:
                    a_part(act, e, "hi", 0)
                if j == 10:
                    a_part(act, e, "hi", 1)
            if more:
                hi(act, e + 1, 0)
                for f in range(2):
                    x_part(act, e + 1, "hi", f)
                hi(act, e + 1, 1)
                hi(act, e + 1, 2)
            rows_out(act, e, u)

        def swiglu_in(dve, e, half):
            dve.wait_ge(S["slots_free"], N * e + self.PER_HALF * (half + 1) + self.SLOTS)
            for i in (2 * half, 2 * half + 1):
                both = self.bank[i].rearrange("p (n a) -> p n a", a=2)
                dve.wait_ge(S["act"], 4 * e + 2 * half)
                dve.tensor_scalar(gv[:, i % 2, :], both[:, :, 0], SWIGLU_LIMIT, None, ALU.min).then_inc(S["gu"], 1)
                dve.tensor_scalar(uv[:, i % 2, :], both[:, :, 1], SWIGLU_LIMIT, -SWIGLU_LIMIT, ALU.min,
                                  ALU.max).then_inc(S["gu"], 1)

        def swiglu_out(dve, e, half):
            for i in (2 * half, 2 * half + 1):
                dve.wait_ge(S["gu"], 8 * e + 2 * i + 2)
                dve.scalar_tensor_tensor(out=uv[:, i % 2, :], in0=uv[:, i % 2, :], scalar=1.0, in1=gv[:, i % 2, :],
                                         op0=ALU.add, op1=ALU.mult).then_inc(S["p"], 1)
            for i in (2 * half, 2 * half + 1):
                dve.wait_ge(S["p"], 4 * e + i + 1)
                dve.wait_ge(S["sig"], 4 * e + i + 1)
                dve.wait_ge(S["act_turned"], 2 * e)
                dve.tensor_tensor(a[:, i * QUARTER:(i + 1) * QUARTER], uv[:, i % 2, :], sg[:, i % 2, :],
                                  ALU.mult).then_inc(S["act"], 1)

        def expert_dve(dve, e, u, more):
            for j in range(self.SLOTS, N):
                if j in (6, 10):
                    swiglu_in(dve, e, j // 8)
                if j != 10:
                    lo(dve, e, j)
                if j in (6, 10):
                    swiglu_out(dve, e, j // 8)
                if j == 10:
                    lo(dve, e, j)
                if j == 3 and more:
                    list_hot(dve, e + 1)
                if j == 5 and more:
                    list_index(dve, e + 1, 1 - u)
                if j in (8, 10):
                    a_part(dve, e, "lo", j // 9)
            if more:
                dve.wait_ge(S["slots_free"], N * e + 9 + self.SLOTS)
                pick_bias(dve, e + 1)
                lo(dve, e + 1, 0)
                for f in range(2):
                    x_part(dve, e + 1, "lo", f)
                lo(dve, e + 1, 1)
                lo(dve, e + 1, 2)

        def scatter(pool, e, u):
            pool.wait_ge(S["y_out"], 2 * e + 2)
            pool.wait_ge(S["scattered"], 16 * e)
            pool.sem_inc(S["passed"], 1)
            pool.indirect_dma_start(self.total, bass.IndirectOffsetOnAxis(ap=index[u][:, 0:1], axis=0), y, None,
                                    bounds_check=self.last_row, oob_is_err=False, compute_op=ALU.add).then_inc(S["scattered"], 16)

        def over_experts(engine, body):
            with engine.Fori(0, E // 2 - 1) as i:
                for u in range(2):
                    body(2 * i + u, u, True)
            body(E - 2, 0, True)
            body(E - 1, 1, False)

        with nc.Block() as block:
            @block.sync
            def _(sp):
                sp.dma_start(slot_no[:], t["slot_numbers"]).then_inc(S["tables_in"], 16)
                sp.dma_start(bias_row[:], t["bias_row"]).then_inc(S["tables_in"], 16)
                with sp.Fori(0, E - 1) as e:
                    for j in range(N):
                        sp.wait_ge(S["lo"], N * e + j + 1)
                        sp.dma_start(raw[j][:], self.expert_weights(e + 1, j)).then_inc(loaded[j], 16)

            @block.gpsimd
            def _(pool):
                pool.memset(rows, 0.0).then_inc(S["cleared"], 1)
                self.last_row = pool.to_reg(SEQ - 1)
                pool.wait_ge(S["cleared"], 1)
                gather(pool, 0, 0)
                def body(e, u, more):
                    if more:
                        gather(pool, e + 1, 1 - u)
                    scatter(pool, e, u)
                over_experts(pool, body)
                pool.wait_ge(S["scattered"], 16 * E)

            @block.scalar
            def _(act):
                for f in range(2):
                    x_part(act, 0, "hi", f)
                for j in range(self.SLOTS):
                    hi(act, 0, j)
                over_experts(act, lambda e, u, more: expert_act(act, e, u, more))

            @block.vector
            def _(dve):
                dve.wait_ge(S["tables_in"], 32)
                list_hot(dve, 0)
                list_index(dve, 0, 0)
                pick_bias(dve, 0)
                for f in range(2):
                    x_part(dve, 0, "lo", f)
                for j in range(self.SLOTS):
                    lo(dve, 0, j)
                over_experts(dve, lambda e, u, more: expert_dve(dve, e, u, more))

            @block.tensor
            def _(pe):
                pe.sem_inc(S["slots_free"], self.SLOTS)
                list_rows(pe, 0)
                turn_rows(pe, 0)
                over_experts(pe, lambda e, u, more: expert_pe(pe, e, more))

    def further_blocks(self, stack):
        nc, t = self.nc, self.t
        E, N, W, RING = N_EXPERTS, self.CHUNKS, self.WIDE, 4
        wgu, wd = t["expert_w_gate_up"][0], t["expert_w_down"][0]
        ring = [self.sb(stack, f"further_chunk{j}", [P, 2, W]) for j in range(RING)]
        bias = self.sb(stack, "further_biases", [E, 3 * W])
        rows = self.sb(stack, "further_rows", [P, W])
        xT = self.sb(stack, "further_rowsT", [P, KT, P])
        gv, uv, sg, a = (self.sb(stack, "further_" + n, [P, FF]) for n in ("gate", "up", "sigmoid", "act"))
        aT = self.sb(stack, "further_actT", [P, KT, P])
        y = self.sb(stack, "further_out", [P, W])
        hot = self.sb(stack, "further_one_hot", [P, NB, P])
        slot_no = self.sb(stack, "further_slot_numbers", [P, P])
        starts = self.sb(stack, "further_starts", [P, self.FURTHER])
        one = self.sb(stack, "further_bias_rows", [P, E])
        pick = self.sb(stack, "further_bias_pick", [E, P])
        place = self.sb(stack, "further_place", [P, NB])
        none = self.sb(stack, "further_empty", [P, 1])
        index = self.sb(stack, "further_index", [P, 1], I32)
        weight = self.sb(stack, "further_weight", [P, 1])
        S = {n: self.sem("further_" + n) for n in (
            "in", "cleared", "place", "hot", "listed", "none", "index", "gathered", "x_turned", "xT", "picked", "used",
            "h_full", "split", "sig", "p", "act", "a_turned", "aT", "y_full", "y_out", "scattered", "passed")}
        loaded = [self.sem(f"further_loaded{j}") for j in range(RING)]
        flat = lambda ap: ap.rearrange("p k n -> p (k n)")

        def when_any(engine, body):
            n = engine.value_load(self.n_further[0:1, 0:1], min_val=0, max_val=self.FURTHER)
            with engine.If(n > 0):
                with engine.Fori(0, self.FURTHER) as i:
                    body(i)
            with engine.Else():
                engine.nop()

        def expert_of(engine, i):
            return engine.value_load(self.block_expert[0:1, bass.ds(i, 1)], min_val=0, max_val=E - 1)

        with nc.Block() as block:
            @block.sync
            def _(sp):
                sp.dma_start(slot_no[:], t["slot_numbers"]).then_inc(S["in"], 16)
                sp.dma_start(starts[:], t["block_starts"]).then_inc(S["in"], 16)
                sp.dma_start(one[:], t["bias_row"]).then_inc(S["in"], 16)
                sp.dma_start(bias[:, 0:2 * W], t["expert_b_gate_up"][0]).then_inc(S["in"], 16)
                sp.dma_start(bias[:, 2 * W:], t["expert_b_down"][0]).then_inc(S["in"], 16)
                sp.wait_ge(S["in"], 80)

                def body(i):
                    e = expert_of(sp, i)
                    for j in range(N):
                        half, k = divmod(j, self.PER_HALF)
                        rows_ = slice(k * 2 * P, (k + 1) * 2 * P)
                        src = wd[bass.ds(e, 1), rows_, :] if half == 2 else wgu[bass.ds(e, 1), rows_, half * W:(half + 1) * W]
                        sp.wait_ge(S["used"], N * i + j + 1)
                        sp.dma_start(ring[j % RING][:], src.rearrange("a (k p) n -> p (a k) n", p=P)).then_inc(loaded[j % RING], 16)
                when_any(sp, body)

            @block.gpsimd
            def _(pool):
                pool.memset(rows[:], 0.0).then_inc(S["cleared"], 1)
                pool.wait_ge(S["cleared"], 1)
                last_row = pool.to_reg(SEQ - 1)

                def body(i):
                    pool.wait_ge(S["index"], 2 * i + 2)
                    pool.sem_inc(S["passed"], 1)
                    pool.indirect_dma_start(rows[:], None, self.normed, bass.IndirectOffsetOnAxis(ap=index[:, 0:1], axis=0),
                                            bounds_check=last_row, oob_is_err=False).then_inc(S["gathered"], 16)
                    pool.wait_ge(S["y_out"], 2 * i + 2)
                    pool.sem_inc(S["passed"], 1)
                    pool.indirect_dma_start(self.total, bass.IndirectOffsetOnAxis(ap=index[:, 0:1], axis=0), y[:], None,
                                            bounds_check=last_row, oob_is_err=False,
                                            compute_op=ALU.add).then_inc(S["scattered"], 16)
                    pool.wait_ge(S["scattered"], 16 * i + 16)
                    pool.sem_inc(S["passed"], 1)
                when_any(pool, body)

            @block.scalar
            def _(act):
                def body(i):
                    for f in range(2):
                        act.wait_ge(S["x_turned"], i + 1)
                        act.copy(flat(xT[:, HALF_KT * f:HALF_KT * (f + 1), :]), self.bank[6 + f]).then_inc(S["xT"], 1)
                    act.wait_ge(S["split"], 8 * i + 8)
                    act.activation(sg[:], gv[:], ACT.Sigmoid, scale=SWIGLU_ALPHA).then_inc(S["sig"], 1)
                    for f in range(2):
                        act.wait_ge(S["a_turned"], i + 1)
                        act.copy(flat(aT[:, HALF_KT * f:HALF_KT * (f + 1), :]), self.bank[6 + f]).then_inc(S["aT"], 1)
                    for f in range(2):
                        act.wait_ge(S["y_full"], i + 1)
                        act.activation(y[:, f * COLS:(f + 1) * COLS], self.bank[4 + f], ACT.Copy,
                                       scale=weight[:, 0:1]).then_inc(S["y_out"], 1)
                when_any(act, body)

            @block.vector
            def _(dve):
                dve.wait_ge(S["in"], 80)

                def body(i):
                    e = expert_of(dve, i)
                    dve.wait_ge(S["scattered"], 16 * i)
                    dve.tensor_tensor(place[:], self.place[:, :, bass.ds(e, 1)].rearrange("p b a -> p (b a)"),
                                      starts[:, bass.ds(i, 1)].to_broadcast([P, NB]), ALU.subtract).then_inc(S["place"], 1)
                    dve.wait_ge(S["place"], i + 1)
                    dve.tensor_tensor(hot[:], slot_no[:].unsqueeze(1).to_broadcast([P, NB, P]),
                                      place[:].unsqueeze(2).to_broadcast([P, NB, P]), ALU.is_equal).then_inc(S["hot"], 1)
                    dve.tensor_copy(pick[:], one[0:E, bass.ds(e, 1)].to_broadcast([E, P])).then_inc(S["picked"], 1)
                    dve.wait_ge(S["listed"], i + 1)
                    dve.tensor_scalar(none[:], self.bank[4][:, 0:1], 0.0, 8.0 * SEQ, ALU.is_equal, ALU.mult).then_inc(S["none"], 1)
                    dve.wait_ge(S["none"], i + 1)
                    dve.scalar_tensor_tensor(out=index[:], in0=none[:], scalar=-1.0, in1=self.bank[4][:, 0:1],
                                             op0=ALU.add, op1=ALU.add).then_inc(S["index"], 1)
                    dve.tensor_copy(weight[:], self.bank[4][:, 1:2]).then_inc(S["index"], 1)
                    dve.wait_ge(S["h_full"], i + 1)
                    for n in range(4):
                        both = self.bank[n].rearrange("p (n a) -> p n a", a=2)
                        at = slice(n * W // 4, (n + 1) * W // 4)
                        dve.tensor_scalar(gv[:, at], both[:, :, 0], SWIGLU_LIMIT, None, ALU.min).then_inc(S["split"], 1)
                        dve.tensor_scalar(uv[:, at], both[:, :, 1], SWIGLU_LIMIT, -SWIGLU_LIMIT, ALU.min,
                                          ALU.max).then_inc(S["split"], 1)
                    dve.wait_ge(S["split"], 8 * i + 8)
                    dve.scalar_tensor_tensor(out=uv[:], in0=uv[:], scalar=1.0, in1=gv[:], op0=ALU.add,
                                             op1=ALU.mult).then_inc(S["p"], 1)
                    dve.wait_ge(S["p"], i + 1)
                    dve.wait_ge(S["sig"], i + 1)
                    dve.tensor_tensor(a[:], uv[:], sg[:], ALU.mult).then_inc(S["act"], 1)
                when_any(dve, body)

            @block.tensor
            def _(pe):
                pe.wait_ge(S["in"], 80)
                pe.sem_inc(S["used"], RING)

                def turn(src, f_done):
                    for f in range(2):
                        for k in range(HALF_KT):
                            last = pe.transpose(self.bank[6 + f][:, k * P:(k + 1) * P],
                                                src[:, (HALF_KT * f + k) * P:(HALF_KT * f + k + 1) * P], self.ident[:])
                    last.then_inc(f_done, 1)

                def body(i):
                    e = expert_of(pe, i)
                    pe.wait_ge(S["hot"], i + 1)
                    pe.wait_ge(S["y_out"], 2 * i)
                    for b in range(NB):
                        last = pe.matmul(self.bank[4][:, 0:2], hot[:, b, :],
                                         self.pairs[:, b, bass.ds(e, 1), :].rearrange("p a n -> p (a n)"),
                                         start=(b == 0), stop=(b == NB - 1))
                    last.then_inc(S["listed"], 1)
                    pe.wait_ge(S["gathered"], 16 * i + 16)
                    turn(rows, S["x_turned"])
                    pe.wait_ge(S["xT"], 2 * i + 2)
                    pe.wait_ge(S["picked"], i + 1)
                    for j in range(N):
                        half, k = divmod(j, self.PER_HALF)
                        banks = [self.bank[2 * half + m] for m in range(2)]
                        if j == 2 * self.PER_HALF:
                            pe.wait_ge(S["act"], i + 1)
                            turn(a, S["a_turned"])
                            pe.wait_ge(S["aT"], 2 * i + 2)
                            pe.wait_ge(S["index"], 2 * i + 2)
                        if k == 0:
                            for m, bank in enumerate(banks):
                                col = half * W + m * COLS
                                pe.matmul(bank, pick[:], bias[:, col:col + COLS], start=True, stop=False)
                        pe.wait_ge(loaded[j % RING], 16 * ((N // RING) * i + j // RING + 1))
                        x = aT if half == 2 else xT
                        for kk in range(2):
                            for m, bank in enumerate(banks):
                                last = pe.matmul(bank, x[:, 2 * k + kk, :], ring[j % RING][:, kk, m * COLS:(m + 1) * COLS],
                                                 start=False, stop=(k == self.PER_HALF - 1 and kk == 1))
                        last.then_inc(S["used"], 1)
                        if j == 2 * self.PER_HALF - 1:
                            pe.wait_ge(S["used"], N * i + j + 1 + RING)
                            pe.sem_inc(S["h_full"], 1)
                    pe.wait_ge(S["used"], N * i + N + RING)
                    pe.sem_inc(S["y_full"], 1)
                when_any(pe, body)

    def normalise_output(self, stack):
        nc, t = self.nc, self.t
        h = self.sb(stack, "total_sb", [P, NB, D_MODEL])
        sq = self.sb(stack, "total_squares", [P, D_MODEL])
        ss = self.sb(stack, "total_sum_squares", [P, NB])
        rs = self.sb(stack, "total_rstd", [P, NB])
        g = self.sb(stack, "norm_final_g_row", [P, D_MODEL])
        half = self.sb(stack, "minus_half3", [P, 1])
        h_in = [self.sem(f"total_in{b}") for b in range(NB)]
        S = {n: self.sem("final_" + n) for n in ("g_in", "sums", "powed", "done", "stored")}
        with nc.Block() as block:
            @block.sync
            def _(sp):
                for b in range(NB):
                    sp.dma_start(h[:, b, :], self.total[b * P:(b + 1) * P, :]).then_inc(h_in[b], 16)
                sp.dma_start(g[:], t["norm_final_g"].unsqueeze(0).partition_broadcast(P).rearrange("p a n -> p (a n)")).then_inc(S["g_in"], 16)
                for b in range(NB):
                    sp.wait_ge(S["done"], b + 1)
                    sp.dma_start(t["out"][0, b * P:(b + 1) * P, :], h[:, b, :]).then_inc(S["stored"], 16)
                sp.wait_ge(S["stored"], 16 * NB)

            @block.gpsimd
            def _(pool):
                link = self.link("pool", pool)
                link(pool.memset(half[:], -0.5))
                for b in range(NB):
                    pool.wait_ge(S["sums"], b + 1)
                    pool.tensor_tensor(rs[:, b:b + 1], ss[:, b:b + 1], half[:], ALU.pow).then_inc(S["powed"], 1)

            @block.vector
            def _(dve):
                link = self.link("dve", dve)
                for b in range(NB):
                    dve.wait_ge(h_in[b], 16)
                    link(dve.scalar_tensor_tensor(out=sq[:], in0=h[:, b, :], scalar=1.0, in1=h[:, b, :], op0=ALU.mult,
                                                  op1=ALU.mult, accum_out=ss[:, b:b + 1]))
                    dve.tensor_scalar(ss[:, b:b + 1], ss[:, b:b + 1], 1.0 / D_MODEL, EPS, ALU.mult,
                                      ALU.add).then_inc(S["sums"], 1)
                dve.wait_ge(S["g_in"], 16)
                for b in range(NB):
                    dve.wait_ge(S["powed"], b + 1)
                    dve.scalar_tensor_tensor(out=h[:, b, :], in0=h[:, b, :], scalar=rs[:, b:b + 1], in1=g[:],
                                             op0=ALU.mult, op1=ALU.mult).then_inc(S["done"], 1)


_OUT = ("out", (1, SEQ, D_MODEL), F32)


def kernel(**inputs):
    import concourse.bacc as bacc
    from concourse.bass_utils import run_bass_kernel_spmd

    nc = bacc.Bacc("TRN2", target_bir_lowering=False, num_devices=1)
    arrays, tensors = {}, {}
    for name, a in list(inputs.items()) + list(CONSTANTS.items()):
        a = np.ascontiguousarray(a)
        arrays[f"in_{name}"] = a
        tensors[name] = nc.dram_tensor(f"in_{name}", a.shape, mybir.dt.from_np(a.dtype), kind="ExternalInput").ap()
    name, shape, dt = _OUT
    tensors[name] = nc.dram_tensor(name, shape, dt, kind="ExternalOutput").ap()
    Kernel(nc, tensors).build()
    results = run_bass_kernel_spmd(nc, [arrays], core_ids=[0])
    return results.results[0][name]
```

```python
import math
from contextlib import ExitStack, contextmanager

import numpy as np

import concourse.bass as bass
from concourse import mybir

F32 = mybir.dt.float32
F32R = mybir.dt.float32r
I32 = mybir.dt.int32
U32 = mybir.dt.uint32
ALU = mybir.AluOpType
ACT = mybir.ActivationFunctionType
AX = mybir.AxisListType

P = 128
SEQ, D_MODEL = 512, 1024
NB = SEQ // P
KT = D_MODEL // P
HALF_KT = KT // 2
COLS = 512

GLA_HEADS, GLA_DK, GLA_DV, GLA_CHUNK, GLA_RANK = 4, 128, 256, 64, 16
GLA_TAU = 16.0
GLA_K_WIDTH, GLA_V_WIDTH = GLA_HEADS * GLA_DK, GLA_HEADS * GLA_DV
N_CHUNKS = SEQ // GLA_CHUNK

ATT_GROUPS = ((128, 1), (512, 4), (2048, 16))
ATT_HEADS, HEAD_DIM, ROT_DIM, ROPE_THETA = 8, 64, 16, 500000.0
RES = 4
ATT_OUT = ATT_HEADS * HEAD_DIM
ATT_QKV = len(ATT_GROUPS) * ATT_OUT
ATT_KEYS = SEQ + P + P
MASKED = -1.0e30

COL_GQ = 0
COL_GK = COL_GQ + GLA_K_WIDTH
COL_GV = COL_GK + GLA_K_WIDTH
COL_GR = COL_GV + GLA_V_WIDTH
COL_GLR = COL_GR + GLA_V_WIDTH
COL_AQ = COL_GLR + GLA_RANK
COL_AV = COL_AQ + 2 * ATT_QKV
COL_GATE = COL_AV + ATT_QKV

N_EXPERTS, TOP_K, FF = 32, 4, D_MODEL
SWIGLU_LIMIT, SWIGLU_ALPHA = 7.0, 1.702
EPS = 1e-5


def shape_constants():
    c = {}
    c["identity"] = np.eye(P, dtype=np.float32)
    half = ROT_DIM // 2
    inv = (np.float32(ROPE_THETA) ** (-np.arange(half, dtype=np.float32) * np.float32(2.0 / ROT_DIM))).astype(np.float32)
    ang = (np.arange(SEQ, dtype=np.float32)[:, None] * inv[None, :]).astype(np.float32)
    cos, sin = np.cos(ang).astype(np.float32), np.sin(ang).astype(np.float32)
    c["rope"] = np.concatenate([cos, cos, -sin, sin], axis=1).astype(np.float32)
    t, r = np.arange(P), np.arange(RES)
    q = (RES * t[None, :] + r[:, None])[:, :, None]
    k0 = np.arange(SEQ)[None, None, :]
    window = ATT_GROUPS[0][0]
    ok0 = (q - k0 >= 0) & (q - k0 <= window)
    lag = np.broadcast_to(t[:, None] - t[None, :], (RES, P, P))
    ok1 = lag >= 0
    ok2 = (lag >= 0) & (lag % (ATT_GROUPS[2][1] // RES) == 0)
    ok = np.concatenate([ok0, ok1, ok2], axis=2)
    c["att_mask"] = np.where(ok, 0.0, MASKED).astype(np.float32)
    i = np.arange(P)
    same = (i[:, None] // GLA_CHUNK) == (i[None, :] // GLA_CHUNK)
    c["gla_mask"] = np.where((i[:, None] <= i[None, :]) & same, np.finfo(np.float32).max, 0).astype(np.float32)
    keep = np.ones((P, GLA_HEADS * SEQ), np.float32)
    keep[:, ::GLA_CHUNK] = 0.0
    c["scan_keep"] = keep
    c["before"] = (i[:, None] < i[None, :]).astype(np.float32)
    c["slot_numbers"] = np.broadcast_to(np.arange(P, dtype=np.float32), (P, P)).copy()
    c["expert_numbers"] = np.broadcast_to(np.arange(N_EXPERTS, dtype=np.float32), (P, N_EXPERTS)).copy()
    c["token_numbers"] = (np.arange(NB)[None, :] * P + i[:, None]).astype(np.float32)
    c["block_starts"] = np.broadcast_to(np.arange(SEQ * TOP_K // P, dtype=np.float32) * P, (P, SEQ * TOP_K // P)).copy()
    e = np.zeros((P, N_EXPERTS), np.float32)
    for x in range(N_EXPERTS):
        e[x, x] = e[N_EXPERTS + x, x] = 1.0
    c["bias_row"] = e
    return c


CONSTANTS = shape_constants()


class Chain:

    def __init__(self, engine, semaphore):
        self.engine, self.semaphore, self.at, self.n = engine, semaphore, 0, 0

    def __call__(self, instruction):
        instruction.then_inc(self.semaphore, 1)
        self.n += 1
        self.engine.wait_ge(self.semaphore, self.at + self.n)

    def enter(self, i, per_iteration):
        self.before = self.at + self.n
        self.at, self.n = self.before + i * per_iteration, 0

    def leave(self, iterations, per_iteration):
        assert self.n == per_iteration, (self.n, per_iteration)
        self.at, self.n = self.before + iterations * per_iteration, 0


class Kernel:
    def __init__(self, nc, t):
        self.nc, self.t, self.groups = nc, t, 0

    def sem(self, name):
        handle = self.nc.alloc_semaphore(name=name)
        if self.stage_sems is not None:
            self.stage_sems.append(handle)
        return handle

    @contextmanager
    def stage(self):
        self.stage_sems = []
        with ExitStack() as stack:
            yield stack
        self.nc.clear_and_free_semaphores(self.stage_sems)
        self.nc.all_engine_barrier()
        self.stage_sems = None

    def sb(self, stack, name, shape, dt=F32):
        return stack.enter_context(self.nc.sbuf_tensor(name, shape, dt))

    def build(self):
        nc = self.nc
        with ExitStack() as top:
            self.stage_sems = None
            self.psum = top.enter_context(nc.psum_tensor("psum", [P, 8, COLS], F32))
            self.bank = [self.psum[:, i, :] for i in range(8)]
            self.chain_sem = {e: self.sem(f"chain_{e}") for e in ("pe", "act", "dve", "pool", "sp")}
            self.chain = {}
            self.loaded = [self.sem(f"chunk_loaded{c}") for c in range(2)]
            self.hi_done = [self.sem(f"chunk_hi_done{c}") for c in range(2)]
            self.lo_done = [self.sem(f"chunk_lo_done{c}") for c in range(2)]
            self.chunk_used = self.sem("chunk0_used")
            self.bank_full = [self.sem(f"bank_full{b}") for b in range(NB)]
            self.bank_free = [self.sem(f"bank_free{b}") for b in range(NB)]
            self.ident = self.sb(top, "identity_sb", [P, P])
            self.rank = self.sb(top, "rank_in_expert", [P, NB, N_EXPERTS])
            self.pairs = self.sb(top, "token_and_weight", [P, NB, N_EXPERTS, 2])
            self.place = self.sb(top, "place_in_further", [P, NB, N_EXPERTS])
            self.block_expert = self.sb(top, "further_block_expert", [P, self.FURTHER], I32)
            self.n_further = self.sb(top, "further_blocks", [P, 1], I32)
            self.normed = nc.dram_tensor("normed_rows", [SEQ, D_MODEL], F32).ap()
            self.total = nc.dram_tensor("residual_rows", [SEQ, D_MODEL], F32).ap()
            self.h = self.sb(top, "h_sb", [P, NB, D_MODEL])
            self.h_sums = self.sb(top, "h_sum_squares", [P, NB])
            self.counts = self.sb(top, "tokens_of_expert", [P, N_EXPERTS])
            with ExitStack() as mixer:
                self.mixer(mixer)
            with ExitStack() as moe:
                self.first_expert = [self.sem(f"expert_chunk_loaded{j}") for j in range(self.CHUNKS)]
                self.expert_ring = [self.sb(moe, f"expert_chunk{j}", [P, 2, self.WIDE]) for j in range(self.CHUNKS)]
                self.bias = self.sb(moe, "bias_hi_lo", [P, 3 * self.WIDE], F32R)
                self.slot_no = self.sb(moe, "slot_numbers_sb", [P, P])
                self.bias_row = self.sb(moe, "bias_row_sb", [P, N_EXPERTS])
                with self.stage() as s:
                    self.route(s)
                with self.stage() as s:
                    self.experts(s)
            with self.stage() as s:
                self.further_blocks(s)
            with self.stage() as s:
                self.normalise_output(s)

    def link(self, name, engine):
        c = self.chain.setdefault(name, Chain(engine, self.chain_sem[name]))
        c.engine = engine
        return c

    def mixer(self, stack):
        self.x_hi = self.sb(stack, "xT_hi", [P, KT, SEQ], F32R)
        self.x_lo = self.sb(stack, "xT_lo", [P, KT, SEQ], F32R)
        self.ring(stack)
        with self.stage() as s:
            self.normalise_input(s)
        self.yg = self.sb(stack, "y_glaT", [P, KT, SEQ])
        with ExitStack() as s:
            self.gla(s)
        self.ya = self.h[:, 0:NB // 2, :].rearrange("p b n -> p (b n)").rearrange("p (k n) -> p k n", n=SEQ)
        with ExitStack() as s:
            self.attention(s)
        with ExitStack() as s:
            self.merge(s)

    def normalise_input(self, stack):
        nc, t = self.nc, self.t
        x = self.sb(stack, "x_sb", [P, NB, D_MODEL])
        sq = self.sb(stack, "x_squares", [P, 2, D_MODEL])
        ss = self.sb(stack, "x_sum_squares", [P, NB])
        rs = self.sb(stack, "x_rstd", [P, NB])
        g = self.sb(stack, "norm_mix_g_row", [P, D_MODEL])
        minus_half = self.sb(stack, "minus_half0", [P, 1])
        x_in = [self.sem(f"x_in{b}") for b in range(NB)]
        ident_in, g_in, squared, mean_done, powed = (self.sem(n) for n in (
            "identity_in", "norm_mix_g_in", "x_squared", "x_mean_done", "x_powed"))
        scaled, turned, xh_done, xl_done = (self.sem(n) for n in ("x_scaled", "x_turned", "xh_done", "xl_done"))
        bank_of = lambda i: self.bank[i % NB].rearrange("p (k n) -> p k n", n=P)

        def part_of(x_part, i):
            b, h = divmod(i, 2)
            return x_part[:, HALF_KT * h:HALF_KT * (h + 1), b * P:(b + 1) * P]

        with nc.Block() as block:
            @block.sync
            def _(sp):
                for b in range(NB):
                    sp.dma_start(x[:, b, :], t["x"][0, b * P:(b + 1) * P, :]).then_inc(x_in[b], 16)
                    if b == 0:
                        sp.dma_start(g[:], t["norm_mix_g"][0:1, :].partition_broadcast(P).rearrange("p a n -> p (a n)")).then_inc(g_in, 16)
                        sp.dma_start(self.ident[:], t["identity"]).then_inc(ident_in, 16)
                self.load_group(sp, self.groups, self.w_in_chunk(COL_GQ))

            @block.gpsimd
            def _(pool):
                link = self.link("pool", pool)
                link(pool.memset(minus_half[:], -0.5))
                for b in range(NB):
                    pool.wait_ge(mean_done, b + 1)
                    pool.tensor_tensor(rs[:, b:b + 1], ss[:, b:b + 1], minus_half[:], ALU.pow).then_inc(powed, 1)

            @block.vector
            def _(dve):
                def mean(b):
                    dve.wait_ge(squared, b + 1)
                    dve.tensor_scalar(ss[:, b:b + 1], ss[:, b:b + 1], 1.0 / D_MODEL, EPS, ALU.mult,
                                      ALU.add).then_inc(mean_done, 1)

                def lo(i):
                    dve.wait_ge(xh_done, i + 1)
                    dve.tensor_tensor(part_of(self.x_lo, i), bank_of(i), part_of(self.x_hi, i).bitcast(F32),
                                      ALU.subtract).then_inc(xl_done, 1)

                mean(0)
                dve.wait_ge(g_in, 16)
                for b in range(NB):
                    if b + 1 < NB:
                        mean(b + 1)
                    dve.wait_ge(powed, b + 1)
                    dve.scalar_tensor_tensor(out=x[:, b, :], in0=x[:, b, :], scalar=rs[:, b:b + 1], in1=g[:],
                                             op0=ALU.mult, op1=ALU.mult).then_inc(scaled, 1)
                    if b:
                        lo(2 * b - 2)
                        lo(2 * b - 1)
                lo(2 * NB - 2)
                lo(2 * NB - 1)
                for c in range(2):
                    self.split_lo(dve, self.groups, c)

            @block.scalar
            def _(act):
                def square(b):
                    act.wait_ge(x_in[b], 16)
                    if b >= 2:
                        act.wait_ge(squared, b - 1)
                    act.activation(sq[:, b % 2, :], x[:, b, :], ACT.Square, accum_out=ss[:, b:b + 1]).then_inc(squared, 1)

                square(0)
                square(1)
                for b in range(NB):
                    if b + 2 < NB:
                        square(b + 2)
                    for i in (2 * b, 2 * b + 1):
                        act.wait_ge(turned, i + 1)
                        act.copy(part_of(self.x_hi, i), bank_of(i)).then_inc(xh_done, 1)
                for c in range(2):
                    self.split_hi(act, self.groups, c)

            @block.tensor
            def _(pe):
                pe.wait_ge(ident_in, 16)
                for i in range(2 * NB):
                    b, h = divmod(i, 2)
                    pe.wait_ge(scaled, b + 1)
                    if i >= NB:
                        pe.wait_ge(xl_done, i - NB + 1)
                    for k in range(HALF_KT):
                        last = pe.transpose(self.bank[i % NB][:, k * P:(k + 1) * P],
                                            x[:, b, (HALF_KT * h + k) * P:(HALF_KT * h + k + 1) * P], self.ident[:])
                    last.then_inc(turned, 1)

    def ring(self, stack):
        self.raw = [self.sb(stack, f"chunk{c}", [P, HALF_KT, COLS]) for c in range(2)]
        self.whi = [self.sb(stack, f"chunk_hi{c}", [P, HALF_KT, COLS], F32R) for c in range(2)]
        self.wlo = [self.sb(stack, f"chunk_lo{c}", [P, HALF_KT, COLS], F32R) for c in range(2)]

    def load_group(self, sp, g, source):
        for c in range(2):
            sp.wait_ge(self.lo_done[c], g)
            sp.dma_start(self.raw[c][:], source(c)).then_inc(self.loaded[c], 16)

    def split_hi(self, act, g, c):
        act.wait_ge(self.loaded[c], g * 16 + 16)
        act.wait_ge(self.bank_full[NB - 1] if c else self.chunk_used, g)
        act.copy(self.whi[c][:], self.raw[c][:]).then_inc(self.hi_done[c], 1)

    def split_lo(self, dve, g, c):
        dve.wait_ge(self.hi_done[c], g + 1)
        dve.tensor_tensor(self.wlo[c][:], self.raw[c][:], self.whi[c][:].bitcast(F32),
                          ALU.subtract).then_inc(self.lo_done[c], 1)

    def multiply_group(self, pe, g, tokens, weights_stay=False, lhs=None, between=None, ready=None):
        x_hi, x_lo = lhs or (self.x_hi, self.x_lo)
        for c in range(2):
            pe.wait_ge(self.lo_done[c], g + 1)
            if ready:
                ready(c)
            for b in range(NB):
                if c == 0:
                    pe.wait_ge(self.bank_free[b], g)
                for kk in range(HALF_KT):
                    k = HALF_KT * c + kk
                    hi, lo = self.whi[c], self.wlo[c]
                    if weights_stay:
                        col = slice(b * P, (b + 1) * P)
                        passes = ((hi[:, kk, col], x_hi[:, k, :]), (hi[:, kk, col], x_lo[:, k, :]),
                                  (lo[:, kk, col], x_hi[:, k, :]))
                    else:
                        tok = tokens(b)
                        passes = ((x_hi[:, k, tok], hi[:, kk, :]), (x_hi[:, k, tok], lo[:, kk, :]),
                                  (x_lo[:, k, tok], hi[:, kk, :]))
                    for n, (stationary, moving) in enumerate(passes):
                        last = pe.matmul(self.bank[b], stationary, moving, start=(k == 0 and n == 0),
                                         stop=(k == KT - 1 and n == 2))
                if c == 1:
                    last.then_inc(self.bank_full[b], 1)
            if c == 0:
                last.then_inc(self.chunk_used, 1)
                if between:
                    between()

    def w_in_chunk(self, col):
        def source(c):
            return self.t["w_in"][0, c * HALF_KT * P:(c + 1) * HALF_KT * P, bass.ds(col, COLS)].rearrange(
                "(k p) n -> p k n", p=P)
        return source

    @staticmethod
    def block_of(b):
        return slice(b * P, (b + 1) * P)

    @staticmethod
    def residue(b):
        return slice(b, SEQ, RES)

    def run_groups(self, kind, engine, base, n, source=None, tokens=None, weights_stay=False, lhs=None,
                   evacuate=None, next_split=False):
        def step(i, last):
            g = base + i
            if kind == "load":
                self.load_group(engine, g, lambda c: source(i)(c))
            elif kind == "multiply":
                self.multiply_group(engine, g, tokens, weights_stay, lhs)
            else:
                split = self.split_hi if kind == "hi" else self.split_lo
                more = next_split or not last
                if more:
                    split(engine, g + 1, 0)
                if evacuate:
                    for b in range(NB):
                        engine.wait_ge(self.bank_full[b], g + 1)
                        evacuate(i, b).then_inc(self.bank_free[b], 1)
                if more:
                    split(engine, g + 1, 1)

        if kind in ("load", "multiply"):
            with engine.Fori(0, n) as i:
                step(i, False)
        else:
            if n > 1:
                with engine.Fori(0, n - 1) as i:
                    step(i, False)
            step(n - 1, True)

    def gla(self, stack):
        nc, t = self.nc, self.t
        H, L = GLA_HEADS, SEQ
        qk = self.sb(stack, "gla_qkT", [P, 2, H, L])
        v = self.sb(stack, "gla_v", [P, NB, GLA_V_WIDTH])
        sg = self.sb(stack, "gla_silu_r", [P, NB, GLA_V_WIDTH])
        b_sum = self.sb(stack, "decay_sums", [P, H, L])
        with self.stage() as s:
            self.gla_project(s, qk, v, sg, b_sum)
        with self.stage() as s:
            self.gla_heads(s, qk, v, sg, b_sum)

    def gla_project(self, stack, qk, v, sg, b_sum):
        nc, t = self.nc, self.t
        H, L = GLA_HEADS, SEQ
        base = self.groups
        z = self.sb(stack, "decay_z", [P, H, L])
        soft = sg[:, 0:NB // 2, :].rearrange("p b n -> p (b n)").rearrange("p (h n) -> p h n", n=L)
        keep = self.sb(stack, "scan_keep_sb", [P, H * L])
        w_lr = self.sb(stack, "w_lr", [P, KT, P])
        w_lr_hi = self.sb(stack, "w_lr_hi", [P, KT, P], F32R)
        w_lr_lo = self.sb(stack, "w_lr_lo", [P, KT, P], F32R)
        lrT = self.sb(stack, "lrT", [GLA_RANK, L])
        up = self.sb(stack, "gate_up_sb", [GLA_RANK, GLA_K_WIDTH])
        bias = self.sb(stack, "gate_bias_col", [P, H])
        g_row = self.sb(stack, "gla_norm_g_row", [P, GLA_DV])
        small_in, lr_in = self.sem("gla_small_in"), self.sem("w_lr_in")
        lr_hi, lr_lo, lr_full, lr_out = (self.sem(n) for n in ("lr_hi_done", "lr_lo_done", "lr_full", "lr_out"))
        z_full, z_out, soft_done, silu_done = (self.sem(n) for n in ("z_full", "z_out", "soft_done", "silu_done"))
        GROUPS_QK, GROUPS_V, GROUPS_R = 2 * GLA_K_WIDTH // COLS, GLA_V_WIDTH // COLS, GLA_V_WIDTH // COLS
        base_r, base_v = base + GROUPS_QK, base + GROUPS_QK + GROUPS_R
        self.groups = base_v + GROUPS_V

        with nc.Block() as block:
            @block.sync
            def _(sp):
                sp.dma_start(w_lr[:], t["w_in"][0, :, COL_GLR:COL_GLR + P].rearrange("(k p) n -> p k n", p=P)
                             ).then_inc(lr_in, 16)
                sp.dma_start(up[:], t["gla_gate_up"][0]).then_inc(small_in, 16)
                sp.dma_start(bias[:], t["gla_gate_bias"][0].rearrange("(h p) -> p h", p=P),
                             allow_slow_non_contiguous=True).then_inc(small_in, 16)
                sp.dma_start(keep[:], t["scan_keep"]).then_inc(small_in, 16)
                sp.dma_start(g_row[:], t["gla_norm_g"][0:1, :].partition_broadcast(P).rearrange("p a n -> p (a n)")).then_inc(small_in, 16)
                self.load_group(sp, base + 1, self.w_in_chunk(COL_GK))
                for first, col, n in ((base_r, COL_GR, GROUPS_R), (base_v, COL_GV, GROUPS_V)):
                    with sp.Fori(0, n) as i:
                        self.load_group(sp, first + i, lambda c: self.w_in_chunk(col + COLS * i)(c))

            @block.tensor
            def _(pe):
                pe.wait_ge(lr_lo, 1)
                for k in range(KT):
                    for n, (w, x) in enumerate(((w_lr_hi, self.x_hi), (w_lr_hi, self.x_lo), (w_lr_lo, self.x_hi))):
                        last = pe.matmul(self.bank[4], w[:, k, :], x[:, k, :], start=(k == 0 and n == 0),
                                         stop=(k == KT - 1 and n == 2))
                last.then_inc(lr_full, 1)
                pe.wait_ge(small_in, 64)
                pe.wait_ge(lr_out, 1)
                for h in range(H):
                    pe.matmul(self.bank[4 + h], up[:, h * P:(h + 1) * P], lrT[:],
                              start=True, stop=True).then_inc(z_full, 1)
                self.run_groups("multiply", pe, base, GROUPS_QK, weights_stay=True)
                self.run_groups("multiply", pe, base_r, GROUPS_R + GROUPS_V, tokens=self.block_of)

            @block.scalar
            def _(act):
                link = self.link("act", act)
                act.wait_ge(lr_in, 16)
                act.copy(w_lr_hi[:], w_lr[:]).then_inc(lr_hi, 1)
                act.wait_ge(lr_full, 1)
                act.copy(lrT[:], self.bank[4][0:GLA_RANK, :]).then_inc(lr_out, 1)
                act.wait_ge(z_out, H)
                link(act.activation(soft, z[:], ACT.Abs))
                link(act.activation(soft, soft, ACT.Exp, scale=-1.0))
                act.activation(soft, soft, ACT.Ln, bias=1.0).then_inc(soft_done, 1)
                self.run_groups("hi", act, base, GROUPS_QK, next_split=True,
                                evacuate=lambda i, b: act.copy(qk[:, i, b, :] if isinstance(i, int) else
                                                               qk[:, bass.ds(i, 1), b, :].rearrange("p a n -> p (a n)"),
                                                               self.bank[b]))
                self.run_groups("hi", act, base_r, GROUPS_R, next_split=True,
                                evacuate=lambda i, b: act.activation(sg[:, b, bass.ds(i * COLS, COLS)],
                                                                     self.bank[b], ACT.Silu))
                self.run_groups("hi", act, base_v, GROUPS_V,
                                evacuate=lambda i, b: act.copy(v[:, b, bass.ds(i * COLS, COLS)], self.bank[b]))

            @block.vector
            def _(dve):
                link = self.link("dve", dve)
                dve.wait_ge(lr_hi, 1)
                dve.tensor_tensor(w_lr_lo[:], w_lr[:], w_lr_hi[:].bitcast(F32), ALU.subtract).then_inc(lr_lo, 1)
                dve.wait_ge(small_in, 64)
                for h in range(H):
                    dve.wait_ge(z_full, h + 1)
                    dve.tensor_scalar(z[:, h, :], self.bank[4 + h], bias[:, h:h + 1], None,
                                      ALU.add).then_inc(z_out, 1)
                self.split_lo(dve, base + 1, 0)
                self.split_lo(dve, base + 1, 1)
                dve.wait_ge(soft_done, 1)
                link(dve.scalar_tensor_tensor(out=z[:], in0=z[:], scalar=0.0, in1=soft, op0=ALU.min,
                                              op1=ALU.subtract))
                link(dve.tensor_tensor_scan(b_sum[:].rearrange("p h n -> p (h n)"), keep[:],
                                            z[:].rearrange("p h n -> p (h n)"), 0.0, ALU.mult, ALU.add))
                for g in range(base_r, base_v):
                    for c in range(2):
                        self.split_lo(dve, g, c)
                for i in range(GROUPS_R):
                    for c in range(2):
                        self.split_lo(dve, base_v + i, c)
                    for b in range(NB):
                        dve.wait_ge(self.bank_free[b], base_r + i + 1)
                        r = sg[:, b, i * COLS:(i + 1) * COLS].rearrange("p (h n) -> p h n", n=GLA_DV)
                        link(dve.tensor_tensor(r, r, g_row[:].unsqueeze(1).to_broadcast([P, COLS // GLA_DV, GLA_DV]), ALU.mult))

    def gla_heads(self, stack, qk, v, sg, b_sum):
        nc, t = self.nc, self.t
        H, L, C = GLA_HEADS, SEQ, GLA_CHUNK
        grow = self.sb(stack, "exp_b", [P, 2, L])
        ke = self.sb(stack, "k_decayed", [P, 2, L])
        kdT = self.sb(stack, "k_to_chunk_endT", [P, 2, L])
        qe = self.sb(stack, "q_decayed", [P, 2, L])
        at = self.sb(stack, "products_masked", [P, 2, NB, P])
        kd = self.sb(stack, "k_to_chunk_end", [P, NB, P])
        mask = self.sb(stack, "gla_mask_sb", [P, P])
        anti = self.sb(stack, "gla_mask_negated", [P, P])
        state = self.sb(stack, "gla_state", [P, N_CHUNKS, GLA_DV])
        sq = self.sb(stack, "gla_squares", [P, GLA_DV])
        ss = self.sb(stack, "gla_sum_squares", [P, H, NB])
        rs = self.sb(stack, "gla_rstd", [P, H, NB])
        y = self.sb(stack, "gla_y", [P, NB, GLA_DV])
        minus_half = self.sb(stack, "minus_half1", [P, 1])
        S = {n: self.sem("gla_" + n) for n in (
            "mask_in", "state_zeroed", "clamped", "half_set", "exps", "to_end", "decayed", "kd_turned", "kd_out", "products",
            "masked", "updates", "state_done", "o_full", "squared", "mean_done", "powed", "y_done", "y_turned",
            "y_out")}
        flat = lambda ap: ap.rearrange("p a n -> p (a n)")
        u_bank = lambda c: self.bank[c % 4][:, (c // 4) * GLA_DV:(c // 4 + 1) * GLA_DV]
        o_bank = lambda n: self.bank[6 + n // 2][:, (n % 2) * GLA_DV:(n % 2 + 1) * GLA_DV]
        chunk = lambda c: slice(c * C, (c + 1) * C)
        by_chunk = lambda ap: ap.rearrange("p (c n) -> p c n", n=C)
        UPDATES = N_CHUNKS - 1

        with nc.Block() as block:
            @block.sync
            def _(sp):
                sp.dma_start(mask[:], t["gla_mask"]).then_inc(S["mask_in"], 16)
                self.load_group(sp, self.groups, self.w_in_chunk(COL_AQ))

            @block.gpsimd
            def _(pool):
                pool.memset(state[:, 0, :], 0.0).then_inc(S["state_zeroed"], 1)
                pool.memset(minus_half[:], -0.5).then_inc(S["half_set"], 1)
                pool.wait_ge(S["half_set"], 1)
                for h in range(H):
                    pool.wait_ge(S["mean_done"], h + 1)
                    pool.tensor_tensor(rs[:, h, :], ss[:, h, :], minus_half[:, 0:1].to_broadcast([P, NB]),
                                       ALU.pow).then_inc(S["powed"], 1)

            @block.scalar
            def _(act):
                def exps(h):
                    u = h % 2
                    if h >= 2:
                        act.wait_ge(S["state_done"], (h - 1) * UPDATES)
                        act.wait_ge(S["products"], h - 1)
                        act.wait_ge(S["kd_turned"], h - 1)
                    act.activation(grow[:, u], b_sum[:, h, :], ACT.Exp, scale=1.0 / GLA_TAU).then_inc(S["exps"], 1)
                    act.activation(ke[:, u], b_sum[:, h, :], ACT.Exp, scale=-1.0 / GLA_TAU).then_inc(S["exps"], 1)
                    act.wait_ge(S["to_end"], h + 1)
                    act.activation(kdT[:, u], kdT[:, u], ACT.Exp, scale=1.0 / GLA_TAU).then_inc(S["exps"], 1)

                def kd_out(h):
                    act.wait_ge(S["kd_turned"], h + 1)
                    if h:
                        act.wait_ge(S["updates"], h)
                    act.copy(flat(kd[:]), self.bank[4]).then_inc(S["kd_out"], 1)

                def squares(h):
                    for n in range(NB):
                        act.wait_ge(S["o_full"], 2 * h + n // 2 + 1)
                        if h or n:
                            act.wait_ge(S["squared"], NB * h + n)
                        act.activation(sq[:], o_bank(n), ACT.Square, accum_out=ss[:, h, n:n + 1]).then_inc(S["squared"], 1)

                def y_out(h):
                    for d in range(2):
                        act.wait_ge(S["y_turned"], 2 * h + d + 1)
                        act.copy(self.yg[:, 2 * h + d, :], self.bank[6 + d]).then_inc(S["y_out"], 1)

                exps(0)
                kd_out(0)
                exps(1)
                for h in range(H):
                    if h:
                        squares(h - 1)
                        y_out(h - 1)
                    if h + 1 < H:
                        kd_out(h + 1)
                    if h + 2 < H:
                        exps(h + 2)
                    if h >= 2:
                        self.split_hi(act, self.groups, h - 2)
                squares(H - 1)
                y_out(H - 1)

            @block.vector
            def _(dve):
                link = self.link("dve", dve)
                dve.wait_ge(S["mask_in"], 16)
                link(dve.tensor_scalar(anti[:], mask[:], -1.0, None, ALU.mult))
                over = lambda m: m[:].unsqueeze(1).to_broadcast([P, NB, P])

                def to_end(h):
                    u = h % 2
                    b_c = by_chunk(b_sum[:, h, :])
                    if h >= 2:
                        dve.wait_ge(S["kd_turned"], h - 1)
                    dve.tensor_tensor(by_chunk(kdT[:, u]), b_c[:, :, C - 1:C].to_broadcast([P, N_CHUNKS, C]), b_c,
                                      ALU.subtract).then_inc(S["to_end"], 1)

                def decays(h):
                    u = h % 2
                    dve.wait_ge(S["exps"], 3 * h + 1)
                    if h >= 2:
                        dve.wait_ge(S["o_full"], 2 * (h - 1))
                    dve.scalar_tensor_tensor(out=qe[:, u], in0=qk[:, 0, h, :], scalar=float(GLA_DK) ** -0.5, in1=grow[:, u],
                                             op0=ALU.mult, op1=ALU.mult).then_inc(S["decayed"], 1)
                    dve.wait_ge(S["exps"], 3 * h + 2)
                    dve.tensor_tensor(ke[:, u], qk[:, 1, h, :], ke[:, u], ALU.mult).then_inc(S["decayed"], 1)
                    dve.wait_ge(S["exps"], 3 * h + 3)
                    dve.tensor_tensor(kdT[:, u], qk[:, 1, h, :], kdT[:, u], ALU.mult).then_inc(S["decayed"], 1)

                def mask_products(h):
                    u = h % 2
                    dve.wait_ge(S["products"], h + 1)
                    if h >= 2:
                        dve.wait_ge(S["o_full"], 2 * (h - 1))
                    dve.tensor_tensor(at[:, u], self.bank[5].rearrange("p (a n) -> p a n", n=P), over(mask),
                                      ALU.min).then_inc(S["clamped"], 1)
                    dve.wait_ge(S["clamped"], h + 1)
                    dve.tensor_tensor(at[:, u], at[:, u], over(anti), ALU.max).then_inc(S["masked"], 1)

                def states(h):
                    if h:
                        dve.wait_ge(S["o_full"], 2 * h)
                    dve.wait_ge(S["updates"], h + 1)
                    for c in range(UPDATES):
                        if h or c:
                            dve.wait_ge(S["state_done"], h * UPDATES + c)
                        if c == 0:
                            dve.tensor_copy(state[:, 1, :], u_bank(0)).then_inc(S["state_done"], 1)
                        else:
                            dve.scalar_tensor_tensor(out=state[:, c + 1, :], in0=state[:, c, :],
                                                     scalar=grow[:, h % 2, c * C + C - 1:c * C + C], in1=u_bank(c),
                                                     op0=ALU.mult, op1=ALU.add).then_inc(S["state_done"], 1)

                def norms(h):
                    dve.wait_ge(S["squared"], NB * h + NB)
                    dve.tensor_scalar(ss[:, h, :], ss[:, h, :], 1.0 / GLA_DV, EPS, ALU.mult, ALU.add).then_inc(S["mean_done"], 1)
                    dve.wait_ge(S["powed"], h + 1)
                    if h:
                        dve.wait_ge(S["y_turned"], 2 * h)
                    for n in range(NB):
                        dve.scalar_tensor_tensor(out=y[:, n, :], in0=o_bank(n), scalar=rs[:, h, n:n + 1],
                                                 in1=sg[:, n, h * GLA_DV:(h + 1) * GLA_DV],
                                                 op0=ALU.mult, op1=ALU.mult).then_inc(S["y_done"], 1)

                to_end(0)
                to_end(1)
                decays(0)
                mask_products(0)
                for h in range(H):
                    if h + 1 < H:
                        decays(h + 1)
                    if h:
                        norms(h - 1)
                    states(h)
                    if h + 2 < H:
                        to_end(h + 2)
                    if h + 1 < H:
                        mask_products(h + 1)
                    if h >= 2:
                        self.split_lo(dve, self.groups, h - 2)
                norms(H - 1)

            @block.tensor
            def _(pe):
                def products(h):
                    u = h % 2
                    pe.wait_ge(S["decayed"], 3 * h + 3)
                    if h:
                        pe.wait_ge(S["kd_out"], h)
                        pe.wait_ge(S["clamped"], h)
                    for n in range(NB):
                        last = pe.transpose(self.bank[4][:, n * P:(n + 1) * P], kdT[:, u, n * P:(n + 1) * P], self.ident[:])
                    last.then_inc(S["kd_turned"], 1)
                    for n in range(NB):
                        blk = self.block_of(n)
                        last = pe.matmul(self.bank[5][:, blk], ke[:, u, blk], qe[:, u, blk], start=True, stop=True)
                    last.then_inc(S["products"], 1)

                def updates(h):
                    pe.wait_ge(S["kd_out"], h + 1)
                    if h:
                        pe.wait_ge(S["state_done"], h * UPDATES)
                    for c in range(UPDATES):
                        half = slice((c % 2) * C, (c % 2 + 1) * C)
                        last = pe.matmul(u_bank(c), kd[half, c // 2, :], v[half, c // 2, h * GLA_DV:(h + 1) * GLA_DV],
                                         start=True, stop=True)
                    last.then_inc(S["updates"], 1)

                def turn_y(h):
                    for d in range(2):
                        for n in range(NB):
                            pe.wait_ge(S["y_done"], NB * (h + 1))
                            last = pe.transpose(self.bank[6 + d][:, n * P:(n + 1) * P],
                                                y[:, n, d * P:(d + 1) * P], self.ident[:])
                        last.then_inc(S["y_turned"], 1)

                def results(h):
                    pe.wait_ge(S["masked"], h + 1)
                    if h:
                        pe.wait_ge(S["y_out"], 2 * h)
                    for n in range(NB):
                        pe.matmul(o_bank(n), at[:, h % 2, n, :], v[:, n, h * GLA_DV:(h + 1) * GLA_DV], start=True, stop=False)
                        for c in (2 * n, 2 * n + 1):
                            if c:
                                pe.wait_ge(S["state_done"], h * UPDATES + c)
                            last = pe.matmul(o_bank(n)[(c % 2) * C:(c % 2 + 1) * C, :], qe[:, h % 2, chunk(c)],
                                             state[:, c, :], start=False, stop=True)
                        if n % 2:
                            last.then_inc(S["o_full"], 1)

                pe.wait_ge(S["state_zeroed"], 1)
                products(0)
                for h in range(H):
                    updates(h)
                    if h:
                        turn_y(h - 1)
                    if h + 1 < H:
                        products(h + 1)
                    results(h)
                turn_y(H - 1)

    def attention(self, stack):
        G = len(ATT_GROUPS)
        q = self.sb(stack, "att_qT", [P, G * HALF_KT, SEQ])
        k = self.sb(stack, "att_kT", [P, G * HALF_KT, SEQ])
        v = self.sb(stack, "att_v", [P, G, NB, ATT_OUT])
        mask = self.sb(stack, "att_mask_sb", [P, 2, ATT_KEYS])
        with self.stage() as s:
            self.att_project(s, q, k, v, mask)
        with self.stage() as s:
            self.att_heads(s, q, k, v, mask)

    def att_project(self, stack, q, k, v, mask):
        nc, t = self.nc, self.t
        G, HALF = len(ATT_GROUPS), ROT_DIM // 2
        base, base_v = self.groups, self.groups + 2 * G
        self.groups = base_v + G
        row = self.sb(stack, "qk_rows", [P, NB, COLS])
        turn = self.sb(stack, "rope_products", [P, 2, ATT_HEADS, ROT_DIM])
        rope = self.sb(stack, "rope_sb", [P, NB, 2 * ROT_DIM])
        rope_in, rotated, turned, stored, masks_in = (self.sem("att_" + n) for n in (
            "rope_in", "rotated", "turned", "stored", "masks_in"))
        prod = self.sem("att_rope_products")

        with nc.Block() as block:
            @block.sync
            def _(sp):
                sp.dma_start(rope[:], t["rope"].rearrange("(b p) n -> p b n", p=P)).then_inc(rope_in, 16)
                with sp.Fori(1, 3 * G) as i:
                    self.load_group(sp, base + i, lambda c: self.w_in_chunk(COL_AQ + COLS * i)(c))
                for r in range(2):
                    sp.dma_start(mask[:, r, :], t["att_mask"][r]).then_inc(masks_in, 16)
                sp.wait_ge(masks_in, 32)

            @block.tensor
            def _(pe):
                def turn_rows(i):
                    for b in range(NB):
                        pe.wait_ge(rotated, NB * i + b + 1)
                        pe.wait_ge(stored, NB * i)
                        for d in range(HALF_KT):
                            last = pe.transpose(self.bank[4 + b][:, d * P:(d + 1) * P],
                                                row[:, b, d * P:(d + 1) * P], self.ident[:])
                        last.then_inc(turned, 1)

                def qk_group(i, before=None):
                    self.multiply_group(pe, base + i, self.block_of, between=before)

                qk_group(0)
                with pe.Fori(1, 2 * G) as i:
                    qk_group(i, lambda: turn_rows(i - 1))
                self.multiply_group(pe, base_v, self.block_of, between=lambda: turn_rows(2 * G - 1))
                self.run_groups("multiply", pe, base_v + 1, G - 1, tokens=self.residue)

            @block.scalar
            def _(act):
                def rows_out(i, b):
                    act.wait_ge(turned, NB * i)
                    return act.copy(row[:, b, :], self.bank[b])

                self.run_groups("hi", act, base, 2 * G, next_split=True, evacuate=rows_out)
                self.run_groups("hi", act, base_v, G,
                                evacuate=lambda i, b: act.copy(v[:, i, b, :] if isinstance(i, int) else
                                                               v[:, bass.ds(i, 1), b, :].rearrange("p a n -> p (a n)"),
                                                               self.bank[b]))

            @block.vector
            def _(dve):
                dve.wait_ge(rope_in, 16)

                def rotate(i, qk, at):
                    for b in range(NB):
                        heads = row[:, b, :].rearrange("p (h n) -> p h n", n=HEAD_DIM)
                        table = lambda a, n: rope[:, b, a:a + n].unsqueeze(1).to_broadcast([P, ATT_HEADS, n])
                        dve.wait_ge(self.bank_free[b], base + i + 1)
                        dve.wait_ge(rotated, NB * i + b)
                        dve.tensor_tensor(turn[:, 0], heads[:, :, 0:ROT_DIM], table(0, ROT_DIM), ALU.mult).then_inc(prod, 1)
                        dve.tensor_tensor(turn[:, 1, :, 0:HALF], heads[:, :, HALF:ROT_DIM], table(ROT_DIM, HALF),
                                          ALU.mult).then_inc(prod, 1)
                        dve.tensor_tensor(turn[:, 1, :, HALF:], heads[:, :, 0:HALF], table(ROT_DIM + HALF, HALF),
                                          ALU.mult).then_inc(prod, 1)
                        dve.wait_ge(prod, 3 * (NB * i + b + 1))
                        dve.tensor_tensor(heads[:, :, 0:ROT_DIM], turn[:, 0], turn[:, 1], ALU.add).then_inc(rotated, 1)
                    for b in range(NB):
                        dve.wait_ge(turned, NB * i + b + 1)
                        dve.tensor_copy(qk[:, bass.ds(at * HALF_KT, HALF_KT), b * P:(b + 1) * P],
                                        self.bank[4 + b].rearrange("p (d n) -> p d n", n=P)).then_inc(stored, 1)

                for first, qk in ((0, q), (G, k)):
                    with dve.Fori(0, G) as i:
                        for c in range(2):
                            self.split_lo(dve, base + first + i + 1, c)
                        rotate(first + i, qk, i)
                with dve.Fori(2 * G + 1, 3 * G) as i:
                    for c in range(2):
                        self.split_lo(dve, base + i, c)

    def att_heads(self, stack, q, k, v, mask):
        nc, t = self.nc, self.t
        HEADS, TILES = ATT_HEADS, ATT_KEYS // P
        STEPS = RES * HEADS
        SPLIT_AT = (STEPS // 2, STEPS // 2 + 4)
        neg = self.sb(stack, "att_negated", [P, 2, ATT_KEYS])
        pT = self.sb(stack, "att_probsT", [P, 2, TILES, P])
        low = self.sb(stack, "att_minus_max", [P, 2])
        den = self.sb(stack, "att_sum", [P, 2])
        inv = self.sb(stack, "att_inverse_sum", [P, 2])
        S = {n: self.sem("att_" + n) for n in ("scores", "max_done", "exp_done", "inverted", "probs_done", "probs_turned",
                                               "probsT_a", "probsT_b", "pv_done", "pair_out")}
        mask_in = [self.sem(f"att_mask_in{i}") for i in range(2)]
        SCALE = HEAD_DIM ** -0.5
        scores = [self.psum[:, 2 * u:2 * u + 2, :].rearrange("p a n -> p (a n)") for u in range(2)]
        flat = lambda ap: ap.rearrange("p a n -> p (a n)")

        with nc.Block() as block:
            @block.sync
            def _(sp):
                for r in range(2, RES):
                    sp.wait_ge(S["max_done"], HEADS * (r - 1))
                    sp.dma_start(mask[:, r % 2, :], t["att_mask"][r]).then_inc(mask_in[r % 2], 16)
                    if r == 2:
                        self.load_group(sp, self.groups, self.w_in_chunk(COL_GATE))

            @block.tensor
            def _(pe):
                def score(m):
                    r, head = divmod(m, HEADS)
                    p, h = divmod(head, 2)
                    part = slice(h * HEAD_DIM, (h + 1) * HEAD_DIM)
                    by4 = slice(r, SEQ, RES)
                    if m >= 2:
                        pe.wait_ge(S["max_done"], m - 1)
                    out = scores[m % 2]
                    pe.matmul(out[:, 0:SEQ], q[part, p, by4], k[part, p, :], start=True, stop=True)
                    for g in (1, 2):
                        at = SEQ + (g - 1) * P
                        last = pe.matmul(out[:, at:at + P], q[part, g * HALF_KT + p, by4], k[part, g * HALF_KT + p, by4],
                                         start=True, stop=True)
                    last.then_inc(S["scores"], 1)

                def turn_probs(m):
                    pe.wait_ge(S["probs_done"], m + 1)
                    if m:
                        pe.wait_ge(S["probsT_a"], m)
                        pe.wait_ge(S["probsT_b"], m)
                    for i in range(TILES):
                        last = pe.transpose(self.bank[4 + i // NB][:, (i % NB) * P:(i % NB + 1) * P],
                                            neg[:, m % 2, i * P:(i + 1) * P], self.ident[:])
                        if i in (NB - 1, TILES - 1):
                            last.then_inc(S["probs_turned"], 1)

                def values(m):
                    r, head = divmod(m, HEADS)
                    pair, h = divmod(m, 2)
                    pe.wait_ge(S["probsT_a"], m + 1)
                    pe.wait_ge(S["probsT_b"], m + 1)
                    if pair >= 2:
                        pe.wait_ge(S["pair_out"], pair - 1)
                    cols = slice(head * HEAD_DIM, (head + 1) * HEAD_DIM)
                    for i in range(TILES):
                        val = v[:, 0, i, cols] if i < NB else v[:, i - NB + 1, r, cols]
                        last = pe.matmul(self.bank[6 + pair % 2][h * HEAD_DIM:(h + 1) * HEAD_DIM, 0:P], val,
                                         pT[:, m % 2, i, :], start=(i == 0), stop=(i == TILES - 1))
                    last.then_inc(S["pv_done"], 1)

                score(0)
                score(1)
                for m in range(STEPS):
                    turn_probs(m)
                    if m + 2 < STEPS:
                        score(m + 2)
                    if m:
                        values(m - 1)
                values(STEPS - 1)

            @block.scalar
            def _(act):
                def exps(m):
                    u = m % 2
                    act.wait_ge(S["max_done"], m + 1)
                    if m >= 2:
                        act.wait_ge(S["inverted"], m - 1)
                    act.activation(neg[:, u, :], neg[:, u, :], ACT.Exp, bias=low[:, u:u + 1], scale=-1.0,
                                   accum_out=den[:, u:u + 1]).then_inc(S["exp_done"], 1)

                def pair_out(pair):
                    r, p = divmod(pair, HEADS // 2)
                    act.wait_ge(S["pv_done"], 2 * pair + 2)
                    act.copy(self.ya[:, p, r:SEQ:RES], self.bank[6 + pair % 2][:, 0:P]).then_inc(S["pair_out"], 1)

                exps(0)
                exps(1)
                for m in range(STEPS):
                    act.wait_ge(S["probs_turned"], 2 * m + 1)
                    if m >= 2:
                        act.wait_ge(S["pv_done"], m - 1)
                    act.copy(flat(pT[:, m % 2, 0:NB, :]), self.bank[4]).then_inc(S["probsT_a"], 1)
                    if m + 2 < STEPS:
                        exps(m + 2)
                    if m % 2 == 0 and m:
                        pair_out(m // 2 - 1)
                    if m in SPLIT_AT:
                        self.split_hi(act, self.groups, SPLIT_AT.index(m))
                pair_out(STEPS // 2 - 1)

            @block.vector
            def _(dve):
                def mask_and_max(m):
                    r, u = m // HEADS, m % 2
                    if m % HEADS == 0 and r >= 2:
                        dve.wait_ge(mask_in[r % 2], 16)
                    dve.wait_ge(S["scores"], m + 1)
                    if m >= 2:
                        dve.wait_ge(S["probs_turned"], 2 * (m - 1))
                        dve.wait_ge(S["exp_done"], m - 1)
                    dve.tensor_tensor_reduce(out=neg[:, u, :], in0=scores[u][:, 0:ATT_KEYS], in1=mask[:, r % 2, :],
                                             scale=-SCALE, scalar=3.0e38, op0=ALU.add, op1=ALU.min,
                                             accum_out=low[:, u:u + 1]).then_inc(S["max_done"], 1)

                def probs(m):
                    u = m % 2
                    dve.wait_ge(S["exp_done"], m + 1)
                    if m >= 2:
                        dve.wait_ge(S["probs_done"], m - 1)
                    dve.reciprocal(inv[:, u:u + 1], den[:, u:u + 1]).then_inc(S["inverted"], 1)
                    dve.wait_ge(S["inverted"], m + 1)
                    dve.tensor_scalar(neg[:, u, :], neg[:, u, :], inv[:, u:u + 1], None, ALU.mult).then_inc(S["probs_done"], 1)

                mask_and_max(0)
                mask_and_max(1)
                probs(0)
                for m in range(STEPS):
                    dve.wait_ge(S["probs_turned"], 2 * m + 2)
                    if m >= 2:
                        dve.wait_ge(S["pv_done"], m - 1)
                    dve.tensor_copy(flat(pT[:, m % 2, NB:, :]), self.bank[5][:, 0:2 * P]).then_inc(S["probsT_b"], 1)
                    if m + 1 < STEPS:
                        probs(m + 1)
                    if m + 2 < STEPS:
                        mask_and_max(m + 2)
                    if m in SPLIT_AT:
                        self.split_lo(dve, self.groups, SPLIT_AT.index(m))

    def chunk_of(self, w, col):
        def source(c):
            return w[c * HALF_KT * P:(c + 1) * HALF_KT * P, bass.ds(col, COLS)].rearrange("(k p) n -> p k n", p=P)
        return source

    def merge(self, stack):
        with self.stage() as s:
            self.gates_and_branches(s)

    def gates_and_branches(self, stack):
        nc, t = self.nc, self.t
        GATES, GLA, MIX = 2 * D_MODEL // COLS, D_MODEL // COLS, D_MODEL // COLS
        base = self.groups
        base_att = base + GATES
        base_gla = base_att + 1
        base_mix = base_gla + GLA
        self.groups = base_mix + MIX
        gate = self.sb(stack, "gatesT", [P, 2 * KT, SEQ])
        yg_hi = self.sb(stack, "y_glaT_hi", [P, KT, SEQ], F32R)
        yg_lo = self.sb(stack, "y_glaT_lo", [P, KT, SEQ], F32R)
        part = self.sb(stack, "gated_gla", [P, 2, SEQ])
        ya_hi, ya_lo = (self.sb(stack, n, [P, HALF_KT, SEQ], F32R) for n in ("y_attT_hi", "y_attT_lo"))
        S = {n: self.sem("mix_" + n) for n in ("y_hi", "y_lo", "x_in", "att_gated", "gla_gated", "added", "merged_hi",
                                               "merged_lo", "gates_ready", "squared")}
        att_full = [self.sem(f"att_branch_full{b}") for b in range(NB)]
        merged = self.yg
        squares = gate[:, 0:2 * 2, :].rearrange("p (a k) n -> p a (k n)", a=2)
        w_gla, w_att, w_mix = t["w_branch_gla"][0], t["w_branch_att"][0], t["w_mix_out"][0]

        with nc.Block() as block:
            @block.sync
            def _(sp):
                with sp.Fori(1, GATES) as i:
                    self.load_group(sp, base + i, lambda c: self.w_in_chunk(COL_GATE + COLS * i)(c))
                self.load_group(sp, base_att, lambda c: w_att[:, c * COLS:(c + 1) * COLS].rearrange("(k p) n -> p k n", p=P))
                for i in range(GLA):
                    self.load_group(sp, base_gla + i, self.chunk_of(w_gla, i * COLS))
                sp.wait_ge(S["y_lo"], 2)
                sp.dma_start(self.h[:], t["x"][0].rearrange("(b p) n -> p b n", p=P)).then_inc(S["x_in"], 16)
                for i in range(MIX):
                    self.load_group(sp, base_mix + i, self.chunk_of(w_mix, i * COLS))

            @block.tensor
            def _(pe):
                self.run_groups("multiply", pe, base, GATES, weights_stay=True)
                pe.wait_ge(S["y_lo"], 2)
                for c in range(2):
                    pe.wait_ge(self.lo_done[c], base_att + 1)
                    for b in range(NB):
                        bank = self.bank[b] if c else self.bank[4 + b]
                        if c:
                            pe.wait_ge(self.bank_free[b], base_att)
                        for k in range(HALF_KT):
                            col = slice(b * P, (b + 1) * P)
                            for n, (w, y) in enumerate(((self.whi, ya_hi), (self.whi, ya_lo), (self.wlo, ya_hi))):
                                last = pe.matmul(bank, w[c][:, k, col], y[:, k, :], start=(k == 0 and n == 0),
                                                 stop=(k == HALF_KT - 1 and n == 2))
                        last.then_inc(self.bank_full[b] if c else att_full[b], 1)
                        if c == 0 and b == NB - 1:
                            pe.wait_ge(att_full[b], 1)
                            pe.sem_inc(self.chunk_used, 1)
                for i in range(GLA):
                    self.multiply_group(pe, base_gla + i, None, weights_stay=True, lhs=(yg_hi, yg_lo))
                for i in range(MIX):
                    self.multiply_group(pe, base_mix + i, self.block_of,
                                        ready=lambda c: pe.wait_ge(S["merged_lo"], HALF_KT * (c + 1)))

            @block.scalar
            def _(act):
                act.copy(ya_hi[:], self.ya[:]).then_inc(S["y_hi"], 1)
                act.copy(yg_hi[:], self.yg[:]).then_inc(S["y_hi"], 1)
                def gate_out(i, b):
                    return act.activation(gate[:, bass.ds(4 * i + b, 1), :].rearrange("p a n -> p (a n)"),
                                          self.bank[b], ACT.Sigmoid)
                self.run_groups("hi", act, base, GATES, next_split=True, evacuate=gate_out)
                for b in range(NB):
                    act.wait_ge(self.bank_free[b], base + GATES)
                act.sem_inc(S["gates_ready"], 1)
                for g in range(base_gla, base_mix + 1):
                    self.split_hi(act, g, 0)
                    self.split_hi(act, g, 1)
                    if g > base_gla:
                        self.merged_hi(act, S, merged, g - 1 - base_gla)
                self.split_hi(act, base_mix + 1, 0)
                self.split_hi(act, base_mix + 1, 1)
                for b in range(NB):
                    act.wait_ge(self.bank_free[b], base_mix + MIX)
                    if b >= 2:
                        act.wait_ge(S["squared"], b - 1)
                    act.activation(squares[:, b % 2, :], self.h[:, b, :], ACT.Square,
                                   accum_out=self.h_sums[:, b:b + 1]).then_inc(S["squared"], 1)

            @block.vector
            def _(dve):
                for n, (lo, y, hi) in enumerate(((ya_lo, self.ya, ya_hi), (yg_lo, self.yg, yg_hi))):
                    dve.wait_ge(S["y_hi"], n + 1)
                    dve.tensor_tensor(lo[:], y[:], hi[:].bitcast(F32), ALU.subtract).then_inc(S["y_lo"], 1)
                with dve.Fori(1, GATES + 1) as i:
                    for c in range(2):
                        self.split_lo(dve, base + i, c)
                dve.wait_ge(S["gates_ready"], 1)
                dve.wait_ge(S["y_lo"], 2)
                for c in range(2):
                    for b in range(NB):
                        m = NB * c + b
                        dve.wait_ge(self.bank_full[b] if c else att_full[b], base_att + 1 if c else 1)
                        dve.tensor_tensor(merged[:, m, :], gate[:, KT + m, :], self.bank[b] if c else self.bank[4 + b],
                                          ALU.mult).then_inc(self.bank_free[b] if c else S["att_gated"], 1)
                    self.split_lo(dve, base_gla, c)
                for i in range(GLA):
                    self.split_lo(dve, base_gla + i + 1, 0)
                    for b in range(NB):
                        m = NB * i + b
                        dve.wait_ge(self.bank_full[b], base_gla + i + 1)
                        if m >= 2:
                            dve.wait_ge(S["added"], m - 1)
                        dve.tensor_tensor(part[:, m % 2], gate[:, m, :], self.bank[b], ALU.mult).then_inc(self.bank_free[b], 1)
                        dve.wait_ge(self.bank_free[b], base_gla + i + 1)
                        dve.wait_ge(S["att_gated"], NB)
                        dve.wait_ge(self.bank_free[b], base_gla)
                        dve.tensor_tensor(merged[:, m, :], merged[:, m, :], part[:, m % 2], ALU.add).then_inc(S["added"], 1)
                        if b == NB - 1:
                            self.split_lo(dve, base_gla + i + 1, 1)
                        if b:
                            self.merged_lo(dve, S, merged, m - 1)
                    self.merged_lo(dve, S, merged, m)
                self.split_lo(dve, base_mix + 1, 0)
                dve.wait_ge(S["x_in"], 16)
                for i in range(MIX):
                    for b in range(NB):
                        dve.wait_ge(self.bank_full[b], base_mix + i + 1)
                        part_h = self.h[:, b, i * COLS:(i + 1) * COLS]
                        dve.tensor_tensor(part_h, part_h, self.bank[b], ALU.add).then_inc(self.bank_free[b], 1)
                    if i == 0:
                        self.split_lo(dve, base_mix + 1, 1)

    def merged_hi(self, act, S, merged, i):
        for m in range(NB * i, NB * (i + 1)):
            act.wait_ge(S["added"], m + 1)
            act.copy(self.x_hi[:, m, :], merged[:, m, :]).then_inc(S["merged_hi"], 1)

    def merged_lo(self, dve, S, merged, m):
        dve.wait_ge(S["merged_hi"], m + 1)
        dve.tensor_tensor(self.x_lo[:, m, :], merged[:, m, :], self.x_hi[:, m, :].bitcast(F32),
                          ALU.subtract).then_inc(S["merged_lo"], 1)

    def route(self, stack):
        nc, t = self.nc, self.t
        h = self.h
        E = N_EXPERTS
        ss = self.h_sums
        rs = self.sb(stack, "h_rstd", [P, NB])
        g = self.sb(stack, "norm_ffn_g_row", [P, D_MODEL])
        hn = self.sb(stack, "hn", [P, NB, D_MODEL])
        hT = self.sb(stack, "hnT", [P, KT, SEQ])
        rw = self.sb(stack, "router_w_sb", [P, KT, E])
        rb = self.sb(stack, "router_b_row", [P, E])
        logits = self.sb(stack, "logits", [P, NB, E])
        top = self.sb(stack, "top_logits", [P, NB, 8])
        who = self.sb(stack, "top_experts", [P, NB, 8], U32)
        who_f = self.sb(stack, "top_experts_f", [P, NB, TOP_K])
        low = self.sb(stack, "minus_top", [P, NB])
        ex = self.sb(stack, "top_exps", [P, NB, TOP_K])
        tot = self.sb(stack, "top_sums", [P, NB])
        weight = self.sb(stack, "top_weights", [P, NB, TOP_K])
        hot = self.sb(stack, "one_hot", [P, NB, E])
        hot_w = self.sb(stack, "one_hot_weighted", [P, NB, E])
        sel = self.sb(stack, "selected", [P, NB, E])
        wsum = self.sb(stack, "weights", [P, NB, E])
        before = self.sb(stack, "before_sb", [P, P])
        ones = self.sb(stack, "ones_sb", [P, P])
        e_no = self.sb(stack, "expert_numbers_sb", [P, E])
        tok = self.sb(stack, "token_numbers_sb", [P, NB])
        half = self.sb(stack, "minus_half2", [P, 1])
        S = {n: self.sem("route_" + n) for n in ("in", "sums", "powed", "hn_done", "stored", "turned", "hT_out", "logits",
                                                 "low", "exps", "selected", "ranks", "bias_in", "bias_hi")}
        bias, raw_bias = self.bias, self.sb(stack, "biases_twice", [2 * E, 3 * self.WIDE])
        with nc.Block() as block:
            @block.sync
            def _(sp):
                sp.dma_start(g[:], t["norm_ffn_g"][0:1, :].partition_broadcast(P).rearrange("p a n -> p (a n)")).then_inc(S["in"], 16)
                sp.dma_start(rw[:], t["router_w"][0].rearrange("(k p) n -> p k n", p=P)).then_inc(S["in"], 16)
                sp.dma_start(rb[:], t["router_b"][0:1, :].partition_broadcast(P).rearrange("p a n -> p (a n)")).then_inc(S["in"], 16)
                sp.dma_start(before[:], t["before"]).then_inc(S["in"], 16)
                sp.dma_start(e_no[:], t["expert_numbers"]).then_inc(S["in"], 16)
                sp.dma_start(tok[:], t["token_numbers"]).then_inc(S["in"], 16)
                sp.dma_start(self.slot_no[:], t["slot_numbers"]).then_inc(S["in"], 16)
                sp.dma_start(self.bias_row[:], t["bias_row"]).then_inc(S["in"], 16)
                sp.dma_start(self.total.rearrange("(b p) n -> p b n", p=P), h[:]).then_inc(S["stored"], 16)
                for n in range(2):
                    at = slice(n * E, (n + 1) * E)
                    sp.dma_start(raw_bias[at, 0:2 * self.WIDE], t["expert_b_gate_up"][0]).then_inc(S["bias_in"], 16)
                    sp.dma_start(raw_bias[at, 2 * self.WIDE:], t["expert_b_down"][0]).then_inc(S["bias_in"], 16)
                for j in range(2):
                    sp.dma_start(self.expert_ring[j][:], self.expert_weights(0, j)).then_inc(self.first_expert[j], 16)
                sp.wait_ge(S["hn_done"], NB)
                sp.dma_start(self.normed.rearrange("(b p) n -> p b n", p=P), hn[:]).then_inc(S["stored"], 16)
                for j in range(2, self.EARLY):
                    sp.dma_start(self.expert_ring[j][:], self.expert_weights(0, j)).then_inc(self.first_expert[j], 16)
                sp.wait_ge(S["stored"], 32)

            @block.gpsimd
            def _(pool):
                link = self.link("pool", pool)
                link(pool.memset(bias[2 * E:, :].bitcast(F32), 0.0))
                link(pool.memset(ones[:], 1.0))
                link(pool.memset(half[:], -0.5))
                pool.wait_ge(S["sums"], 1)
                pool.tensor_tensor(rs[:], ss[:], half[:, 0:1].to_broadcast([P, NB]), ALU.pow).then_inc(S["powed"], 1)

            @block.tensor
            def _(pe):
                for b in range(NB):
                    pe.wait_ge(S["hn_done"], b + 1)
                    for hf in range(2):
                        i = 2 * b + hf
                        if i >= 2:
                            pe.wait_ge(S["hT_out"], i - 1)
                        for k in range(HALF_KT):
                            last = pe.transpose(self.bank[i % 2][:, k * P:(k + 1) * P],
                                                hn[:, b, (HALF_KT * hf + k) * P:(HALF_KT * hf + k + 1) * P], self.ident[:])
                        last.then_inc(S["turned"], 1)
                pe.wait_ge(S["in"], 8 * 16)
                pe.wait_ge(S["hT_out"], 2 * NB)
                for b in range(NB):
                    for k in range(KT):
                        last = pe.matmul(self.bank[2][:, b * E:(b + 1) * E], hT[:, k, b * P:(b + 1) * P], rw[:, k, :],
                                         start=(k == 0), stop=(k == KT - 1))
                last.then_inc(S["logits"], 1)
                pe.wait_ge(S["selected"], 1)
                pe.wait_ge(S["powed"], 1)
                for b in range(NB):
                    for a in range(b + 1):
                        last = pe.matmul(self.bank[3][:, b * E:(b + 1) * E], (before if a == b else ones)[:], sel[:, a, :],
                                         start=(a == 0), stop=(a == b))
                for a in range(NB):
                    last = pe.matmul(self.bank[4][:, 0:E], ones[:], sel[:, a, :], start=(a == 0), stop=(a == NB - 1))
                last.then_inc(S["ranks"], 1)

            @block.scalar
            def _(act):
                for i in range(2 * NB):
                    b, hf = divmod(i, 2)
                    act.wait_ge(S["turned"], i + 1)
                    act.copy(hT[:, HALF_KT * hf:HALF_KT * (hf + 1), b * P:(b + 1) * P],
                             self.bank[i % 2].rearrange("p (k n) -> p k n", n=P)).then_inc(S["hT_out"], 1)
                act.wait_ge(S["bias_in"], 64)
                act.copy(bias[0:2 * E, :], raw_bias[:]).then_inc(S["bias_hi"], 1)
                act.wait_ge(S["low"], 1)
                for b in range(NB):
                    act.activation(ex[:, b, :], top[:, b, 0:TOP_K], ACT.Exp, bias=low[:, b:b + 1],
                                   accum_out=tot[:, b:b + 1]).then_inc(S["exps"], 1)

            @block.vector
            def _(dve):
                link = self.link("dve", dve)
                dve.tensor_scalar(ss[:], ss[:], 1.0 / D_MODEL, EPS, ALU.mult, ALU.add).then_inc(S["sums"], 1)
                dve.wait_ge(S["in"], 8 * 16)
                dve.wait_ge(S["powed"], 1)
                for b in range(NB):
                    dve.scalar_tensor_tensor(out=hn[:, b, :], in0=h[:, b, :], scalar=rs[:, b:b + 1], in1=g[:],
                                             op0=ALU.mult, op1=ALU.mult).then_inc(S["hn_done"], 1)
                dve.wait_ge(S["bias_hi"], 1)
                low_rows = slice(E, 2 * E)
                link(dve.tensor_tensor(bias[low_rows, :], raw_bias[low_rows, :], bias[low_rows, :].bitcast(F32), ALU.subtract))
                dve.wait_ge(S["logits"], 1)
                link(dve.tensor_tensor(logits[:], self.bank[2][:, 0:NB * E].rearrange("p (b n) -> p b n", n=E),
                                       rb[:].unsqueeze(1).to_broadcast([P, NB, E]), ALU.add))
                for b in range(NB):
                    link(dve.max(top[:, b, :], logits[:, b, :]))
                    link(dve.max_index(who[:, b, :], top[:, b, :], logits[:, b, :]))
                dve.tensor_scalar(low[:], top[:, :, 0], -1.0, None, ALU.mult).then_inc(S["low"], 1)
                link(dve.tensor_copy(who_f[:], who[:, :, 0:TOP_K]))
                dve.wait_ge(S["exps"], NB)
                link(dve.reciprocal(tot[:], tot[:]))
                link(dve.tensor_tensor(weight[:], ex[:], tot[:].unsqueeze(2).to_broadcast([P, NB, TOP_K]), ALU.mult))
                for k in range(TOP_K):
                    dst, dst_w = (hot, hot_w) if k else (sel, wsum)
                    link(dve.tensor_tensor(dst[:], e_no[:].unsqueeze(1).to_broadcast([P, NB, E]),
                                           who_f[:, :, k:k + 1].to_broadcast([P, NB, E]), ALU.is_equal))
                    link(dve.tensor_tensor(dst_w[:], dst[:], weight[:, :, k:k + 1].to_broadcast([P, NB, E]), ALU.mult))
                    if k:
                        link(dve.tensor_tensor(sel[:], sel[:], hot[:], ALU.add))
                        link(dve.tensor_tensor(wsum[:], wsum[:], hot_w[:], ALU.add))
                dve.sem_inc(S["selected"], 1)
                dve.tensor_copy(self.pairs[:, :, :, 1], wsum[:])
                dve.tensor_scalar(self.pairs[:, :, :, 0], tok[:].unsqueeze(2).to_broadcast([P, NB, E]), 1.0, None, ALU.add)
                dve.wait_ge(S["ranks"], 1)
                link(dve.scalar_tensor_tensor(out=self.rank[:], in0=self.bank[3][:, 0:NB * E].rearrange("p (b n) -> p b n", n=E),
                                              scalar=1.0, in1=sel[:], op0=ALU.add, op1=ALU.mult))
                link(dve.tensor_scalar(self.rank[:], self.rank[:], -1.0, None, ALU.add))
                dve.tensor_copy(self.counts[:], self.bank[4][:, 0:E])

    CHUNKS, PER_HALF, SLOTS, WIDE = 12, 4, 3, 1024
    EARLY = 9
    FURTHER = SEQ * TOP_K // P

    def expert_weights(self, e, j):
        wgu, wd, W = self.t["expert_w_gate_up"][0], self.t["expert_w_down"][0], self.WIDE
        stage, k = divmod(j, self.PER_HALF)
        rows = slice(k * 2 * P, (k + 1) * 2 * P)
        src = wd[bass.ds(e, 1), rows, :] if stage == 2 else wgu[bass.ds(e, 1), rows, stage * W:(stage + 1) * W]
        return src.rearrange("a (k p) n -> p (a k) n", p=P)

    def experts(self, stack):
        nc, t = self.nc, self.t
        E, N, W = N_EXPERTS, self.CHUNKS, self.WIDE
        raw, loaded = self.expert_ring, self.first_expert
        whi = [self.sb(stack, f"expert_hi{j}", [P, 2, W], F32R) for j in range(self.SLOTS)]
        wlo = [self.sb(stack, f"expert_lo{j}", [P, 2, W], F32R) for j in range(self.SLOTS)]
        bias = self.bias
        rows, y, a = (self.h[:, b, :] for b in range(3))
        x_hi, x_lo = (self.sb(stack, n, [P, KT, P], F32R) for n in ("rowsT_hi", "rowsT_lo"))
        gv = self.sb(stack, "gate_values", [P, 2, W // 4])
        uv = self.sb(stack, "up_values", [P, 2, W // 4])
        sg = self.sb(stack, "gate_sigmoid", [P, 2, W // 4])
        a_hi, a_lo = (self.sb(stack, n, [P, KT, P], F32R) for n in ("activationsT_hi", "activationsT_lo"))
        hot = self.sb(stack, "slots_one_hot", [P, NB, P])
        slot_no, bias_row = self.slot_no, self.bias_row
        pick = self.sb(stack, "bias_pick", [P, P], F32R)
        none = self.sb(stack, "empty_slot", [P, 1])
        index = [self.sb(stack, f"row_index{u}", [P, 1], I32) for u in range(2)]
        weight = [self.sb(stack, f"row_weight{u}", [P, 1]) for u in range(2)]
        extra, run, past, ones_e = (self.sb(stack, n, [P, E]) for n in ("extra_blocks", "extra_sums", "past", "ones_e"))
        starts = self.sb(stack, "block_starts_sb", [P, self.FURTHER])
        cmp = self.sb(stack, "blocks_before", [P, self.FURTHER, E])
        be = self.sb(stack, "block_expert_f", [P, self.FURTHER])
        far = self.sb(stack, "beyond_first_block", [P, NB, E])
        S = {n: self.sem("moe_" + n) for n in (
            "tables_in", "hi", "lo", "slots_free", "hA_full", "hB_full", "gu", "sig", "p", "act",
            "act_turned", "aT_hi", "aT_lo", "y_full", "y_out", "scattered", "hot", "listed", "none", "index", "gathered",
            "x_turned", "x_hi", "x_lo", "picked", "cleared", "passed")}
        h_full = (S["hA_full"], S["hB_full"])
        QUARTER = W // 4

        def hi(act, e, j):
            act.wait_ge(loaded[j], 16 * e + 16)
            act.wait_ge(S["slots_free"], N * e + j + 1)
            act.copy(whi[j % self.SLOTS][:], raw[j][:]).then_inc(S["hi"], 1)

        def lo(dve, e, j):
            dve.wait_ge(S["hi"], N * e + j + 1)
            s = j % self.SLOTS
            dve.tensor_tensor(wlo[s][:], raw[j][:], whi[s][:].bitcast(F32), ALU.subtract).then_inc(S["lo"], 1)

        def list_hot(dve, e):
            dve.wait_ge(S["listed"], e)
            dve.tensor_tensor(hot[:], slot_no[:].unsqueeze(1).to_broadcast([P, NB, P]),
                              self.rank[:, :, bass.ds(e, 1)].to_broadcast([P, NB, P]), ALU.is_equal).then_inc(S["hot"], 1)

        def list_rows(pe, e):
            pe.wait_ge(S["hot"], e + 1)
            if not isinstance(e, int) or e:
                pe.wait_ge(S["y_out"], 2 * e - 2)
            for b in range(NB):
                last = pe.matmul(self.bank[4][:, 0:2], hot[:, b, :],
                                 self.pairs[:, b, bass.ds(e, 1), :].rearrange("p a n -> p (a n)"),
                                 start=(b == 0), stop=(b == NB - 1))
            last.then_inc(S["listed"], 1)

        def list_index(dve, e, u):
            dve.wait_ge(S["listed"], e + 1)
            dve.wait_ge(S["index"], 2 * e)
            if not isinstance(e, int) or e:
                dve.wait_ge(S["scattered"], 16 * (e - 1))
            dve.tensor_scalar(none[:], self.bank[4][:, 0:1], 0.0, 8.0 * SEQ, ALU.is_equal, ALU.mult).then_inc(S["none"], 1)
            dve.wait_ge(S["none"], e + 1)
            dve.scalar_tensor_tensor(out=index[u][:], in0=none[:], scalar=-1.0, in1=self.bank[4][:, 0:1],
                                     op0=ALU.add, op1=ALU.add).then_inc(S["index"], 1)
            dve.tensor_copy(weight[u][:], self.bank[4][:, 1:2]).then_inc(S["index"], 1)

        def gather(pool, e, u):
            pool.wait_ge(S["index"], 2 * e + 2)
            if not isinstance(e, int) or e:
                pool.wait_ge(S["x_turned"], 2 * e)
            pool.sem_inc(S["passed"], 1)
            pool.indirect_dma_start(rows, None, self.normed, bass.IndirectOffsetOnAxis(ap=index[u][:, 0:1], axis=0),
                                    bounds_check=self.last_row, oob_is_err=False).then_inc(S["gathered"], 16)

        def turn_rows(pe, e):
            pe.wait_ge(S["gathered"], 16 * e + 16)
            pe.wait_ge(S["aT_lo"], 2 * e)
            for f in range(2):
                for k in range(HALF_KT):
                    last = pe.transpose(self.bank[6 + f][:, k * P:(k + 1) * P],
                                        rows[:, (HALF_KT * f + k) * P:(HALF_KT * f + k + 1) * P], self.ident[:])
                last.then_inc(S["x_turned"], 1)

        def split_turned(eng, e, part, f, turned, first, second, hi_t, lo_t):
            dst = slice(HALF_KT * f, HALF_KT * (f + 1))
            bank = self.bank[6 + f].rearrange("p (k n) -> p k n", n=P)
            if part == "hi":
                eng.wait_ge(turned, 2 * e + f + 1)
                eng.copy(hi_t[:, dst, :], bank).then_inc(first, 1)
            else:
                eng.wait_ge(first, 2 * e + f + 1)
                eng.tensor_tensor(lo_t[:, dst, :], bank, hi_t[:, dst, :].bitcast(F32), ALU.subtract).then_inc(second, 1)

        x_part = lambda eng, e, part, f: split_turned(eng, e, part, f, S["x_turned"], S["x_hi"], S["x_lo"], x_hi, x_lo)
        a_part = lambda eng, e, part, f: split_turned(eng, e, part, f, S["act_turned"], S["aT_hi"], S["aT_lo"], a_hi, a_lo)

        def pick_bias(dve, e):
            dve.tensor_copy(pick[:], bias_row[:, bass.ds(e, 1)].to_broadcast([P, P])).then_inc(S["picked"], 1)

        def further_tables(dve):
            link = self.link("dve", dve)
            counts = self.counts[:]
            link(dve.tensor_scalar(extra[:], counts, float(P), None, ALU.is_gt))
            for n in range(2, NB):
                link(dve.tensor_scalar(past[:], counts, float(n * P), None, ALU.is_gt))
                link(dve.tensor_tensor(extra[:], extra[:], past[:], ALU.add))
            link(dve.memset(ones_e[:], 1.0))
            link(dve.tensor_tensor_scan(run[:], ones_e[:], extra[:], 0.0, ALU.mult, ALU.add))
            link(dve.tensor_copy(self.n_further[:], run[:, E - 1:E]))
            link(dve.tensor_scalar(past[:], run[:], float(P), None, ALU.mult))
            link(dve.tensor_tensor(cmp[:], past[:].unsqueeze(1).to_broadcast([P, self.FURTHER, E]),
                                   starts[:].unsqueeze(2).to_broadcast([P, self.FURTHER, E]), ALU.is_le))
            link(dve.tensor_reduce(be[:], cmp[:], AX.X, ALU.add))
            link(dve.tensor_scalar(self.block_expert[:], be[:], float(E - 1), None, ALU.min))
            link(dve.tensor_scalar(extra[:], extra[:], -float(P), 1.0 - P, ALU.mult, ALU.add))
            link(dve.tensor_tensor(extra[:], extra[:], past[:], ALU.add))
            link(dve.tensor_scalar(far[:], self.rank[:], float(P), None, ALU.is_ge))
            link(dve.tensor_tensor(self.place[:], self.rank[:], extra[:].unsqueeze(1).to_broadcast([P, NB, E]), ALU.add))
            link(dve.tensor_tensor(self.place[:], self.place[:], far[:], ALU.mult))
            link(dve.tensor_scalar(self.place[:], self.place[:], -1.0, None, ALU.add))

        def expert_pe(pe, e, more):
            for j in range(N):
                s = j % self.SLOTS
                stage, k = divmod(j, self.PER_HALF)
                banks = [self.bank[2 * stage + i] for i in range(2)]
                t_hi, t_lo = (a_hi, a_lo) if stage == 2 else (x_hi, x_lo)
                if j == 0:
                    pe.wait_ge(S["x_lo"], 2 * e + 2)
                    pe.wait_ge(S["picked"], e + 1)
                if stage == 2:
                    pe.wait_ge(S["aT_lo"], 2 * e + k // 2 + 1)
                if k == 0:
                    if stage < 2:
                        pe.wait_ge(S["gu"], 8 * e)
                    else:
                        pe.wait_ge(S["y_out"], 2 * e)
                        if more:
                            pe.wait_ge(S["index"], 2 * e + 4)
                    for i, bank in enumerate(banks):
                        col = stage * W + i * COLS
                        pe.matmul(bank, pick[:], bias[:, col:col + COLS], start=True, stop=False)
                pe.wait_ge(S["lo"], N * e + j + 1)
                for kk in range(2):
                    row = 2 * k + kk
                    for x, w in ((t_hi, whi), (t_hi, wlo), (t_lo, whi)):
                        for i, bank in enumerate(banks):
                            last = pe.matmul(bank, x[:, row, :], w[s][:, kk, i * COLS:(i + 1) * COLS], start=False,
                                             stop=(k == self.PER_HALF - 1 and kk == 1 and x is t_lo))
                last.then_inc(S["slots_free"], 1)
                if j == 2 and more:
                    list_rows(pe, e + 1)
                if j in (5, 8):
                    f = j // 8
                    pe.wait_ge(S["act"], 4 * e + 2 * f + 2)
                    pe.wait_ge(S["x_lo"], 2 * e + 2)
                    for k2 in range(HALF_KT):
                        last = pe.transpose(self.bank[6 + f][:, k2 * P:(k2 + 1) * P],
                                            a[:, (HALF_KT * f + k2) * P:(HALF_KT * f + k2 + 1) * P], self.ident[:])
                    last.then_inc(S["act_turned"], 1)
                if j == 9 and more:
                    turn_rows(pe, e + 1)

        def gate_sigmoid(act, e, i):
            act.wait_ge(S["gu"], 8 * e + 2 * i + 1)
            act.wait_ge(S["act"], 4 * e + (2 if i >= 2 else 0))
            act.activation(sg[:, i % 2, :], gv[:, i % 2, :], ACT.Sigmoid, scale=SWIGLU_ALPHA).then_inc(S["sig"], 1)

        def rows_out(act, e, u):
            for i in range(2):
                act.wait_ge(S["slots_free"], N * e + N + self.SLOTS)
                act.wait_ge(S["scattered"], 16 * e)
                act.activation(y[:, i * COLS:(i + 1) * COLS], self.bank[4 + i], ACT.Copy,
                               scale=weight[u][:, 0:1]).then_inc(S["y_out"], 1)

        def expert_act(act, e, u, more):
            for j in range(self.SLOTS, N):
                hi(act, e, j)
                if j in (6, 9):
                    for i in range(2):
                        gate_sigmoid(act, e, 2 * (j // 9) + i)
                if j == 8:
                    a_part(act, e, "hi", 0)
                if j == 10:
                    a_part(act, e, "hi", 1)
            if more:
                hi(act, e + 1, 0)
                for f in range(2):
                    x_part(act, e + 1, "hi", f)
                hi(act, e + 1, 1)
                hi(act, e + 1, 2)
            rows_out(act, e, u)

        def swiglu_in(dve, e, half):
            dve.wait_ge(S["slots_free"], N * e + self.PER_HALF * (half + 1) + self.SLOTS)
            for i in (2 * half, 2 * half + 1):
                both = self.bank[i].rearrange("p (n a) -> p n a", a=2)
                dve.wait_ge(S["act"], 4 * e + 2 * half)
                dve.tensor_scalar(gv[:, i % 2, :], both[:, :, 0], SWIGLU_LIMIT, None, ALU.min).then_inc(S["gu"], 1)
                dve.tensor_scalar(uv[:, i % 2, :], both[:, :, 1], SWIGLU_LIMIT, -SWIGLU_LIMIT, ALU.min,
                                  ALU.max).then_inc(S["gu"], 1)

        def swiglu_out(dve, e, half):
            for i in (2 * half, 2 * half + 1):
                dve.wait_ge(S["gu"], 8 * e + 2 * i + 2)
                dve.scalar_tensor_tensor(out=uv[:, i % 2, :], in0=uv[:, i % 2, :], scalar=1.0, in1=gv[:, i % 2, :],
                                         op0=ALU.add, op1=ALU.mult).then_inc(S["p"], 1)
            for i in (2 * half, 2 * half + 1):
                dve.wait_ge(S["p"], 4 * e + i + 1)
                dve.wait_ge(S["sig"], 4 * e + i + 1)
                dve.wait_ge(S["act_turned"], 2 * e)
                dve.tensor_tensor(a[:, i * QUARTER:(i + 1) * QUARTER], uv[:, i % 2, :], sg[:, i % 2, :],
                                  ALU.mult).then_inc(S["act"], 1)

        def expert_dve(dve, e, u, more):
            for j in range(self.SLOTS, N):
                if j in (6, 10):
                    swiglu_in(dve, e, j // 8)
                if j != 10:
                    lo(dve, e, j)
                if j in (6, 10):
                    swiglu_out(dve, e, j // 8)
                if j == 10:
                    lo(dve, e, j)
                if j == 3 and more:
                    list_hot(dve, e + 1)
                if j == 5 and more:
                    list_index(dve, e + 1, 1 - u)
                if j in (8, 10):
                    a_part(dve, e, "lo", j // 9)
            if more:
                dve.wait_ge(S["slots_free"], N * e + 9 + self.SLOTS)
                pick_bias(dve, e + 1)
                lo(dve, e + 1, 0)
                for f in range(2):
                    x_part(dve, e + 1, "lo", f)
                lo(dve, e + 1, 1)
                lo(dve, e + 1, 2)

        def scatter(pool, e, u):
            pool.wait_ge(S["y_out"], 2 * e + 2)
            pool.wait_ge(S["scattered"], 16 * e)
            pool.sem_inc(S["passed"], 1)
            pool.indirect_dma_start(self.total, bass.IndirectOffsetOnAxis(ap=index[u][:, 0:1], axis=0), y, None,
                                    bounds_check=self.last_row, oob_is_err=False, compute_op=ALU.add).then_inc(S["scattered"], 16)

        def over_experts(engine, body):
            with engine.Fori(0, E // 2 - 1) as i:
                for u in range(2):
                    body(2 * i + u, u, True)
            body(E - 2, 0, True)
            body(E - 1, 1, False)

        with nc.Block() as block:
            @block.sync
            def _(sp):
                sp.wait_ge(S["passed"], 1)
                for j in range(self.EARLY, N):
                    sp.dma_start(raw[j][:], self.expert_weights(0, j)).then_inc(loaded[j], 16)
                sp.dma_start(starts[:], t["block_starts"]).then_inc(S["tables_in"], 16)
                sp.dma_start(self.h[:, 3, :], t["norm_final_g"].unsqueeze(0).partition_broadcast(P).rearrange("p a n -> p (a n)")
                             ).then_inc(S["tables_in"], 16)
                with sp.Fori(0, E - 1) as e:
                    for j in range(N):
                        sp.wait_ge(S["lo"], N * e + j + 1)
                        sp.dma_start(raw[j][:], self.expert_weights(e + 1, j)).then_inc(loaded[j], 16)

            @block.gpsimd
            def _(pool):
                pool.memset(rows, 0.0).then_inc(S["cleared"], 1)
                self.last_row = pool.to_reg(SEQ - 1)
                pool.wait_ge(S["cleared"], 1)
                gather(pool, 0, 0)
                def body(e, u, more):
                    if more:
                        gather(pool, e + 1, 1 - u)
                    scatter(pool, e, u)
                over_experts(pool, body)
                pool.wait_ge(S["scattered"], 16 * E)

            @block.scalar
            def _(act):
                for f in range(2):
                    x_part(act, 0, "hi", f)
                for j in range(self.SLOTS):
                    hi(act, 0, j)
                over_experts(act, lambda e, u, more: expert_act(act, e, u, more))

            @block.vector
            def _(dve):
                list_hot(dve, 0)
                list_index(dve, 0, 0)
                pick_bias(dve, 0)
                for f in range(2):
                    x_part(dve, 0, "lo", f)
                for j in range(self.SLOTS):
                    lo(dve, 0, j)
                over_experts(dve, lambda e, u, more: expert_dve(dve, e, u, more))
                dve.wait_ge(S["tables_in"], 32)
                further_tables(dve)

            @block.tensor
            def _(pe):
                pe.sem_inc(S["slots_free"], self.SLOTS)
                list_rows(pe, 0)
                turn_rows(pe, 0)
                over_experts(pe, lambda e, u, more: expert_pe(pe, e, more))

    def further_blocks(self, stack):
        nc, t = self.nc, self.t
        E, N, W, RING = N_EXPERTS, self.CHUNKS, self.WIDE, 4
        wgu, wd = t["expert_w_gate_up"][0], t["expert_w_down"][0]
        ring = [self.sb(stack, f"further_chunk{j}", [P, 2, W]) for j in range(RING)]
        bias = self.sb(stack, "further_biases", [E, 3 * W])
        rows = self.sb(stack, "further_rows", [P, W])
        xT = self.sb(stack, "further_rowsT", [P, KT, P])
        gv, uv, sg, a = (self.sb(stack, "further_" + n, [P, FF]) for n in ("gate", "up", "sigmoid", "act"))
        aT = self.sb(stack, "further_actT", [P, KT, P])
        y = self.sb(stack, "further_out", [P, W])
        hot = self.sb(stack, "further_one_hot", [P, NB, P])
        slot_no = self.sb(stack, "further_slot_numbers", [P, P])
        starts = self.sb(stack, "further_starts", [P, self.FURTHER])
        one = self.sb(stack, "further_bias_rows", [P, E])
        pick = self.sb(stack, "further_bias_pick", [E, P])
        place = self.sb(stack, "further_place", [P, NB])
        none = self.sb(stack, "further_empty", [P, 1])
        index = self.sb(stack, "further_index", [P, 1], I32)
        weight = self.sb(stack, "further_weight", [P, 1])
        S = {n: self.sem("further_" + n) for n in (
            "in", "cleared", "place", "hot", "listed", "none", "index", "gathered", "x_turned", "xT", "picked", "used",
            "h_full", "split", "sig", "p", "act", "a_turned", "aT", "y_full", "y_out", "scattered", "passed")}
        loaded = [self.sem(f"further_loaded{j}") for j in range(RING)]
        flat = lambda ap: ap.rearrange("p k n -> p (k n)")

        def when_any(engine, body, first=None):
            n = engine.value_load(self.n_further[0:1, 0:1], min_val=0, max_val=self.FURTHER)
            with engine.If(n > 0):
                if first:
                    first()
                with engine.Fori(0, self.FURTHER) as i:
                    body(i)
            with engine.Else():
                engine.nop()

        def expert_of(engine, i):
            return engine.value_load(self.block_expert[0:1, bass.ds(i, 1)], min_val=0, max_val=E - 1)

        with nc.Block() as block:
            @block.sync
            def _(sp):
                def tables():
                    sp.dma_start(slot_no[:], t["slot_numbers"]).then_inc(S["in"], 16)
                    sp.dma_start(starts[:], t["block_starts"]).then_inc(S["in"], 16)
                    sp.dma_start(one[:], t["bias_row"]).then_inc(S["in"], 16)
                    sp.dma_start(bias[:, 0:2 * W], t["expert_b_gate_up"][0]).then_inc(S["in"], 16)
                    sp.dma_start(bias[:, 2 * W:], t["expert_b_down"][0]).then_inc(S["in"], 16)

                def body(i):
                    e = expert_of(sp, i)
                    for j in range(N):
                        half, k = divmod(j, self.PER_HALF)
                        rows_ = slice(k * 2 * P, (k + 1) * 2 * P)
                        src = wd[bass.ds(e, 1), rows_, :] if half == 2 else wgu[bass.ds(e, 1), rows_, half * W:(half + 1) * W]
                        sp.wait_ge(S["used"], N * i + j + 1)
                        sp.dma_start(ring[j % RING][:], src.rearrange("a (k p) n -> p (a k) n", p=P)).then_inc(loaded[j % RING], 16)
                when_any(sp, body, tables)

            @block.gpsimd
            def _(pool):
                pool.memset(rows[:], 0.0).then_inc(S["cleared"], 1)
                pool.wait_ge(S["cleared"], 1)
                last_row = pool.to_reg(SEQ - 1)

                def body(i):
                    pool.wait_ge(S["index"], 2 * i + 2)
                    pool.sem_inc(S["passed"], 1)
                    pool.indirect_dma_start(rows[:], None, self.normed, bass.IndirectOffsetOnAxis(ap=index[:, 0:1], axis=0),
                                            bounds_check=last_row, oob_is_err=False).then_inc(S["gathered"], 16)
                    pool.wait_ge(S["y_out"], 2 * i + 2)
                    pool.sem_inc(S["passed"], 1)
                    pool.indirect_dma_start(self.total, bass.IndirectOffsetOnAxis(ap=index[:, 0:1], axis=0), y[:], None,
                                            bounds_check=last_row, oob_is_err=False,
                                            compute_op=ALU.add).then_inc(S["scattered"], 16)
                    pool.wait_ge(S["scattered"], 16 * i + 16)
                    pool.sem_inc(S["passed"], 1)
                when_any(pool, body)

            @block.scalar
            def _(act):
                def body(i):
                    for f in range(2):
                        act.wait_ge(S["x_turned"], i + 1)
                        act.copy(flat(xT[:, HALF_KT * f:HALF_KT * (f + 1), :]), self.bank[6 + f]).then_inc(S["xT"], 1)
                    act.wait_ge(S["split"], 8 * i + 8)
                    act.activation(sg[:], gv[:], ACT.Sigmoid, scale=SWIGLU_ALPHA).then_inc(S["sig"], 1)
                    for f in range(2):
                        act.wait_ge(S["a_turned"], i + 1)
                        act.copy(flat(aT[:, HALF_KT * f:HALF_KT * (f + 1), :]), self.bank[6 + f]).then_inc(S["aT"], 1)
                    for f in range(2):
                        act.wait_ge(S["y_full"], i + 1)
                        act.activation(y[:, f * COLS:(f + 1) * COLS], self.bank[4 + f], ACT.Copy,
                                       scale=weight[:, 0:1]).then_inc(S["y_out"], 1)
                when_any(act, body)

            @block.vector
            def _(dve):

                def body(i):
                    e = expert_of(dve, i)
                    dve.wait_ge(S["scattered"], 16 * i)
                    dve.tensor_tensor(place[:], self.place[:, :, bass.ds(e, 1)].rearrange("p b a -> p (b a)"),
                                      starts[:, bass.ds(i, 1)].to_broadcast([P, NB]), ALU.subtract).then_inc(S["place"], 1)
                    dve.wait_ge(S["place"], i + 1)
                    dve.tensor_tensor(hot[:], slot_no[:].unsqueeze(1).to_broadcast([P, NB, P]),
                                      place[:].unsqueeze(2).to_broadcast([P, NB, P]), ALU.is_equal).then_inc(S["hot"], 1)
                    dve.tensor_copy(pick[:], one[0:E, bass.ds(e, 1)].to_broadcast([E, P])).then_inc(S["picked"], 1)
                    dve.wait_ge(S["listed"], i + 1)
                    dve.tensor_scalar(none[:], self.bank[4][:, 0:1], 0.0, 8.0 * SEQ, ALU.is_equal, ALU.mult).then_inc(S["none"], 1)
                    dve.wait_ge(S["none"], i + 1)
                    dve.scalar_tensor_tensor(out=index[:], in0=none[:], scalar=-1.0, in1=self.bank[4][:, 0:1],
                                             op0=ALU.add, op1=ALU.add).then_inc(S["index"], 1)
                    dve.tensor_copy(weight[:], self.bank[4][:, 1:2]).then_inc(S["index"], 1)
                    dve.wait_ge(S["h_full"], i + 1)
                    for n in range(4):
                        both = self.bank[n].rearrange("p (n a) -> p n a", a=2)
                        at = slice(n * W // 4, (n + 1) * W // 4)
                        dve.tensor_scalar(gv[:, at], both[:, :, 0], SWIGLU_LIMIT, None, ALU.min).then_inc(S["split"], 1)
                        dve.tensor_scalar(uv[:, at], both[:, :, 1], SWIGLU_LIMIT, -SWIGLU_LIMIT, ALU.min,
                                          ALU.max).then_inc(S["split"], 1)
                    dve.wait_ge(S["split"], 8 * i + 8)
                    dve.scalar_tensor_tensor(out=uv[:], in0=uv[:], scalar=1.0, in1=gv[:], op0=ALU.add,
                                             op1=ALU.mult).then_inc(S["p"], 1)
                    dve.wait_ge(S["p"], i + 1)
                    dve.wait_ge(S["sig"], i + 1)
                    dve.tensor_tensor(a[:], uv[:], sg[:], ALU.mult).then_inc(S["act"], 1)
                when_any(dve, body, lambda: dve.wait_ge(S["in"], 80))

            @block.tensor
            def _(pe):
                pe.sem_inc(S["used"], RING)

                def turn(src, f_done):
                    for f in range(2):
                        for k in range(HALF_KT):
                            last = pe.transpose(self.bank[6 + f][:, k * P:(k + 1) * P],
                                                src[:, (HALF_KT * f + k) * P:(HALF_KT * f + k + 1) * P], self.ident[:])
                    last.then_inc(f_done, 1)

                def body(i):
                    e = expert_of(pe, i)
                    pe.wait_ge(S["hot"], i + 1)
                    pe.wait_ge(S["y_out"], 2 * i)
                    for b in range(NB):
                        last = pe.matmul(self.bank[4][:, 0:2], hot[:, b, :],
                                         self.pairs[:, b, bass.ds(e, 1), :].rearrange("p a n -> p (a n)"),
                                         start=(b == 0), stop=(b == NB - 1))
                    last.then_inc(S["listed"], 1)
                    pe.wait_ge(S["gathered"], 16 * i + 16)
                    turn(rows, S["x_turned"])
                    pe.wait_ge(S["xT"], 2 * i + 2)
                    pe.wait_ge(S["picked"], i + 1)
                    for j in range(N):
                        half, k = divmod(j, self.PER_HALF)
                        banks = [self.bank[2 * half + m] for m in range(2)]
                        if j == 2 * self.PER_HALF:
                            pe.wait_ge(S["act"], i + 1)
                            turn(a, S["a_turned"])
                            pe.wait_ge(S["aT"], 2 * i + 2)
                            pe.wait_ge(S["index"], 2 * i + 2)
                        if k == 0:
                            for m, bank in enumerate(banks):
                                col = half * W + m * COLS
                                pe.matmul(bank, pick[:], bias[:, col:col + COLS], start=True, stop=False)
                        pe.wait_ge(loaded[j % RING], 16 * ((N // RING) * i + j // RING + 1))
                        x = aT if half == 2 else xT
                        for kk in range(2):
                            for m, bank in enumerate(banks):
                                last = pe.matmul(bank, x[:, 2 * k + kk, :], ring[j % RING][:, kk, m * COLS:(m + 1) * COLS],
                                                 start=False, stop=(k == self.PER_HALF - 1 and kk == 1))
                        last.then_inc(S["used"], 1)
                        if j == 2 * self.PER_HALF - 1:
                            pe.wait_ge(S["used"], N * i + j + 1 + RING)
                            pe.sem_inc(S["h_full"], 1)
                    pe.wait_ge(S["used"], N * i + N + RING)
                    pe.sem_inc(S["y_full"], 1)
                when_any(pe, body, lambda: pe.wait_ge(S["in"], 80))

    def normalise_output(self, stack):
        nc, t = self.nc, self.t
        h = self.sb(stack, "total_sb", [P, NB, D_MODEL])
        sq = self.sb(stack, "total_squares", [P, NB, D_MODEL])
        ss = self.sb(stack, "total_sum_squares", [P, NB])
        rs = self.sb(stack, "total_rstd", [P, NB])
        g = self.h[:, 3, :]
        half = self.sb(stack, "minus_half3", [P, 1])
        h_in = [self.sem(f"total_in{b}") for b in range(NB)]
        S = {n: self.sem("final_" + n) for n in ("squared", "means", "powed", "done", "stored")}
        with nc.Block() as block:
            @block.sync
            def _(sp):
                for b in range(NB):
                    sp.dma_start(h[:, b, :], self.total[b * P:(b + 1) * P, :]).then_inc(h_in[b], 16)
                for b in range(NB):
                    sp.wait_ge(S["done"], b + 1)
                    sp.dma_start(t["out"][0, b * P:(b + 1) * P, :], h[:, b, :]).then_inc(S["stored"], 16)
                sp.wait_ge(S["stored"], 16 * NB)

            @block.scalar
            def _(act):
                for b in range(NB):
                    act.wait_ge(h_in[b], 16)
                    act.activation(sq[:, b, :], h[:, b, :], ACT.Square, accum_out=ss[:, b:b + 1]).then_inc(S["squared"], 1)

            @block.gpsimd
            def _(pool):
                link = self.link("pool", pool)
                link(pool.memset(half[:], -0.5))
                for b in range(NB):
                    pool.wait_ge(S["means"], b + 1)
                    pool.tensor_tensor(rs[:, b:b + 1], ss[:, b:b + 1], half[:], ALU.pow).then_inc(S["powed"], 1)

            @block.vector
            def _(dve):
                def mean(b):
                    dve.wait_ge(S["squared"], b + 1)
                    dve.tensor_scalar(ss[:, b:b + 1], ss[:, b:b + 1], 1.0 / D_MODEL, EPS, ALU.mult,
                                      ALU.add).then_inc(S["means"], 1)

                mean(0)
                for b in range(NB):
                    if b + 1 < NB:
                        mean(b + 1)
                    dve.wait_ge(S["powed"], b + 1)
                    dve.scalar_tensor_tensor(out=h[:, b, :], in0=h[:, b, :], scalar=rs[:, b:b + 1], in1=g,
                                             op0=ALU.mult, op1=ALU.mult).then_inc(S["done"], 1)


_OUT = ("out", (1, SEQ, D_MODEL), F32)


def kernel(**inputs):
    import concourse.bacc as bacc
    from concourse.bass_utils import run_bass_kernel_spmd

    nc = bacc.Bacc("TRN2", target_bir_lowering=False, num_devices=1)
    arrays, tensors = {}, {}
    for name, a in list(inputs.items()) + list(CONSTANTS.items()):
        a = np.ascontiguousarray(a)
        arrays[f"in_{name}"] = a
        tensors[name] = nc.dram_tensor(f"in_{name}", a.shape, mybir.dt.from_np(a.dtype), kind="ExternalInput").ap()
    name, shape, dt = _OUT
    tensors[name] = nc.dram_tensor(name, shape, dt, kind="ExternalOutput").ap()
    Kernel(nc, tensors).build()
    results = run_bass_kernel_spmd(nc, [arrays], core_ids=[0])
    return results.results[0][name]
```
